# Optimizing a Trainium2 kernel written in Bass

```python
import math
import jax
import jax.numpy as jnp
from jax import lax
import numpy as np
import jax, jax.numpy as jnp

D_MODEL = 1024
BATCH = 1
SEQ = 256
DEPTH = 2

N_MIXERS = 4
EPS = 1e-6
MACARON_W = 0.5
D_FF = 2816
ROPE_BASE = 10000.0
REL_BUCKETS = 32
REL_MAX_DIST = 128
MLA_HEADS = 16
MLA_Q_RANK = 384
MLA_KV_RANK = 256
MLA_NOPE = 64
MLA_ROPE = 32
MLA_V = 64
MLA_Q_BLOCK = 128
RWKV_HEAD = 64
RWKV_HEADS = D_MODEL // RWKV_HEAD
RWKV_DECAY_LORA = 64
RWKV_A_LORA = 64
RWKV_GATE_LORA = 160
RWKV_GN_EPS = 64e-5
MOBA_HEADS = 16
MOBA_HEAD_DIM = D_MODEL // MOBA_HEADS
MOBA_BLOCK = 256
MOBA_TOPK = 3
MOBA_Q_CHUNK = 32
RET_HEADS = 4
RET_DK = D_MODEL // RET_HEADS
RET_DV = 2 * D_MODEL // RET_HEADS
RET_CHUNK = 128
RET_GN_EPS = 1e-5


def _rmsnorm(x, g):
    xf = x.astype(jnp.float32)
    y = xf * lax.rsqrt(jnp.mean(xf * xf, axis=-1, keepdims=True) + EPS)
    return (y * g.astype(jnp.float32)).astype(x.dtype)

def _modulate(x, g, shift, scale):
    return _rmsnorm(x, g) * (1 + scale[:, None, :]) + shift[:, None, :]

def _groupnorm_heads(y, w, b, eps):
    B, S, H, N = y.shape
    yf = y.astype(jnp.float32)
    mu = jnp.mean(yf, axis=-1, keepdims=True)
    var = jnp.mean(jnp.square(yf - mu), axis=-1, keepdims=True)
    yn = ((yf - mu) * lax.rsqrt(var + eps)).reshape(B, S, H * N)
    return yn * w.astype(jnp.float32) + b.astype(jnp.float32)

def _swiglu(h, w_in, w_out):
    gt, up = jnp.split(h @ w_in, 2, axis=-1)
    return (jax.nn.silu(gt) * up) @ w_out

def _rope_tables(seq, dim):
    inv = ROPE_BASE ** (-jnp.arange(0, dim, 2, dtype=jnp.float32) / dim)
    ang = jnp.arange(seq, dtype=jnp.float32)[:, None] * inv[None, :]
    return jnp.cos(ang), jnp.sin(ang)

def _apply_rope(x, cos, sin):
    half = x.shape[-1] // 2
    x1 = x[..., :half].astype(jnp.float32)
    x2 = x[..., half:].astype(jnp.float32)
    c = cos[None, :, None, :]
    s = sin[None, :, None, :]
    return jnp.concatenate([x1 * c - x2 * s, x1 * s + x2 * c], axis=-1).astype(x.dtype)

def _t5_bucket(dist):
    n = jnp.maximum(dist, 0)
    max_exact = REL_BUCKETS // 2
    nf = jnp.maximum(n, max_exact).astype(jnp.float32)
    large = max_exact + (jnp.log(nf / max_exact) / math.log(REL_MAX_DIST / max_exact)
                         * (REL_BUCKETS - max_exact)).astype(jnp.int32)
    large = jnp.minimum(large, REL_BUCKETS - 1)
    return jnp.where(n < max_exact, n, large)

def _dense_causal_attention(q, k, v):
    B, S, H, dq = q.shape
    dv = v.shape[-1]
    nq = S // MLA_Q_BLOCK
    qb = q.reshape(B, nq, MLA_Q_BLOCK, H, dq).transpose(1, 0, 3, 2, 4)
    kpos = jnp.arange(S)

    def one_block(args):
        qi, bi = args
        s = jnp.einsum('bhqd,bkhd->bhqk', qi, k).astype(jnp.float32)
        qpos = bi * MLA_Q_BLOCK + jnp.arange(MLA_Q_BLOCK)
        s = jnp.where(kpos[None, :] <= qpos[:, None], s, -jnp.inf)
        p = jax.nn.softmax(s, axis=-1).astype(v.dtype)
        return jnp.einsum('bhqk,bkhd->bqhd', p, v)

    o = lax.map(one_block, (qb, jnp.arange(nq)))
    return o.transpose(1, 0, 2, 3, 4).reshape(B, S, H * dv)

def _mla_mixer(h, w_in, q_norm, w_uq, kv_norm, w_ukv, w_out):
    B, S, _ = h.shape
    H = MLA_HEADS
    cq, ckv, k_rope = jnp.split(h @ w_in, [MLA_Q_RANK, MLA_Q_RANK + MLA_KV_RANK], axis=-1)
    q = (_rmsnorm(cq, q_norm) @ w_uq).reshape(B, S, H, MLA_NOPE + MLA_ROPE)
    kv = (_rmsnorm(ckv, kv_norm) @ w_ukv).reshape(B, S, H, MLA_NOPE + MLA_V)
    cos, sin = _rope_tables(S, MLA_ROPE)
    q = jnp.concatenate([q[..., :MLA_NOPE], _apply_rope(q[..., MLA_NOPE:], cos, sin)], axis=-1)
    k_rope = jnp.broadcast_to(_apply_rope(k_rope[:, :, None, :], cos, sin), (B, S, H, MLA_ROPE))
    k = jnp.concatenate([kv[..., :MLA_NOPE], k_rope], axis=-1)
    v = kv[..., MLA_NOPE:]
    o = _dense_causal_attention(q * (MLA_NOPE + MLA_ROPE) ** -0.5, k, v)
    return o @ w_out

def _rwkv7_mixer(h, mu, w_rkv, w0, wd1, wd2, a0, wa1, wa2, wg1, wg2, k_k, k_a, r_k, gn_w, gn_b, w_out):
    B, S, D = h.shape
    H, N = RWKV_HEADS, RWKV_HEAD
    xx = jnp.pad(h, ((0, 0), (1, 0), (0, 0)))[:, :-1] - h
    xs = h[:, :, None, :] + xx[:, :, None, :] * mu
    rkv = jnp.einsum('bsnd,nde->bsne', xs[:, :, :3], w_rkv)
    r, k, v = rkv[:, :, 0], rkv[:, :, 1], rkv[:, :, 2]
    xw, xa, xg = xs[:, :, 3], xs[:, :, 4], xs[:, :, 5]
    w = -jax.nn.softplus(-(w0 + jnp.tanh(xw @ wd1) @ wd2)) - 0.5
    decay = jnp.exp(-jnp.exp(w.astype(jnp.float32)))
    a = jax.nn.sigmoid((a0 + (xa @ wa1) @ wa2).astype(jnp.float32))
    g = jax.nn.sigmoid(xg @ wg1) @ wg2
    kk = (k * k_k).astype(jnp.float32).reshape(B, S, H, N)
    kk = kk / jnp.maximum(jnp.sqrt(jnp.sum(kk * kk, axis=-1, keepdims=True)), 1e-12)
    k_mod = k.astype(jnp.float32) * (1 + (a - 1) * k_a.astype(jnp.float32))

    def heads(t):
        return t.astype(jnp.float32).reshape(B, S, H, N)

    r_h, k_h, v_h, a_h, w_h = heads(r), heads(k_mod), heads(v), heads(a), heads(decay)

    def tm(t):
        return t.transpose(1, 0, 2, 3)

    def step(state, inp):
        r_t, w_t, k_t, v_t, ka_t, kb_t = inp
        sa = jnp.einsum('bhvk,bhk->bhv', state, ka_t)
        state = (state * w_t[:, :, None, :] + sa[..., None] * kb_t[:, :, None, :]
                 + v_t[..., None] * k_t[:, :, None, :])
        return state, jnp.einsum('bhvk,bhk->bhv', state, r_t)

    state0 = jnp.zeros((B, H, N, N), jnp.float32)
    _, y = lax.scan(step, state0, (tm(r_h), tm(w_h), tm(k_h), tm(v_h), tm(-kk), tm(kk * a_h)))
    y = y.transpose(1, 0, 2, 3)
    yn = _groupnorm_heads(y, gn_w, gn_b, RWKV_GN_EPS)
    bonus = (jnp.sum(r_h * k_h * r_k.astype(jnp.float32), axis=-1, keepdims=True) * v_h).reshape(B, S, D)
    return ((yn + bonus) * g.astype(jnp.float32)).astype(h.dtype) @ w_out

def _moba_mixer(h, w_in, rel_table, w_out):
    B, S, _ = h.shape
    H, dh, BLK, QC = MOBA_HEADS, MOBA_HEAD_DIM, MOBA_BLOCK, MOBA_Q_CHUNK
    qkv = (h @ w_in).reshape(B, S, 3, H, dh)
    q = qkv[:, :, 0].transpose(0, 2, 1, 3) * dh ** -0.5
    k = qkv[:, :, 1].transpose(0, 2, 1, 3)
    v = qkv[:, :, 2].transpose(0, 2, 1, 3)
    nb = -(-S // BLK)
    K = min(MOBA_TOPK, nb)
    pad = nb * BLK - S
    kb = jnp.pad(k, ((0, 0), (0, 0), (0, pad), (0, 0))).reshape(B, H, nb, BLK, dh)
    vb = jnp.pad(v, ((0, 0), (0, 0), (0, pad), (0, 0))).reshape(B, H, nb, BLK, dh)
    kmean = jnp.mean(kb.astype(jnp.float32), axis=3)
    table_t = rel_table.astype(jnp.float32).T
    nc = S // QC
    qc = q.reshape(B, H, nc, QC, dh).transpose(2, 0, 1, 3, 4)
    b_ix = jnp.arange(B)[:, None, None, None]
    h_ix = jnp.arange(H)[None, :, None, None]
    blk_ids = jnp.arange(nb)
    offs = jnp.arange(BLK)

    def chunk(args):
        qi, ci = args
        start = ci * QC
        qpos = start + jnp.arange(QC)
        own = start // BLK
        gate = jnp.einsum('bhqd,bhnd->bhqn', qi.astype(jnp.float32), kmean)
        gate = jnp.where(blk_ids < own, gate, -jnp.inf)
        top_s, top_i = lax.top_k(gate, K)
        valid = jnp.isfinite(top_s)
        k_sel = kb[b_ix, h_ix, top_i]
        v_sel = vb[b_ix, h_ix, top_i]
        pos_sel = top_i[..., None] * BLK + offs
        bias_sel = table_t[h_ix[..., None], _t5_bucket(qpos[:, None, None] - pos_sel)]
        s_sel = jnp.einsum('bhqd,bhqjkd->bhqjk', qi, k_sel).astype(jnp.float32) + bias_sel
        s_sel = jnp.where(valid[..., None], s_sel, -jnp.inf).reshape(B, H, QC, K * BLK)
        k_own = lax.dynamic_index_in_dim(kb, own, axis=2, keepdims=False)
        v_own = lax.dynamic_index_in_dim(vb, own, axis=2, keepdims=False)
        dist_own = qpos[:, None] - (own * BLK + offs)[None, :]
        s_own = jnp.einsum('bhqd,bhkd->bhqk', qi, k_own).astype(jnp.float32) + table_t[:, _t5_bucket(dist_own)]
        s_own = jnp.where(dist_own >= 0, s_own, -jnp.inf)
        p = jax.nn.softmax(jnp.concatenate([s_sel, s_own], axis=-1), axis=-1).astype(v.dtype)
        p_sel = p[..., :K * BLK].reshape(B, H, QC, K, BLK)
        p_own = p[..., K * BLK:]
        return (jnp.einsum('bhqjk,bhqjkd->bhqd', p_sel, v_sel)
                + jnp.einsum('bhqk,bhkd->bhqd', p_own, v_own))

    o = lax.map(chunk, (qc, jnp.arange(nc)))
    o = o.transpose(1, 0, 3, 2, 4).reshape(B, S, H * dh)
    return o @ w_out

def _retnet_mixer(h, w_in, gn_w, gn_b, w_out):
    B, S, D = h.shape
    H, DK, DV, C = RET_HEADS, RET_DK, RET_DV, RET_CHUNK
    q, k, v, g = jnp.split(h @ w_in, [D, 2 * D, 4 * D], axis=-1)
    cos, sin = _rope_tables(S, DK)
    q = _apply_rope(q.reshape(B, S, H, DK), cos, sin).astype(jnp.float32)
    k = _apply_rope(k.reshape(B, S, H, DK) * DK ** -0.5, cos, sin).astype(jnp.float32)
    v = v.reshape(B, S, H, DV).astype(jnp.float32)
    log_gamma = jnp.log1p(-jnp.exp2(-5.0 - jnp.arange(H, dtype=jnp.float32)))
    idx = jnp.arange(C, dtype=jnp.float32)
    diff = idx[:, None] - idx[None, :]
    dmask = jnp.where(diff >= 0, jnp.exp(jnp.maximum(diff, 0.0)[None] * log_gamma[:, None, None]), 0.0)
    zeta = jnp.exp((C - 1 - idx)[None, :] * log_gamma[:, None])
    xi = jnp.exp((idx + 1)[None, :] * log_gamma[:, None])
    gamma_c = jnp.exp(C * log_gamma)
    nc = S // C

    def chunks(t):
        return t.reshape(B, nc, C, H, t.shape[-1]).transpose(1, 0, 3, 2, 4)

    def step(R, inp):
        qc, kc, vc = inp
        inner = jnp.einsum('bhnd,bhmd->bhnm', qc, kc) * dmask
        o = (jnp.einsum('bhnm,bhme->bhne', inner, vc)
             + jnp.einsum('bhnd,bhde->bhne', qc, R) * xi[None, :, :, None])
        R = gamma_c[None, :, None, None] * R + jnp.einsum('bhmd,hm,bhme->bhde', kc, zeta, vc)
        return R, o

    R0 = jnp.zeros((B, H, DK, DV), jnp.float32)
    _, o = lax.scan(step, R0, (chunks(q), chunks(k), chunks(v)))
    o = o.transpose(1, 0, 3, 2, 4).reshape(B, S, H, DV)
    yn = _groupnorm_heads(o, gn_w, gn_b, RET_GN_EPS)
    return (jax.nn.silu(g.astype(jnp.float32)) * yn).astype(h.dtype) @ w_out

def first_inputs(seed: int = 0) -> dict:
    key = jax.random.key(seed)
    ks = iter(jax.random.split(key, 48))
    f32 = jnp.float32

    def nrm(shape, scale):
        return scale * jax.random.normal(next(ks), shape, f32)

    def uni(shape, lo, hi):
        return jax.random.uniform(next(ks), shape, f32, lo, hi)

    D = D_MODEL
    n_mla, n_rwkv, n_moba, n_ret = [len(range(m, DEPTH, N_MIXERS)) for m in range(N_MIXERS)]
    gate_offset = jnp.zeros((3,), f32).at[2].set(1.0)
    return {
        'x': nrm((BATCH, SEQ, D), 1.0),
        'c': nrm((BATCH, D), 1.0),
        'ada_w': nrm((DEPTH, D, 9 * D), 0.2 * D ** -0.5),
        'ada_b': (nrm((DEPTH, 3, 3, D), 0.02) + gate_offset[None, None, :, None]).reshape(DEPTH, 9 * D),
        'norm_g': 1.0 + nrm((DEPTH, 3, D), 0.05),
        'ffn_w_in': nrm((DEPTH, 2, D, 2 * D_FF), D ** -0.5),
        'ffn_w_out': nrm((DEPTH, 2, D_FF, D), D_FF ** -0.5),
        'final_g': 1.0 + nrm((D,), 0.05),
        'rel_table': nrm((REL_BUCKETS, MOBA_HEADS), 0.5),
        'mla_w_in': nrm((n_mla, D, MLA_Q_RANK + MLA_KV_RANK + MLA_ROPE), D ** -0.5),
        'mla_q_norm': 1.0 + nrm((n_mla, MLA_Q_RANK), 0.05),
        'mla_w_uq': nrm((n_mla, MLA_Q_RANK, MLA_HEADS * (MLA_NOPE + MLA_ROPE)), MLA_Q_RANK ** -0.5),
        'mla_kv_norm': 1.0 + nrm((n_mla, MLA_KV_RANK), 0.05),
        'mla_w_ukv': nrm((n_mla, MLA_KV_RANK, MLA_HEADS * (MLA_NOPE + MLA_V)), MLA_KV_RANK ** -0.5),
        'mla_w_out': nrm((n_mla, MLA_HEADS * MLA_V, D), (MLA_HEADS * MLA_V) ** -0.5),
        'rwkv_mu': uni((n_rwkv, 6, D), 0.0, 1.0),
        'rwkv_w_rkv': nrm((n_rwkv, 3, D, D), D ** -0.5),
        'rwkv_w0': uni((n_rwkv, D), -6.5, -1.5),
        'rwkv_wd1': nrm((n_rwkv, D, RWKV_DECAY_LORA), D ** -0.5),
        'rwkv_wd2': nrm((n_rwkv, RWKV_DECAY_LORA, D), 0.5 * RWKV_DECAY_LORA ** -0.5),
        'rwkv_a0': nrm((n_rwkv, D), 0.1),
        'rwkv_wa1': nrm((n_rwkv, D, RWKV_A_LORA), D ** -0.5),
        'rwkv_wa2': nrm((n_rwkv, RWKV_A_LORA, D), RWKV_A_LORA ** -0.5),
        'rwkv_wg1': nrm((n_rwkv, D, RWKV_GATE_LORA), D ** -0.5),
        'rwkv_wg2': nrm((n_rwkv, RWKV_GATE_LORA, D), RWKV_GATE_LORA ** -0.5),
        'rwkv_k_k': 0.85 + nrm((n_rwkv, D), 0.05),
        'rwkv_k_a': 1.0 + nrm((n_rwkv, D), 0.05),
        'rwkv_r_k': nrm((n_rwkv, RWKV_HEADS, RWKV_HEAD), 0.1),
        'rwkv_gn_w': 1.0 + nrm((n_rwkv, D), 0.05),
        'rwkv_gn_b': nrm((n_rwkv, D), 0.02),
        'rwkv_w_out': nrm((n_rwkv, D, D), D ** -0.5),
        'moba_w_in': nrm((n_moba, D, 3 * D), D ** -0.5),
        'moba_w_out': nrm((n_moba, D, D), D ** -0.5),
        'ret_w_in': nrm((n_ret, D, 6 * D), D ** -0.5),
        'ret_gn_w': 1.0 + nrm((n_ret, 2 * D), 0.05),
        'ret_gn_b': nrm((n_ret, 2 * D), 0.02),
        'ret_w_out': nrm((n_ret, 2 * D, D), (2 * D) ** -0.5),
    }

def first_block(x, c, ada_w, ada_b, norm_g, ffn_w_in, ffn_w_out, final_g, rel_table,
              mla_w_in, mla_q_norm, mla_w_uq, mla_kv_norm, mla_w_ukv, mla_w_out,
              rwkv_mu, rwkv_w_rkv, rwkv_w0, rwkv_wd1, rwkv_wd2, rwkv_a0, rwkv_wa1, rwkv_wa2,
              rwkv_wg1, rwkv_wg2, rwkv_k_k, rwkv_k_a, rwkv_r_k, rwkv_gn_w, rwkv_gn_b, rwkv_w_out,
              moba_w_in, moba_w_out, ret_w_in, ret_gn_w, ret_gn_b, ret_w_out):
    B = x.shape[0]
    c_act = jax.nn.silu(c)
    for i in range(DEPTH):
        mods = (c_act @ ada_w[i] + ada_b[i]).reshape(B, 3, 3, D_MODEL)
        h = _modulate(x, norm_g[i, 0], mods[:, 0, 0], mods[:, 0, 1])
        x = x + MACARON_W * mods[:, 0, 2][:, None, :] * _swiglu(h, ffn_w_in[i, 0], ffn_w_out[i, 0])
        h = _modulate(x, norm_g[i, 1], mods[:, 1, 0], mods[:, 1, 1])
        kind, j = i % N_MIXERS, i // N_MIXERS
        if kind == 0:
            y = _mla_mixer(h, mla_w_in[j], mla_q_norm[j], mla_w_uq[j], mla_kv_norm[j], mla_w_ukv[j], mla_w_out[j])
        elif kind == 1:
            y = _rwkv7_mixer(h, rwkv_mu[j], rwkv_w_rkv[j], rwkv_w0[j], rwkv_wd1[j], rwkv_wd2[j], rwkv_a0[j],
                             rwkv_wa1[j], rwkv_wa2[j], rwkv_wg1[j], rwkv_wg2[j], rwkv_k_k[j], rwkv_k_a[j],
                             rwkv_r_k[j], rwkv_gn_w[j], rwkv_gn_b[j], rwkv_w_out[j])
        elif kind == 2:
            y = _moba_mixer(h, moba_w_in[j], rel_table, moba_w_out[j])
        else:
            y = _retnet_mixer(h, ret_w_in[j], ret_gn_w[j], ret_gn_b[j], ret_w_out[j])
        x = x + mods[:, 1, 2][:, None, :] * y
        h = _modulate(x, norm_g[i, 2], mods[:, 2, 0], mods[:, 2, 1])
        x = x + MACARON_W * mods[:, 2, 2][:, None, :] * _swiglu(h, ffn_w_in[i, 1], ffn_w_out[i, 1])
    return _rmsnorm(x, final_g)


DEPTH_2 = 1

CTX_LEN = 256
GRID_W = 64
MIX_WIDTH = D_MODEL
HY_WIDTH = MIX_WIDTH // 2
HG_WIDTH = MIX_WIDTH - HY_WIDTH
HG_HEADS = 4
HG_HEAD_DIM = HG_WIDTH // HG_HEADS
HY_ORDER = 2
HY_SHORT = 3
HY_BANDS = 16
HY_POS_DIM = 2 * HY_BANDS + 1
HY_FILTER_HIDDEN = 64
HY_DECAY_TARGET = 1e-2
HY_FAST_DECAY = 0.3
HY_SLOW_DECAY = 1.5
HY_WINDOW_SHIFT = 0.05
CHUNK = 64
N_EXPERTS = 16
CAPACITY_FACTOR = 2
EXPERT_FF = 2 * D_MODEL
IN_COLS = 3 * HY_WIDTH + 5 * HG_WIDTH


def rmsnorm(x, g):
    xf = x.astype(jnp.float32)
    y = xf * lax.rsqrt(jnp.mean(xf * xf, axis=-1, keepdims=True) + EPS)
    return (y * g.astype(jnp.float32)).astype(x.dtype)

def modulate(h, shift, scale):
    return h * (1 + scale) + shift

def short_conv(u, w, b, n_rows):
    bn, L, C = u.shape
    row_len = L // n_rows
    pad = HY_SHORT // 2
    up = jnp.pad(u.reshape(bn, n_rows, row_len, C), ((0, 0), (0, 0), (pad, pad), (0, 0)))
    y = b + sum(up[:, :, j:j + row_len] * w[j] for j in range(HY_SHORT))
    return y.reshape(bn, L, C)

def hyena_filter_freqs(L, w1, b1, fr1, w2, b2, fr2, w3):
    C = w3.shape[1] // (HY_ORDER * 2)
    t = jnp.linspace(0.0, 1.0, L, dtype=jnp.float32)[:, None]
    w = 2.0 * math.pi * jnp.arange(L, dtype=jnp.float32)[:, None] / L
    f = jnp.linspace(1e-4, HY_BANDS - 1, HY_BANDS, dtype=jnp.float32)[None, :]
    z = jnp.concatenate([t, jnp.cos(f * w), -jnp.sin(f * w)], axis=-1)
    h = jnp.sin(fr1.astype(jnp.float32) * (z @ w1.astype(jnp.float32) + b1.astype(jnp.float32)))
    h = jnp.sin(fr2.astype(jnp.float32) * (h @ w2.astype(jnp.float32) + b2.astype(jnp.float32)))
    h = (h @ w3.astype(jnp.float32)).reshape(L, HY_ORDER, 2, C)
    min_decay = math.log(HY_DECAY_TARGET) / HY_SLOW_DECAY
    max_decay = math.log(HY_DECAY_TARGET) / HY_FAST_DECAY
    deltas = jnp.abs(jnp.linspace(min_decay, max_decay, C, dtype=jnp.float32))
    window = jnp.exp(-t * deltas[None, :]) + HY_WINDOW_SHIFT
    h = h * window[:, None, None, :]
    full = jnp.concatenate([h[:, :, 0], jnp.zeros((1, HY_ORDER, C), jnp.float32), h[:0:-1, :, 1]], axis=0)
    full = full / (jnp.sum(jnp.abs(full), axis=0, keepdims=True) + EPS)
    return jnp.fft.rfft(full, axis=0)

def long_conv(u, hf, bias):
    L = u.shape[1]
    U = jnp.fft.rfft(u, n=2 * L, axis=1)
    y = jnp.fft.irfft(U * hf[None], n=2 * L, axis=1)[:, :L]
    return y + u * bias.astype(jnp.float32)

def hyena_mixer(p, n_rows, conv_w, conv_b, filt, bias):
    L = p.shape[1]
    u = short_conv(p, conv_w, conv_b, n_rows).astype(jnp.float32)
    v, x1, x2 = jnp.split(u, 3, axis=-1)
    hf = hyena_filter_freqs(L, *filt)
    z = x1 * long_conv(v, hf[:, 0], bias[0])
    y = x2 * long_conv(z, hf[:, 1], bias[1])
    return y.astype(p.dtype)

def chunk_scan(q, k, v, logf, s0):
    bn, L, H, K = q.shape
    n = L // CHUNK

    def blocks(a):
        return a.reshape(bn, n, CHUNK, H, a.shape[-1]).swapaxes(0, 1)

    earlier_or_same = jnp.tril(jnp.ones((CHUNK, CHUNK), dtype=bool))[None, :, :, None, None]

    def step(S, inp):
        qb, kb, vb, gb = inp
        G = jnp.cumsum(gb, axis=1)
        o_inter = jnp.einsum('bthk,bhkv->bthv', qb * jnp.exp(G), S)
        decay = jnp.exp(jnp.where(earlier_or_same, G[:, :, None] - G[:, None, :], -jnp.inf))
        A = jnp.einsum('bthk,bshk,btshk->bhts', qb, kb, decay)
        o_intra = jnp.einsum('bhts,bshv->bthv', A, vb)
        G_last = G[:, -1]
        S_new = jnp.exp(G_last)[..., None] * S + jnp.einsum('bshk,bshv->bhkv', kb * jnp.exp(G_last[:, None] - G), vb)
        return S_new, o_inter + o_intra

    S_fin, o = lax.scan(step, s0, (blocks(q), blocks(k), blocks(v), blocks(logf)))
    return o.swapaxes(0, 1).reshape(bn, L, H, v.shape[-1]), S_fin

def hgrn_project(p, lb):
    bn, L, _ = p.shape
    q, i, zf, zb, g = jnp.split(p, 5, axis=-1)

    def heads(a):
        return a.reshape(bn, L, HG_HEADS, HG_HEAD_DIM)

    q = heads(jax.nn.silu(q.astype(jnp.float32)) * HG_HEAD_DIM ** -0.5)
    v = heads(i.astype(jnp.float32))

    def gate(z, lb_d):
        f = lb_d + (1.0 - lb_d) * jax.nn.sigmoid(z.astype(jnp.float32))
        return heads(1.0 - f), heads(jnp.log(f))

    return q, v, gate(zf, lb[0]), gate(zb, lb[1]), g

def hgrn_readout(o, g, norm_g):
    bn, L = o.shape[:2]
    o = rmsnorm(o, norm_g).reshape(bn, L, HG_WIDTH)
    return (o * jax.nn.silu(g.astype(jnp.float32))).astype(g.dtype)

def hgrn_mixer(p_lat, p_ctx, lb, norm_g, need_ctx):
    ql, vl, (kfl, gfl), (kbl, gbl), g_lat = hgrn_project(p_lat, lb)
    qc, vc, (kfc, gfc), (kbc, gbc), g_ctx = hgrn_project(p_ctx, lb)
    s0 = jnp.zeros((p_lat.shape[0], HG_HEADS, HG_HEAD_DIM, HG_HEAD_DIM), jnp.float32)
    flip = lambda a: a[:, ::-1]
    oc_f, S_f = chunk_scan(qc, kfc, vc, gfc, s0)
    oc_b, S_b = chunk_scan(flip(qc), flip(kbc), flip(vc), flip(gbc), s0)
    ol_f, _ = chunk_scan(ql, kfl, vl, gfl, S_f)
    ol_b, _ = chunk_scan(flip(ql), flip(kbl), flip(vl), flip(gbl), S_b)
    out_lat = hgrn_readout(ol_f + flip(ol_b), g_lat, norm_g)
    out_ctx = hgrn_readout(oc_f + flip(oc_b), g_ctx, norm_g) if need_ctx else None
    return out_lat, out_ctx

def ec_moe(h, router_w, w1, w3, w2):
    bn, N, D = h.shape
    cap = CAPACITY_FACTOR * N // N_EXPERTS
    aff = jax.nn.softmax(jnp.einsum('bnd,de->bne', h, router_w).astype(jnp.float32), axis=-1)
    gates, idx = lax.top_k(jnp.swapaxes(aff, 1, 2), cap)
    xg = jax.vmap(lambda hb, ib: hb[ib])(h, idx)
    a = jnp.einsum('becd,edf->becf', xg, w1)
    b = jnp.einsum('becd,edf->becf', xg, w3)
    y = jnp.einsum('becf,efd->becd', jax.nn.silu(a) * b, w2)
    y = y * gates[..., None].astype(y.dtype)
    return jax.vmap(lambda yb, ib: jnp.zeros((N, D), yb.dtype).at[ib.reshape(-1)].add(yb.reshape(-1, D)))(y, idx)

def second_inputs(seed: int = 0) -> dict:
    key = jax.random.key(seed)
    ks = jax.random.split(key, 28)

    def nrm(k, shape, s):
        return jax.random.normal(k, shape, jnp.float32) * s

    D, L_ = D_MODEL, DEPTH_2
    return {
        "x": nrm(ks[0], (BATCH, SEQ, D), 1.0),
        "c": nrm(ks[1], (BATCH, D), 1.0),
        "ctx": nrm(ks[2], (BATCH, CTX_LEN, D), 1.0),
        "c_ctx": nrm(ks[3], (D,), 1.0),
        "ada_w": nrm(ks[4], (L_, D, 6 * D), 0.5 * D ** -0.5),
        "ada_b": nrm(ks[5], (L_, 6 * D), 0.02),
        "norm1_g": 1.0 + nrm(ks[6], (L_, D), 0.05),
        "w_in": nrm(ks[7], (L_, D, IN_COLS), D ** -0.5),
        "hy_conv_w": nrm(ks[8], (L_, HY_SHORT, 3 * HY_WIDTH), HY_SHORT ** -0.5),
        "hy_conv_b": nrm(ks[9], (L_, 3 * HY_WIDTH), 0.02),
        "hy_pos_w1": nrm(ks[10], (L_, HY_POS_DIM, HY_FILTER_HIDDEN), HY_POS_DIM ** -0.5),
        "hy_pos_b1": nrm(ks[11], (L_, HY_FILTER_HIDDEN), 0.1),
        "hy_freq1": 1.0 + nrm(ks[12], (L_, HY_FILTER_HIDDEN), 0.1),
        "hy_pos_w2": nrm(ks[13], (L_, HY_FILTER_HIDDEN, HY_FILTER_HIDDEN), HY_FILTER_HIDDEN ** -0.5),
        "hy_pos_b2": nrm(ks[14], (L_, HY_FILTER_HIDDEN), 0.1),
        "hy_freq2": 1.0 + nrm(ks[15], (L_, HY_FILTER_HIDDEN), 0.1),
        "hy_pos_w3": nrm(ks[16], (L_, HY_FILTER_HIDDEN, HY_ORDER * 2 * HY_WIDTH), HY_FILTER_HIDDEN ** -0.5),
        "hy_bias": nrm(ks[17], (L_, HY_ORDER, HY_WIDTH), 0.5),
        "hy_norm_g": 1.0 + nrm(ks[18], (L_, HY_WIDTH), 0.05),
        "hg_lb": nrm(ks[19], (L_ + 1, 2, HG_WIDTH), 1.0),
        "hg_norm_g": 1.0 + nrm(ks[20], (L_, HG_HEAD_DIM), 0.05),
        "w_out": nrm(ks[21], (L_, MIX_WIDTH, D), MIX_WIDTH ** -0.5),
        "norm2_g": 1.0 + nrm(ks[22], (L_, D), 0.05),
        "router_w": nrm(ks[23], (L_, D, N_EXPERTS), D ** -0.5),
        "exp_w1": nrm(ks[24], (L_, N_EXPERTS, D, EXPERT_FF), D ** -0.5),
        "exp_w3": nrm(ks[25], (L_, N_EXPERTS, D, EXPERT_FF), D ** -0.5),
        "exp_w2": nrm(ks[26], (L_, N_EXPERTS, EXPERT_FF, D), EXPERT_FF ** -0.5),
        "final_g": 1.0 + nrm(ks[27], (D,), 0.05),
    }

def second_block(x, c, ctx, c_ctx, ada_w, ada_b, norm1_g, w_in, hy_conv_w, hy_conv_b, hy_pos_w1, hy_pos_b1,
              hy_freq1, hy_pos_w2, hy_pos_b2, hy_freq2, hy_pos_w3, hy_bias, hy_norm_g, hg_lb, hg_norm_g,
              w_out, norm2_g, router_w, exp_w1, exp_w3, exp_w2, final_g):
    rows = x.shape[1] // GRID_W
    lb_all = jnp.cumsum(jax.nn.softmax(hg_lb.astype(jnp.float32), axis=0), axis=0)
    xc = ctx
    s_lat = jax.nn.silu(c)
    s_ctx = jax.nn.silu(c_ctx)
    for l in range(DEPTH_2):
        last = l == DEPTH_2 - 1
        sh1, sc1, g1, sh2, sc2, g2 = jnp.split((s_lat @ ada_w[l] + ada_b[l])[:, None, :], 6, axis=-1)
        sh1c, sc1c, g1c, sh2c, sc2c, g2c = jnp.split(s_ctx @ ada_w[l] + ada_b[l], 6, axis=-1)

        h = modulate(rmsnorm(x, norm1_g[l]), sh1, sc1)
        hc = modulate(rmsnorm(xc, norm1_g[l]), sh1c, sc1c)
        p = h @ w_in[l]
        pc = hc @ w_in[l]
        filt = (hy_pos_w1[l], hy_pos_b1[l], hy_freq1[l], hy_pos_w2[l], hy_pos_b2[l], hy_freq2[l], hy_pos_w3[l])
        y_hy = hyena_mixer(p[..., :3 * HY_WIDTH], rows, hy_conv_w[l], hy_conv_b[l], filt, hy_bias[l])
        y_hg, y_hg_c = hgrn_mixer(p[..., 3 * HY_WIDTH:], pc[..., 3 * HY_WIDTH:], lb_all[l], hg_norm_g[l], not last)
        mix = jnp.concatenate([rmsnorm(y_hy, hy_norm_g[l]).astype(x.dtype), y_hg.astype(x.dtype)], axis=-1) @ w_out[l]
        x = x + g1 * mix
        if not last:
            y_hy_c = hyena_mixer(pc[..., :3 * HY_WIDTH], 1, hy_conv_w[l], hy_conv_b[l], filt, hy_bias[l])
            mix_c = jnp.concatenate([rmsnorm(y_hy_c, hy_norm_g[l]).astype(xc.dtype), y_hg_c.astype(xc.dtype)], axis=-1) @ w_out[l]
            xc = xc + g1c * mix_c

        h2 = modulate(rmsnorm(x, norm2_g[l]), sh2, sc2)
        x = x + g2 * ec_moe(h2, router_w[l], exp_w1[l], exp_w3[l], exp_w2[l])
        if not last:
            h2c = modulate(rmsnorm(xc, norm2_g[l]), sh2c, sc2c)
            xc = xc + g2c * ec_moe(h2c, router_w[l], exp_w1[l], exp_w3[l], exp_w2[l])
    return rmsnorm(x, final_g)


def setup_inputs(seed=0):
    out = dict(first_inputs(seed))
    for name, value in second_inputs(seed + 1).items():
        if name != "x":
            out[name + "_2"] = value
    return out


def reference(
    x, c, ada_w, ada_b, norm_g, ffn_w_in, ffn_w_out, final_g, rel_table, mla_w_in, mla_q_norm,
    mla_w_uq, mla_kv_norm, mla_w_ukv, mla_w_out, rwkv_mu, rwkv_w_rkv, rwkv_w0, rwkv_wd1,
    rwkv_wd2, rwkv_a0, rwkv_wa1, rwkv_wa2, rwkv_wg1, rwkv_wg2, rwkv_k_k, rwkv_k_a, rwkv_r_k,
    rwkv_gn_w, rwkv_gn_b, rwkv_w_out, moba_w_in, moba_w_out, ret_w_in, ret_gn_w, ret_gn_b,
    ret_w_out, c_2, ctx_2, c_ctx_2, ada_w_2, ada_b_2, norm1_g_2, w_in_2, hy_conv_w_2,
    hy_conv_b_2, hy_pos_w1_2, hy_pos_b1_2, hy_freq1_2, hy_pos_w2_2, hy_pos_b2_2, hy_freq2_2,
    hy_pos_w3_2, hy_bias_2, hy_norm_g_2, hg_lb_2, hg_norm_g_2, w_out_2, norm2_g_2, router_w_2,
    exp_w1_2, exp_w3_2, exp_w2_2, final_g_2,
):
    x = first_block(
        x, c, ada_w, ada_b, norm_g, ffn_w_in, ffn_w_out, final_g, rel_table, mla_w_in,
        mla_q_norm, mla_w_uq, mla_kv_norm, mla_w_ukv, mla_w_out, rwkv_mu, rwkv_w_rkv, rwkv_w0,
        rwkv_wd1, rwkv_wd2, rwkv_a0, rwkv_wa1, rwkv_wa2, rwkv_wg1, rwkv_wg2, rwkv_k_k, rwkv_k_a,
        rwkv_r_k, rwkv_gn_w, rwkv_gn_b, rwkv_w_out, moba_w_in, moba_w_out, ret_w_in, ret_gn_w,
        ret_gn_b, ret_w_out,
    )
    return second_block(
        x, c_2, ctx_2, c_ctx_2, ada_w_2, ada_b_2, norm1_g_2, w_in_2, hy_conv_w_2, hy_conv_b_2,
        hy_pos_w1_2, hy_pos_b1_2, hy_freq1_2, hy_pos_w2_2, hy_pos_b2_2, hy_freq2_2, hy_pos_w3_2,
        hy_bias_2, hy_norm_g_2, hg_lb_2, hg_norm_g_2, w_out_2, norm2_g_2, router_w_2, exp_w1_2,
        exp_w3_2, exp_w2_2, final_g_2,
    )


_drawn_inputs = setup_inputs


def setup_inputs(seed=0):
    import zlib

    import numpy as np

    out = dict(_drawn_inputs(seed))
    spreads = {}
    factors = {'mla_q_norm': 4.717,
     'rwkv_wd1': 4.492,
     'rwkv_wd2': 4.583,
     'rwkv_a0': 3.289,
     'rwkv_gn_b': 6.034,
     'ctx_2': 8.0,
     'c_ctx_2': 8.0,
     'norm1_g_2': 2.968,
     'hy_conv_b_2': 6.742,
     'hy_pos_b1_2': 3.593,
     'hy_freq1_2': 8.0,
     'hy_freq2_2': 8.0,
     'hy_norm_g_2': 4.83,
     'hg_lb_2': 6.098,
     'hg_norm_g_2': 6.924,
     'norm2_g_2': 5.123}
    for name, (base, spread) in spreads.items():
        noise = np.random.default_rng([zlib.crc32(name.encode()), seed]).standard_normal(out[name].shape)
        drawn = base * np.exp(spread * noise) if base else spread * noise
        out[name] = jnp.asarray(drawn.astype(out[name].dtype))
    for name, factor in factors.items():
        out[name] = (out[name] * factor).astype(out[name].dtype)
    return out
```

```python
from contextlib import ExitStack

import numpy as np

import concourse.bass as bass
from concourse import mybir

P = 128
D = 1024
KT = D // P
T = 256
TT = T // P
FF = 2816
FG = 256
NG = FF // FG
NFFN = 4
SLOT = 2048
NRING = 4
NADA = 4
EPS = 1e-6

HEADS = 16
NOPE, ROPE = 64, 32
QK = NOPE + ROPE
HD = 64
CH = 64
NCH = T // CH
GN_EPS = 64e-5

HYW = 512
HGH = 4
GRID = 64
NE = 16
CAP = 2 * T // NE
EFF = 2048

SEQ_MLA = 0
SEQ_RWKV = 12
SEQ_B2 = 32
SEQ_MOE = 52
PER_EXPERT = 24

ADA_FIRST = 2
N_MODS = 72 + 72 + 48

F32 = mybir.dt.float32
BF16 = mybir.dt.bfloat16
U32 = mybir.dt.uint32
ALU = mybir.AluOpType
ACT = mybir.ActivationFunctionType
AXX = mybir.AxisListType.X


def layout(sizes):
    at, out = 0, {}
    for name, n in sizes:
        out[name] = (at, n)
        at += n
    return out, at


VEC, NVEC = layout([
    ("norm_g", 48), ("final_g", 8), ("ada_b", N_MODS), ("q_norm", 3), ("kv_norm", 2),
    ("mu", 48), ("w0", 8), ("a0", 8), ("k_k", 8), ("k_a", 8), ("r_k", 8), ("gn_w", 8), ("gn_b", 8),
    ("norm1_g", 8), ("conv_w", 36), ("conv_b", 12), ("pos_b1", 1), ("freq1", 1), ("pos_b2", 1),
    ("freq2", 1), ("hy_norm_g", 4), ("hg_lb", 16), ("hg_norm_g", 1), ("norm2_g", 8), ("final_g2", 8),
    ("rw", KT * NE),
])
NLEV = 7
CON, NCON = layout([
    ("ident", P), ("ones", P), ("blk", P), ("causal", P), ("before", P), ("upto", P),
    ("low", NLEV * P), ("up", NLEV * P), ("i64", HD), ("i32", CAP), ("iota", CAP), ("rope", T), ("keep", T),
])
BIG, NBIG = layout([
    ("cos", 2 * T), ("sin", 2 * T), ("sinq", 2 * T), ("cosq", 2 * P), ("inv", 4 * T),
])
WIN, NWIN = layout([("win", TT * 2 * HYW), ("zT", T)])


def shape_constants():
    con = np.zeros((P, NCON), np.float32)

    def put(name, a):
        o, n = CON[name]
        con[:, o:o + n] = np.asarray(a).reshape(P, n)

    i = np.arange(P)
    put("ident", np.eye(P))
    put("ones", np.ones((P, P)))
    same = (i[:, None] // HD) == (i[None, :] // HD)
    put("blk", same)
    put("causal", np.where(i[None, :] <= i[:, None], 0.0, -1e30))
    put("before", same & (i[:, None] < i[None, :]))
    put("upto", same & (i[:, None] <= i[None, :]))
    low = np.zeros((P, NLEV, P), np.float32)
    for lev in range(NLEV):
        h = 1 << lev
        low[:, lev, :] = ((i[:, None] // (2 * h)) == (i[None, :] // (2 * h))) \
            & ((i[:, None] // h) % 2 == 1) & ((i[None, :] // h) % 2 == 0)
    put("low", low)
    put("up", low.transpose(2, 1, 0))
    put("i64", np.concatenate([np.eye(HD)] * 2))
    put("i32", np.concatenate([np.eye(CAP)] * 4))
    put("iota", np.broadcast_to(np.arange(CAP), (P, CAP)))
    inv = (np.float32(10000.0) ** (-np.arange(0, ROPE, 2, dtype=np.float32) / np.float32(ROPE))).astype(np.float32)
    ang = (np.arange(T, dtype=np.float32)[:, None] * inv[None, :]).astype(np.float64)
    rope = np.zeros((P, T))
    rope[64:96] = np.concatenate([np.cos(ang), np.cos(ang)], 1).T
    rope[96:128] = np.concatenate([-np.sin(ang), np.sin(ang)], 1).T
    put("rope", rope)
    put("keep", np.broadcast_to(np.arange(T) % CH != 0, (P, T)))

    big = np.zeros((P, NBIG), np.float32)

    def put_big(name, a):
        o, n = BIG[name]
        big[:, o:o + n] = np.asarray(a).reshape(P, n)

    t = np.arange(T)
    f = np.arange(T)
    turn = 2 * np.pi * ((t[:, None] * f[None, :]) % (2 * T)) / (2 * T)
    alt = 1.0 - 2.0 * (t % 2)
    cos, sin = np.cos(turn), np.sin(turn)
    sinq, cosq = sin.copy(), cos.copy()
    sinq[:, 0] = alt
    cosq[:, 0] = alt

    def by_tile(a):
        return a.reshape(TT, P, -1).transpose(1, 0, 2)

    put_big("cos", by_tile(cos))
    put_big("sin", by_tile(sin))
    put_big("sinq", by_tile(sinq))
    put_big("cosq", by_tile(cosq[:, :P]))
    ci, si = cos.T / T, sin.T / T
    ci[0] = 1.0 / (2 * T)
    si[0] = alt / (2 * T)
    put_big("inv", np.concatenate([ci, si]).reshape(4, P, T).transpose(1, 0, 2))

    pos = np.linspace(0.0, 1.0, T, dtype=np.float32)
    first, last = np.log(1e-2) / 1.5, np.log(1e-2) / 0.3
    deltas = np.abs(np.linspace(first, last, HYW, dtype=np.float32))
    window = np.exp(-pos[:, None].astype(np.float64) * deltas[None, :]) + 0.05
    both = np.stack([window, window], 1)
    both[0, 1, :] = 0.0
    omega = 2.0 * np.pi * t[:, None] / T
    band = np.linspace(1e-4, 15, 16, dtype=np.float32)[None, :].astype(np.float64)
    z = np.concatenate([pos[:, None], np.cos(band * omega), -np.sin(band * omega)], 1)
    win = np.zeros((P, NWIN), np.float32)
    o, n = WIN["win"]
    win[:, o:o + n] = both.reshape(TT, P, 2 * HYW).transpose(1, 0, 2).reshape(P, n)
    o, n = WIN["zT"]
    win[:33, o:o + n] = z.T
    lt = (np.arange(T)[None, :] < t[:, None]).astype(np.float32)
    lt = lt.reshape(TT, P, T).transpose(1, 0, 2).reshape(P, TT * T)
    return {"con": con, "big": big, "win": win, "earlier": lt}


def cols(a):
    a = np.asarray(a).reshape(-1)
    return a.reshape(-1, P).T


def k_major(w):
    k = w.shape[0] // P
    return w.reshape(k, P, -1).transpose(1, 0, 2).reshape(P, -1)


def slots(w):
    n = -(-w.shape[1] // SLOT)
    out = np.zeros((P, n * SLOT), np.float32)
    out[:, :w.shape[1]] = w
    return out.reshape(P, n, SLOT).transpose(1, 0, 2)


def lay_out(i):
    out = dict(shape_constants())
    vec = np.zeros((P, NVEC), np.float32)

    def put(name, a):
        o, n = VEC[name]
        a = np.asarray(a)
        vec[:a.shape[0], o:o + n] = a

    put("norm_g", cols(i["norm_g"]))
    put("final_g", cols(i["final_g"]))
    put("ada_b", np.concatenate([cols(i["ada_b"]), cols(i["ada_b_2"])], 1))
    put("q_norm", cols(i["mla_q_norm"]))
    put("kv_norm", cols(i["mla_kv_norm"]))
    put("mu", cols(i["rwkv_mu"]))
    for name, key in (("w0", "rwkv_w0"), ("a0", "rwkv_a0"), ("k_k", "rwkv_k_k"), ("k_a", "rwkv_k_a"),
                      ("r_k", "rwkv_r_k"), ("gn_w", "rwkv_gn_w"), ("gn_b", "rwkv_gn_b"),
                      ("norm1_g", "norm1_g_2"), ("conv_w", "hy_conv_w_2"), ("conv_b", "hy_conv_b_2"),
                      ("hy_norm_g", "hy_norm_g_2"), ("hg_lb", "hg_lb_2"), ("hg_norm_g", "hg_norm_g_2"),
                      ("norm2_g", "norm2_g_2"), ("final_g2", "final_g_2")):
        put(name, cols(i[key]))
    for name, key in (("pos_b1", "hy_pos_b1_2"), ("freq1", "hy_freq1_2"), ("pos_b2", "hy_pos_b2_2"),
                      ("freq2", "hy_freq2_2")):
        put(name, np.asarray(i[key]).reshape(-1, 1))
    put("rw", k_major(np.asarray(i["router_w_2"])[0]))
    out["vec"] = vec

    out["xT"] = k_major(np.asarray(i["x"])[0].T)
    out["ctxT"] = k_major(np.asarray(i["ctx_2"])[0].T)
    out["c_rows"] = np.broadcast_to(np.concatenate([np.asarray(i[k]).reshape(1, D) for k in ("c", "c_2", "c_ctx_2")], 1),
                                    (P, 3 * D))
    ada = np.concatenate([np.asarray(i["ada_w"])[0].T, np.asarray(i["ada_w"])[1].T, np.asarray(i["ada_w_2"])[0].T])
    out["ada"] = ada.reshape(-1, 2, P, D).transpose(0, 2, 1, 3).reshape(-1, P, 2 * D)

    w_in = np.asarray(i["ffn_w_in"]).reshape(NFFN, KT, P, 2, NG, FG).transpose(3, 0, 4, 2, 1, 5)
    out["ffn_gate"] = w_in[0].reshape(NFFN * NG, P, SLOT)
    out["ffn_up"] = w_in[1].reshape(NFFN * NG, P, SLOT)
    out["ffn_down"] = np.asarray(i["ffn_w_out"]).reshape(NFFN * NG, 2, P, D).transpose(0, 2, 1, 3).reshape(NFFN * NG, P, SLOT)

    w = np.asarray(i["mla_w_in"])[0]
    kr = w[:, 640:672]
    w = np.concatenate([w[:, :640], kr, kr, kr, kr[:, 16:], kr[:, :16]], 1)
    uq = np.asarray(i["mla_w_uq"])[0].reshape(384, HEADS, QK)
    uq = np.concatenate([uq, uq[:, :, 80:], uq[:, :, 64:80]], 2).reshape(384, HEADS * P)
    ukv = np.asarray(i["mla_w_ukv"])[0].reshape(256, HEADS, P)
    ukv = np.concatenate([ukv[:, :, :NOPE].reshape(256, D), ukv[:, :, NOPE:].reshape(256, D)], 1)
    mla = [slots(k_major(w)), slots(k_major(uq)), slots(k_major(ukv)), slots(k_major(np.asarray(i["mla_w_out"])[0]))]

    low = np.zeros((4, P, SLOT), np.float32)
    dw = np.concatenate([np.asarray(i["rwkv_wd1"])[0], np.asarray(i["rwkv_wa1"])[0]], 1)
    low[0, :, :D] = k_major(dw)
    low[0, :64, D:] = np.asarray(i["rwkv_wd2"])[0]
    low[1, :, :KT * 160] = k_major(np.asarray(i["rwkv_wg1"])[0])
    low[2, :64, :D] = np.asarray(i["rwkv_wa2"])[0]
    low[2, :, D:] = np.asarray(i["rwkv_wg2"])[0][:P]
    low[3, :32, :D] = np.asarray(i["rwkv_wg2"])[0][P:]
    rwkv = [low] + [slots(k_major(np.asarray(i["rwkv_w_rkv"])[0, n])) for n in range(3)] \
        + [slots(k_major(np.asarray(i["rwkv_w_out"])[0]))]

    w = np.asarray(i["w_in_2"])[0].reshape(KT, P, 16, 256).transpose(2, 1, 0, 3).reshape(16, P, SLOT)
    out["ring_w"] = np.concatenate(mla + rwkv + [w, slots(k_major(np.asarray(i["w_out_2"])[0]))])
    out["w1"] = np.asarray(i["exp_w1_2"])[0].reshape(NE * KT, P, EFF)
    out["w3"] = np.asarray(i["exp_w3_2"])[0].reshape(NE * KT, P, EFF)
    out["w2"] = np.asarray(i["exp_w2_2"])[0].reshape(NE * 8, 2, P, D)
    pos = np.zeros((P, P + HYW * 4), np.float32)
    pos[:33, :64] = np.asarray(i["hy_pos_w1_2"])[0]
    pos[:64, 64:128] = np.asarray(i["hy_pos_w2_2"])[0]
    pos[:64, 128:] = np.asarray(i["hy_pos_w3_2"])[0]
    out["pos_w"] = pos
    out["hy_bias"] = np.broadcast_to(np.asarray(i["hy_bias_2"]).reshape(1, 2 * HYW), (P, 2 * HYW))
    return out


def build(nc, a, out):
    with ExitStack() as ctx:
        def sb(name, n, dt=F32):
            return ctx.enter_context(nc.sbuf_tensor(name, [P, n], dt))

        sems = {}

        def sem(name):
            if name not in sems:
                sems[name] = ctx.enter_context(nc.semaphore(name))
            return sems[name]

        ring = sb("ring", NRING * SLOT)
        xT = sb("xT", KT * T)
        hT = sb("hT", KT * T)
        sq = sb("sq", KT * T)
        vec = sb("vec", NVEC)
        con = sb("con", NCON)
        mods = sb("mods", N_MODS)
        cmods = sb("cmods", 16)
        dots = sb("dots", 16)
        coef = sb("coef", 64)
        rstd = sb("rstd", T)
        sil = sb("sil", 2 * T)
        hid = sb("hid", 2 * T)
        small = sb("small", 256)
        zeros = sb("zeros", 512, BF16)
        ARENA = 33008
        arena = sb("arena", ARENA)
        FFN0 = ARENA - 3 * SLOT
        ADA0 = FFN0 - NADA * SLOT - 3 * D
        gate_w, up_w, down_w = (arena[:, FFN0 + i * SLOT:FFN0 + (i + 1) * SLOT] for i in range(3))
        c_rows = arena[:, FFN0 - 3 * D:FFN0]
        ps = ctx.enter_context(nc.psum_tensor("ps", [P, 8, 512], F32))

        def v(name, i=0, n=1):
            o, _ = VEC[name]
            return vec[:, o + i:o + i + n]

        def k(name, i=0, n=None):
            o, m = CON[name]
            return con[:, o + i:o + i + (m if n is None else n)]

        def ar(off, n):
            assert off + n <= ARENA, (off, n)
            return arena[:, off:off + n]

        def tiles(ap, b=T):
            return ap.rearrange("p (a b) -> p a b", b=b)

        x3, h3, sq3 = (tiles(t[:, :]) for t in (xT, hT, sq))
        gate3, up3 = tiles(gate_w[:, :], FG), tiles(up_w[:, :], FG)
        down3 = tiles(down_w[:, :], D)
        sil3, hid3 = tiles(sil[:, :]), tiles(hid[:, :])
        ident, ones, blk = k("ident"), k("ones"), k("blk")

        def slot(seq):
            s = seq % NRING
            return ring[:, s * SLOT:(s + 1) * SLOT]

        def ada_slot(j):
            return tiles(ar(ADA0 + j * SLOT, SLOT), D)

        def acc(m):
            return ps[:, 2 + m // 2, (m % 2) * T:(m % 2 + 1) * T]

        def half(bank, m):
            return ps[:, bank + m // 2, (m % 2) * T:(m % 2 + 1) * T]

        def bc(ap, n):
            return ap.unsqueeze(2).to_broadcast([ap.shape[0], ap.shape[1], n])

        def bcm(ap, n):
            return ap.unsqueeze(1).to_broadcast([ap.shape[0], n, ap.shape[1]])

        m_c = tiles(ar(0, 6 * T))
        m_q = tiles(ar(1536, HEADS * T))
        m_k = tiles(ar(5632, HEADS * T))
        m_v = tiles(ar(9728, TT * D), D)
        m_p0 = tiles(ar(11776, 4 * P), P)
        m_p1 = tiles(ar(12288, 4 * T))
        m_t0 = tiles(ar(13312, 4 * T))
        m_t1 = tiles(ar(14336, 4 * P), P)
        m_rope = tiles(ar(14848, 2 * T))
        m_st = ar(15360, 64)
        m_o = h3

        r_x = tiles(ar(0, 2048))
        r_g = tiles(ar(2048, 2048))
        r_b = tiles(ar(4096, 2048))
        r_r, r_k, r_v, r_a = (tiles(ar(6144 + 2048 * n, 2048)) for n in range(4))
        r_w = tiles(ar(14336, 2048))
        r_o = tiles(ar(16384, 2048))
        cb = [ar(18432 + 1024 * n, 1024).rearrange("p (a b) -> p a b", b=P) for n in range(10)]
        c_r, c_a, c_b, c_k, c_ab, c_ak, c_y, c_t, c_tt, c_kt = cb
        c_v, c_rk, c_rb, c_bt, c_yb = c_y, c_y, c_ab, c_t, c_ak
        c_vs, c_rhs, c_u = (tiles(ar(28672 + 512 * n, 512), HD) for n in range(3))
        c_s = tiles(sil[:, :], HD)
        r_dec = small[:, 0:KT * NCH].rearrange("p (a b) -> p a b", b=NCH)
        r_e1, r_e2, r_e3 = (tiles(ar(18432 + 2048 * n, 2048)) for n in range(3))
        c_st = small[:, 32:160]

        f_A = [tiles(ar(0 + 2560 * o, 1024), HYW) for o in range(2)]
        f_B = [tiles(ar(1024 + 2560 * o, 1024), HYW) for o in range(2)]
        f_D = [ar(2048 + 2560 * o, 512) for o in range(2)]
        big = ar(5120, NBIG)
        B0 = 5120 + NBIG
        hy_p = tiles(ar(B0, 3072))
        B1 = B0 + 3072
        f_win = ar(B1, NWIN)
        f_h = ar(B1 + NWIN, 4096).rearrange("p (t s c) -> p t s c", t=TT, c=HYW)
        f_pos = ar(B1 + NWIN + 4096, P + 2048)
        f_abs = ar(B1 + NWIN + 8320, 512)
        f_rn = tiles(ar(B1 + NWIN + 8832, 1024), HYW)
        f_sum = tiles(sq[:, 0:1024], HYW)
        f_dif = tiles(sq[:, 1024:2048], HYW)
        f_in = f_rn
        f_bias = tiles(ar(B1 + NWIN + 9856, 1024), HYW)

        def bigt(name, n):
            o, m = BIG[name]
            return big[:, o:o + m].rearrange("p (a b) -> p a b", b=n)

        g_q = tiles(ar(B1, 1024))
        g_g = tiles(ar(B1 + 1024, 1024))
        g_f = ar(B1 + 2048, 2048).rearrange("p (d h t) -> p d h t", d=2, t=T)
        g_k = ar(B1 + 4096, 2048).rearrange("p (d h t) -> p d h t", d=2, t=T)
        g_F = ar(B1 + 6144, 2048).rearrange("p (d h t) -> p d h t", d=2, t=T)
        g_E = ar(B1 + 8192, 2048).rearrange("p (d h t) -> p d h t", d=2, t=T)
        g_Q = ar(B1 + 10240, 2048).rearrange("p (d h t) -> p d h t", d=2, t=T)
        g_K = ar(B1 + 12288, 2048).rearrange("p (d h t) -> p d h t", d=2, t=T)
        g_v = tiles(ar(B1 + 14336, 1024), HYW)
        g_A = ar(B1 + 15360, 2048).rearrange("p (d t h s) -> p d t h s", d=2, t=TT, s=P)
        g_X = ar(B1 + 17408, 1024).rearrange("p (d h s) -> p d h s", d=2, s=P)
        g_S = sil[:, :].rearrange("p (h s) -> p h s", s=P), hid[:, :].rearrange("p (h s) -> p h s", s=P)
        x_f, x_k, x_E = g_F, g_E, g_Q
        x_kt = ar(B1 + 12288, 2048).rearrange("p (d t c) -> p d t c", d=2, t=TT)
        x_v = tiles(ar(B1 + 15360, 1024), HYW)
        ctx3 = tiles(ar(B1 + 6144, 2048))
        hc3 = tiles(ar(B1 + 17408, 2048))
        mix3 = h3

        y_c = tiles(ar(B1, 3072))
        y_t = ar(B1 + 3072, 3072).rearrange("p (t c) -> p t c", t=TT)
        y_cc = tiles(ar(B1 + 6144, 1024), HYW)
        y_ss = tiles(ar(B1 + 7168, 1024), HYW)
        y_z = tiles(ar(B1 + 8192, 1024), HYW)
        y_m = tiles(ar(B1 + 9216, 1024), HYW)

        e_h = tiles(ar(0, TT * D), D)
        e_aff = ar(2048, TT * NE).rearrange("p (t e) -> p t e", t=TT)
        e_rank = ar(2080, TT * NE).rearrange("p (t e) -> p t e", t=TT)
        e_tie = ar(2112, TT * NE).rearrange("p (t e) -> p t e", t=TT)
        e_row = ar(2144, T)
        e_st = ar(2400, 16)
        e_cmp = tiles(ar(8432, 8 * T))
        e_early = tiles(ar(2672, TT * T))
        e_sel = ar(3184, TT * NE * CAP).rearrange("p (t e c) -> p t e c", t=TT, c=CAP)
        e_rep = ar(4208, P)
        e_diag = tiles(ar(4336, TT * NE * P), P)
        e_back = tiles(ar(8432, NE * T))
        e_x = tiles(ar(12528, KT * NE * CAP), NE * CAP)
        e_xe = tiles(ar(16624, KT * CAP), CAP)
        e_s = ar(20976, 512)
        e_h2 = ar(21488, 512)
        e_hT = tiles(ar(22000, 512), P)
        e_y = ar(22512, 512)
        e_bk = ar(25088, T)
        o_row = tiles(ar(23024, TT * D), D)

        block = ctx.enter_context(nc.Block())

        def slot_done(seq):
            if seq < 3:
                return "mla_in", 6
            if seq < 6:
                return "mla_q", 8
            if seq < 8:
                return "mla_kv", 8
            if seq < SEQ_RWKV:
                return "proj_slot", seq - 8 + 1
            if seq < 16:
                return "rwkv_low2", 3
            if seq < 28:
                return "rkv_slot", seq - 16 + 1
            if seq < SEQ_B2:
                return "proj_slot", 4 + seq - 28 + 1
            if seq < 48:
                return "b2_unit", B2_LAST[seq - SEQ_B2] + 1
            return "proj_slot", 8 + seq - 48 + 1

        B2_UNITS = []
        for s in range(16):
            what = "hy" if s < 6 else ("q", "i", "zf", "zb", "g")[(s - 6) // 2]
            B2_UNITS.append((s, what, False))
            if what in ("i", "zf", "zb"):
                B2_UNITS.append((s, what, True))
        B2_LAST = [max(u for u, unit in enumerate(B2_UNITS) if unit[0] == s) for s in range(16)]

        @block.sync
        def _(sp):
            for dst, name in ((con, "con"), (vec, "vec"), (xT, "xT")):
                sp.dma_start(dst[:, :], a[name]).then_inc(sem("start_landed"), 16)
            sp.dma_start(c_rows, a["c_rows"]).then_inc(sem("start_landed"), 16)

            def ada_round(r, wait):
                for j in range(NADA):
                    if wait:
                        sp.wait_ge(sem("ada_used"), 4 * r - 3 + j)
                    sp.dma_start(ada_slot(j).rearrange("p a b -> p (a b)"), a["ada"][4 * r + j, :, :]) \
                        .then_inc(sem(f"ada_landed{j}"), 16)

            def ffn(n):
                with sp.Fori(0, NG) as g:
                    t = g + NG * n
                    sp.wait_ge(sem("gate_used"), t + 1)
                    sp.dma_start(gate_w[:, :], a["ffn_gate"][t, :, :]).then_inc(sem("gate_landed"), 16)
                    sp.wait_ge(sem("gate_up_ready"), 2 * t + 1)
                    sp.dma_start(up_w[:, :], a["ffn_up"][t, :, :]).then_inc(sem("up_landed"), 16)
                    sp.wait_ge(sem("down_used"), t + 1)
                    sp.dma_start(down_w[:, :], a["ffn_down"][t, :, :]).then_inc(sem("down_landed"), 16)
                    if n < 2:
                        ada_round(t + ADA_FIRST, True)

            def load(seq):
                if seq >= NRING:
                    name, n = slot_done(seq - NRING)
                    sp.wait_ge(sem(name), n)
                sp.dma_start(slot(seq), a["ring_w"][seq, :, :]).then_inc(sem(f"ring_landed{seq % NRING}"), 16)

            def expert_load(e, j):
                dst = slot(SEQ_MOE + j)
                if j < 8:
                    d = sp.dma_start(dst, a["w1"][8 * e + j, :, :])
                elif j < 16:
                    d = sp.dma_start(dst, a["w3"][8 * e + (j - 8), :, :])
                else:
                    d = sp.dma_start(tiles(dst, D), a["w2"][8 * e + (j - 16), :, :, :].rearrange("t p n -> p t n"))
                d.then_inc(sem(f"ring_landed{j % NRING}"), 16)

            for r in range(ADA_FIRST):
                ada_round(r, r > 0)
            ffn(0)
            for seq in range(SEQ_MLA, SEQ_RWKV):
                load(seq)
            ffn(1)
            ffn(2)
            for seq in range(SEQ_RWKV, SEQ_B2):
                load(seq)
            sp.wait_ge(sem("x_ready"), 5)
            for dst, name in ((big, "big"), (f_win, "win"), (f_pos, "pos_w"), (f_bias.rearrange("p a b -> p (a b)"), "hy_bias")):
                sp.dma_start(dst, a[name]).then_inc(sem("filter_landed"), 16)
            ffn(3)
            for seq in range(SEQ_B2, SEQ_B2 + NRING):
                load(seq)
            sp.wait_ge(sem("filter_done"), 2)
            sp.dma_start(ctx3.rearrange("p a b -> p (a b)"), a["ctxT"]).then_inc(sem("ctx_landed"), 16)
            for seq in range(SEQ_B2 + NRING, SEQ_MOE):
                load(seq)
            for j in range(NRING):
                sp.wait_ge(sem("proj_slot"), 8 + j + 1)
                expert_load(0, j)
            sp.wait_ge(sem("x_ready"), 8)
            sp.dma_start(e_early.rearrange("p a b -> p (a b)"), a["earlier"]).then_inc(sem("early_landed"), 16)
            with sp.Fori(0, NE - 1) as e:
                for j in range(NRING, PER_EXPERT):
                    sp.wait_ge(sem("moe_slot"), PER_EXPERT * e + (j - NRING + 1))
                    expert_load(e, j)
                for j in range(NRING):
                    sp.wait_ge(sem("moe_slot"), PER_EXPERT * e + (PER_EXPERT - NRING + j + 1))
                    expert_load(e + 1, j)
            for j in range(NRING, PER_EXPERT):
                sp.wait_ge(sem("moe_slot"), PER_EXPERT * (NE - 1) + j - NRING + 1)
                expert_load(NE - 1, j)
            sp.wait_ge(sem("row_ready"), 1)
            sp.dma_start(out.rearrange("(t p) n -> p t n", p=P), o_row).then_inc(sem("out_stored"), 16)
            sp.wait_ge(sem("out_stored"), 16)

        @block.tensor
        def _(pe):
            mm, tr = nc.tensor.matmul, nc.tensor.transpose

            def landed(seq):
                pe.wait_ge(sem(f"ring_landed{seq % NRING}"), 16 * (seq // NRING + 1))

            def norm(i):
                pe.wait_ge(sem("squares"), i + 1)
                for kt in range(KT):
                    last = mm(ps[:, 7, 0:T], ones, sq3[:, kt, :], start=kt == 0, stop=kt == KT - 1)
                last.then_inc(sem("norm_sum"), 1)

            def open_banks(b0, signals=()):
                for b in range(4):
                    mm_ = mm(ps[:, b0 + b, :], zeros[:, 0:P], zeros[:, :], start=True, stop=False, skip_group_check=True)
                    if b < len(signals):
                        mm_.then_inc(sem(signals[b]), 1)

            def ffn(n, ready):
                if n > 0:
                    pe.wait_ge(sem("h_ready"), ready)
                    open_banks(2)
                else:
                    pe.wait_ge(sem("h_ready"), ready)
                with pe.Fori(0, NG) as g:
                    t = g + NG * n
                    for ft in range(2):
                        if ft == 0:
                            pe.wait_ge(sem("gate_landed"), 16 * t + 16)
                        for kt in range(KT):
                            last = mm(ps[:, ft, 0:T], gate3[:, kt, ft * P:(ft + 1) * P], h3[:, kt, :],
                                      start=kt == 0, stop=kt == KT - 1)
                        if ft == 1:
                            last.then_inc(sem("gate_used"), 1)
                        else:
                            pe.wait_ge(sem("up_landed"), 16 * t + 16)
                        for kt in range(KT):
                            last = mm(ps[:, ft, T:2 * T], up3[:, kt, ft * P:(ft + 1) * P], h3[:, kt, :],
                                      start=kt == 0, stop=kt == KT - 1)
                        last.then_inc(sem("gate_up_ready"), 1)
                    pe.wait_ge(sem("down_landed"), 16 * t + 16)
                    for ft in range(2):
                        pe.wait_ge(sem("hid_ready"), 2 * t + ft + 1)
                        for m in range(KT):
                            last = mm(acc(m), down3[:, ft, m * P:(m + 1) * P], hid3[:, ft, :],
                                      start=False, stop=True, skip_group_check=True)
                    last.then_inc(sem("down_used"), 1)

            def k_outer(out_of, seq0, rhs3, done):
                for kt in range(KT):
                    if kt % 2 == 0:
                        landed(seq0 + kt // 2)
                    for m in range(KT):
                        last = mm(out_of(m), slot(seq0 + kt // 2)[:, (kt % 2) * D + m * P:(kt % 2) * D + (m + 1) * P],
                                  rhs3[:, kt, :], start=(kt == 0 and m % 2 == 0), stop=kt == KT - 1,
                                  skip_group_check=True)
                    if kt % 2 == 1:
                        last.then_inc(sem(done), 1)

            def mla():
                pe.wait_ge(sem("h_ready"), 2)
                for s in range(3):
                    landed(s)
                for m in range(6):
                    for kt in range(KT):
                        last = mm(half(0, m), ring[:, kt * 768 + m * P:kt * 768 + (m + 1) * P], h3[:, kt, :],
                                  start=kt == 0, stop=kt == KT - 1)
                    last.then_inc(sem("mla_in"), 1)
                pe.wait_ge(sem("mla_c"), 4)
                for o, k0, k1 in ((0, 0, 3), (T, 3, 5)):
                    for kt in range(k0, k1):
                        last = mm(ps[:, 3, o:o + T], ones, sq3[:, kt, :], start=kt == k0, stop=kt == k1 - 1)
                last.then_inc(sem("mla_in"), 1)
                pe.wait_ge(sem("mla_normed"), 1)
                for s in range(3, 6):
                    landed(s)
                for h in range(HEADS):
                    for kt in range(3):
                        last = mm(half(0, h), slot(3 + kt)[:, h * P:(h + 1) * P], m_c[:, kt, :],
                                  start=kt == 0, stop=kt == 2)
                    if h % 2:
                        last.then_inc(sem("mla_q"), 1)
                for s in (6, 7):
                    landed(s)
                pe.wait_ge(sem("mla_q_nope"), 8)
                pe.wait_ge(sem("mla_q_rope"), 8)
                for i in range(8):
                    for kt in range(2):
                        last = mm(half(0, i), slot(6 + kt)[:, i * P:(i + 1) * P], m_c[:, 3 + kt, :],
                                  start=kt == 0, stop=kt == 1)
                    if i % 2:
                        last.then_inc(sem("mla_kv"), 1)
                for i in range(4):
                    tt, hb = i // 2, i % 2
                    for kt in range(2):
                        last = mm(ps[:, 4 + i, :], m_c[:, 3 + kt, tt * P:(tt + 1) * P],
                                  slot(6 + kt)[:, D + hb * 512:D + (hb + 1) * 512], start=kt == 0, stop=kt == 1)
                    last.then_inc(sem("mla_kv"), 1)

                def scores(b):
                    s = 3 * (b % 2)
                    if b == 0:
                        pe.wait_ge(sem("mla_k_nope"), 8)
                        pe.wait_ge(sem("mla_k_rope"), 1)
                        pe.wait_ge(sem("mla_v"), 4)
                    if b >= 2:
                        pe.wait_ge(sem("mla_o"), b - 1)
                    for hh in range(4):
                        h = 4 * b + hh
                        mm(ps[:, s, hh * P:(hh + 1) * P], m_q[0:QK, h, 0:P], m_k[0:QK, h, 0:P], start=True, stop=True)
                        last = mm(half(s + 1, hh), m_q[0:QK, h, P:T], m_k[0:QK, h, :], start=True, stop=True)
                    last.then_inc(sem("mla_scores"), 1)

                scores(0)
                for b in range(4):
                    s = 3 * (b % 2)
                    if b < 3:
                        scores(b + 1)
                    pe.wait_ge(sem("mla_probs"), b + 1)
                    if b >= 1:
                        pe.wait_ge(sem("mla_t0"), b)
                    for hh in range(4):
                        o = (hh % 2) * T
                        tr(ps[:, 6 + hh // 2, o:o + P], m_p0[:, hh, :], ident)
                        tr(ps[:, 6 + hh // 2, o + P:o + T], m_p1[:, hh, 0:P], ident)
                        last = tr(ps[:, s, hh * P:(hh + 1) * P], m_p1[:, hh, P:T], ident)
                    last.then_inc(sem("mla_turned"), 1)
                    pe.wait_ge(sem("mla_t0"), b + 1)
                    pe.wait_ge(sem("mla_t1"), b + 1)
                    for hh in range(4):
                        h, r, o = 4 * b + hh, 64 * (hh % 2), (hh // 2) * T
                        mm(ps[r:r + 64, s + 1, o:o + T], m_v[:, 0, h * 64:h * 64 + 64], m_t0[:, hh, :],
                           start=True, stop=False, skip_group_check=True)
                        last = mm(ps[r:r + 64, s + 1, o + P:o + T], m_v[:, 1, h * 64:h * 64 + 64], m_t1[:, hh, :],
                                  start=False, stop=True, skip_group_check=True)
                    last.then_inc(sem("mla_pv"), 1)
                pe.wait_ge(sem("mla_o"), 4)
                k_outer(acc, 8, m_o, "proj_slot")

            def bank8(b, kt):
                return ps[:, b + kt // 4, (kt % 4) * P:(kt % 4 + 1) * P]

            def rwkv():
                pe.wait_ge(sem("rwkv_mix"), 1)
                landed(12)
                for n, (buf, o) in enumerate(((r_g, 0), (r_b, 64))):
                    pe.wait_ge(sem("rwkv_mix"), n + 1)
                    for kt in range(KT):
                        last = mm(ps[0:64, 6 - n, 0:T], slot(12)[:, kt * P + o:kt * P + o + 64], buf[:, kt, :],
                                  start=kt == 0, stop=kt == KT - 1)
                    last.then_inc(sem("rwkv_low1"), 1)
                pe.wait_ge(sem("rwkv_mix"), 3)
                landed(13)
                for o, w in ((0, P), (P, 32)):
                    for kt in range(KT):
                        last = mm(ps[0:w, 7, 2 * o:2 * o + T], slot(13)[:, kt * 160 + o:kt * 160 + o + w], r_g[:, kt, :],
                                  start=kt == 0, stop=kt == KT - 1)
                last.then_inc(sem("rwkv_low1"), 1)
                pe.wait_ge(sem("rwkv_low"), 1)
                for m in range(KT):
                    last = mm(half(0, m), slot(12)[0:64, D + m * P:D + (m + 1) * P], hid3[0:64, 0, :], start=True, stop=True)
                last.then_inc(sem("rwkv_low2"), 1)
                landed(14)
                pe.wait_ge(sem("rwkv_low"), 2)
                pe.wait_ge(sem("rwkv_sig"), 1)
                for m in range(KT):
                    last = mm(half(0, m), slot(14)[0:64, m * P:(m + 1) * P], hid3[0:64, 1, :], start=True, stop=True)
                last.then_inc(sem("rwkv_low2"), 1)
                landed(15)
                pe.wait_ge(sem("rwkv_low"), 3)
                pe.wait_ge(sem("rwkv_sig"), 2)
                for m in range(KT):
                    mm(half(0, m), slot(14)[:, D + m * P:D + (m + 1) * P], sil3[:, 0, :], start=True, stop=False)
                    last = mm(half(0, m), slot(15)[:, m * P:(m + 1) * P], sil3[:, 1, :], start=False, stop=True)
                last.then_inc(sem("rwkv_low2"), 1)
                pe.wait_ge(sem("rwkv_mix"), 4)
                k_outer(lambda m: half(4, m), 16, r_b, "rkv_slot")
                pe.wait_ge(sem("rwkv_sig"), 3)
                pe.wait_ge(sem("rwkv_mix"), 5)
                k_outer(lambda m: half(0, m), 20, r_g, "rkv_slot")
                pe.wait_ge(sem("rwkv_rkv"), 1)
                pe.wait_ge(sem("rwkv_mix"), 6)
                k_outer(lambda m: half(4, m), 24, r_b, "rkv_slot")
                pe.wait_ge(sem("rwkv_kk2"), 1)
                for b in range(4):
                    last = mm(ps[:, b, :], blk, sq[:, b * 512:(b + 1) * 512], start=True, stop=True)
                last.then_inc(sem("rwkv_sums"), 1)
                pe.wait_ge(sem("rwkv_prod"), 1)
                for b in range(4):
                    last = mm(ps[:, 4 + b, :], blk, r_b[:, 2 * b:2 * b + 2, :].rearrange("p a b -> p (a b)"),
                              start=True, stop=True)
                last.then_inc(sem("rwkv_sums"), 1)
                for c in range(NCH):
                    pe.wait_ge(sem("rw_blocks"), c + 1)
                    pe.wait_ge(sem("rw_blocks_k"), 6 * (c + 1))
                    for kt in range(KT):
                        last = mm(bank8(0, kt), c_b[:, kt, :], c_a[:, kt, :], start=True, stop=True)
                    last.then_inc(sem("rw_ab"), 1)
                    for kt in range(KT):
                        mm(bank8(2, kt), c_k[:, kt, :], c_a[:, kt, :], start=True, stop=True)
                    for kt in range(KT):
                        last = mm(ps[:, 4, kt * HD:(kt + 1) * HD], c_v[:, kt, :], k("i64"), start=True, stop=True)
                    last.then_inc(sem("rw_ak"), 1)
                    for lev in range(6):
                        n = 6 * c + lev
                        if lev == 0:
                            pe.wait_ge(sem("rw_m"), 2 * c + 1)
                        else:
                            pe.wait_ge(sem("rw_T"), n)
                        for kt in range(KT):
                            last = mm(bank8(0, kt), c_ab[:, kt, :], c_t[:, kt, :], start=True, stop=True)
                        last.then_inc(sem("rw_Y"), 1)
                        pe.wait_ge(sem("rw_Ys"), n + 1)
                        if lev == 0:
                            pe.wait_ge(sem("rw_m"), 2 * c + 2)
                            if c >= 1:
                                pe.wait_ge(sem("rw_y"), c)
                        for kt in range(KT):
                            mm(bank8(2, kt), c_tt[:, kt, :], c_y[:, kt, :], start=True, stop=True)
                        for kt in range(KT):
                            last = mm(bank8(5, kt), c_y[:, kt, :], c_tt[:, kt, :], start=True, stop=True)
                        last.then_inc(sem("rw_Z"), 1)
                    pe.wait_ge(sem("rw_T"), 6 * c + 6)
                    for kt in range(KT):
                        last = mm(bank8(0, kt), c_b[:, kt, :], c_r[:, kt, :], start=True, stop=True)
                    last.then_inc(sem("rw_rb"), 1)
                    for kt in range(KT):
                        last = mm(bank8(2, kt), c_k[:, kt, :], c_r[:, kt, :], start=True, stop=True)
                    last.then_inc(sem("rw_rb"), 1)
                    for kt in range(KT):
                        last = tr(bank8(5, kt), c_b[:, kt, :], ident)
                    last.then_inc(sem("rw_turned"), 1)
                    pe.wait_ge(sem("rw_vs"), c + 1)
                    if c >= 1:
                        pe.wait_ge(sem("rw_S"), c)
                    for kt in range(KT):
                        o = ps[:, 4, kt * HD:(kt + 1) * HD]
                        mm(o, c_a[:, kt, :], c_s[:, kt, :], start=True, stop=False)
                        last = mm(o, c_ak[:, kt, :], c_vs[:, kt, :], start=False, stop=True)
                    last.then_inc(sem("rw_rhs"), 1)
                    pe.wait_ge(sem("rw_m_rb"), 2 * c + 1)
                    for kt in range(KT):
                        last = tr(bank8(0, kt), c_k[:, kt, :], ident)
                    last.then_inc(sem("rw_turned"), 1)
                    pe.wait_ge(sem("rw_rhs_s"), c + 1)
                    for kt in range(KT):
                        last = mm(ps[:, 7, kt * HD:(kt + 1) * HD], c_tt[:, kt, :], c_rhs[:, kt, :], start=True, stop=True)
                    last.then_inc(sem("rw_u"), 1)
                    pe.wait_ge(sem("rw_u_s"), c + 1)
                    pe.wait_ge(sem("rw_m_rb"), 2 * c + 2)
                    for kt in range(KT):
                        o = ps[:, 4, kt * HD:(kt + 1) * HD]
                        mm(o, c_r[:, kt, :], c_s[:, kt, :], start=True, stop=False)
                        mm(o, c_rb[:, kt, :], c_u[:, kt, :], start=False, stop=False)
                        last = mm(o, c_rk[:, kt, :], c_vs[:, kt, :], start=False, stop=True)
                    last.then_inc(sem("rw_o"), 1)
                    pe.wait_ge(sem("rw_tok"), 2 * c + 2)
                    for kt in range(KT):
                        o = ps[:, 7, kt * HD:(kt + 1) * HD]
                        mm(o, c_bt[:, kt, :], c_u[:, kt, :], start=True, stop=False)
                        last = mm(o, c_kt[:, kt, :], c_vs[:, kt, :], start=False, stop=True)
                    last.then_inc(sem("rw_ds"), 1)
                    pe.wait_ge(sem("rw_yb"), c + 1)
                    for kt in range(KT):
                        last = mm(ps[:, 5, kt * HD:(kt + 1) * HD], c_yb[:, kt, :], k("i64"), start=True, stop=True)
                    last.then_inc(sem("rw_out"), 1)
                pe.wait_ge(sem("rwkv_y"), 1)
                k_outer(acc, 28, r_w, "proj_slot")

            def filters():
                pe.wait_ge(sem("filter_landed"), 64)
                pe.wait_ge(sem("x_ready"), 6)
                zT = f_win[0:33, WIN["zT"][0]:WIN["zT"][0] + T]
                mm(ps[0:64, 0, 0:T], f_pos[0:33, 0:64], zT, start=True, stop=True).then_inc(sem("filter_mm"), 1)
                pe.wait_ge(sem("filter_sin"), 1)
                mm(ps[0:64, 1, 0:T], f_pos[0:64, 64:128], f_in[0:64, 0, 0:T], start=True, stop=True) \
                    .then_inc(sem("filter_mm"), 1)
                pe.wait_ge(sem("filter_sin"), 2)
                for tt in range(TT):
                    for q in range(4):
                        mm(ps[:, 4 * tt + q, :], f_in[0:64, 0, tt * P:(tt + 1) * P],
                           f_pos[0:64, P + q * HYW:P + (q + 1) * HYW], start=True, stop=True).then_inc(sem("filter_mm"), 1)
                for o in range(2):
                    pe.wait_ge(sem("filter_abs"), o + 1)
                    for n in range(4):
                        last = mm(ps[:, o, :], ones, sq[:, n * HYW:(n + 1) * HYW], start=n == 0, stop=n == 3)
                    last.then_inc(sem("filter_l1"), 1)
                cos, sin, cosq = bigt("cos", T), bigt("sin", T), bigt("cosq", P)
                for o in range(2):
                    pe.wait_ge(sem("filter_sides"), o + 1)
                    if o == 1:
                        pe.wait_ge(sem("filter_done"), 1)
                    for ft in range(2):
                        for tt in range(TT):
                            mm(ps[:, 2 + ft, :], cos[:, tt, ft * P:(ft + 1) * P], f_sum[:, tt, :], start=tt == 0, stop=tt == 1)
                        for tt in range(TT):
                            mm(ps[:, 4 + ft, :], sin[:, tt, ft * P:(ft + 1) * P], f_dif[:, tt, :], start=tt == 0, stop=tt == 1)
                    for tt in range(TT):
                        last = mm(ps[:, 6, :], cosq[:, tt, :], f_sum[:, tt, :], start=tt == 0, stop=tt == 1)
                    last.then_inc(sem("filter_freq"), 1)

            def b2_in():
                pe.wait_ge(sem("h_ready"), 7)
                for u, (s, what, context) in enumerate(B2_UNITS):
                    if context:
                        pe.wait_ge(sem("h_ready"), 8)
                    src = hc3 if context else h3
                    landed(SEQ_B2 + s)
                    if u >= 7:
                        pe.wait_ge(sem("b2_evac"), u - 6)
                    w = tiles(slot(SEQ_B2 + s), 256)
                    for j in range(2):
                        o = ps[:, u % 7, j * T:(j + 1) * T]
                        for kt in range(KT):
                            if what == "i":
                                last = mm(o, src[:, kt, j * P:(j + 1) * P], w[:, kt, :], start=kt == 0, stop=kt == KT - 1)
                            else:
                                last = mm(o, w[:, kt, j * P:(j + 1) * P], src[:, kt, :], start=kt == 0, stop=kt == KT - 1)
                    last.then_inc(sem("b2_unit"), 1)

            def hgrn():
                pe.wait_ge(sem("hg_gates"), 1)
                pe.wait_ge(sem("b2_evac"), len(B2_UNITS))
                for d in range(2):
                    for tt in range(TT):
                        for h in range(HGH):
                            last = tr(ps[:, 2 * d + tt, h * P:(h + 1) * P], x_k[:, d, h, tt * P:(tt + 1) * P], ident)
                        last.then_inc(sem("hg_ctx_t"), 1)
                pe.wait_ge(sem("hg_ctx_kt"), 4)
                for d in range(2):
                    for h in range(HGH):
                        for tt in range(TT):
                            last = mm(ps[:, 4 + d, h * P:(h + 1) * P], x_kt[:, d, tt, h * P:(h + 1) * P],
                                      x_v[:, tt, h * P:(h + 1) * P], start=tt == 0, stop=tt == 1)
                    last.then_inc(sem("hg_state"), 1)

                def level(n, kk, qq):
                    for d in range(2):
                        for tt in range(TT):
                            for h in range(HGH):
                                last = mm(ps[:, 4 * (n % 2) + 2 * d + tt, h * P:(h + 1) * P],
                                          kk(d)[:, h, tt * P:(tt + 1) * P], qq(d)[:, h, tt * P:(tt + 1) * P],
                                          start=True, stop=True)
                    last.then_inc(sem("hg_level"), 1)

                pe.wait_ge(sem("hg_gates"), 2)
                level(0, lambda d: g_k[:, d], lambda d: g_q)
                pe.wait_ge(sem("hg_state_s"), 2)
                for lev in range(NLEV):
                    pe.wait_ge(sem("hg_scaled"), lev + 1)
                    if lev >= 1:
                        pe.wait_ge(sem("hg_taken"), lev)
                    level(lev + 1, lambda d: g_K[:, d], lambda d: g_Q[:, d])
                pe.wait_ge(sem("hg_scaled"), NLEV + 1)
                pe.wait_ge(sem("hg_taken"), NLEV)
                for d in range(2):
                    for h in range(HGH):
                        last = mm(ps[:, d, h * P:(h + 1) * P], g_K[:, d, h, d * P:(d + 1) * P],
                                  g_Q[:, d, h, (1 - d) * P:(2 - d) * P], start=True, stop=True)
                last.then_inc(sem("hg_cross"), 1)
                pe.wait_ge(sem("hg_cross_s"), 1)
                pe.wait_ge(sem("hg_taken"), NLEV + 1)
                pe.wait_ge(sem("hg_scaled"), NLEV + 2)
                for h in range(HGH):
                    o, e0 = half(2, h), slice(h * P, (h + 1) * P)
                    mm(o, g_S[0][:, h, :], g_Q[:, 0, h, :], start=True, stop=False, skip_group_check=True)
                    mm(o, g_S[1][:, h, :], g_Q[:, 1, h, :], start=False, stop=False, skip_group_check=True)
                    for d in range(2):
                        for tt in range(TT):
                            mm(o[:, tt * P:(tt + 1) * P], g_v[:, tt, e0], g_A[:, d, tt, h, :],
                               start=False, stop=False, skip_group_check=True)
                        last = mm(o[:, (1 - d) * P:(2 - d) * P], g_v[:, d, e0], g_X[:, d, h, :],
                                  start=False, stop=d == 1, skip_group_check=True)
                last.then_inc(sem("hg_out"), 1)
                pe.wait_ge(sem("hg_os"), 2)
                for b in range(2):
                    last = mm(ps[:, 4 + b, :], ones, sq[:, b * 512:(b + 1) * 512], start=True, stop=True)
                last.then_inc(sem("hg_out"), 1)

            def hyena():
                pe.wait_ge(sem("hy_conv"), 1)
                for tt in range(TT):
                    for w in range(3):
                        for j in range(4):
                            last = tr(ps[:, 3 * tt + w, j * P:(j + 1) * P], y_c[:, 4 * w + j, tt * P:(tt + 1) * P], ident)
                        last.then_inc(sem("hy_turned"), 1)
                cos, sinq, inv = bigt("cos", T), bigt("sinq", T), bigt("inv", T)
                for o in range(2):
                    if o == 0:
                        pe.wait_ge(sem("hy_rows"), 6)
                    else:
                        pe.wait_ge(sem("hy_z"), 1)
                    for ft in range(2):
                        for b, table in ((0, cos), (2, sinq)):
                            for tt in range(TT):
                                u = y_t[:, tt, 0:HYW] if o == 0 else y_z[:, tt, :]
                                last = mm(ps[:, b + ft, :], table[:, tt, ft * P:(ft + 1) * P], u, start=tt == 0, stop=tt == 1)
                    last.then_inc(sem("hy_u"), 1)
                    pe.wait_ge(sem("hy_y"), o + 1)
                    for tt in range(TT):
                        for f in range(4):
                            y = y_cc[:, f, :] if f < 2 else y_ss[:, f - 2, :]
                            last = mm(ps[:, 4 + tt, :], inv[:, f, tt * P:(tt + 1) * P], y, start=f == 0, stop=f == 3)
                    last.then_inc(sem("hy_v"), 1)
                pe.wait_ge(sem("hy_normed"), 1)
                for m in range(4):
                    for tt in range(TT):
                        last = tr(ps[:, m, tt * P:(tt + 1) * P],
                                  y_m[:, tt, m * P:(m + 1) * P], ident)
                    last.then_inc(sem("hy_back"), 1)
                pe.wait_ge(sem("hy_mixed"), 4)
                pe.wait_ge(sem("hg_mixed"), 1)
                k_outer(acc, 48, mix3, "proj_slot")

            def routing():
                pe.wait_ge(sem("h_ready"), 9)
                for tt in range(TT):
                    for kt in range(KT):
                        last = tr(ps[:, 2 * tt + kt // 4, (kt % 4) * P:(kt % 4 + 1) * P], h3[:, kt, tt * P:(tt + 1) * P], ident)
                last.then_inc(sem("e_turned"), 1)
                for tt in range(TT):
                    for kt in range(KT):
                        last = mm(ps[:, 4, tt * NE:(tt + 1) * NE], h3[:, kt, tt * P:(tt + 1) * P], v("rw", kt * NE, NE),
                                  start=kt == 0, stop=kt == KT - 1)
                last.then_inc(sem("e_turned"), 1)
                pe.wait_ge(sem("e_aff"), 2)
                for tt in range(TT):
                    last = tr(ps[0:NE, 5, tt * P:(tt + 1) * P], e_aff[:, tt, :], ident)
                last.then_inc(sem("e_aff_t"), 1)
                pe.wait_ge(sem("e_rows"), 3)
                for e in range(NE):
                    mm(half(0, e), ident[0:NE, e:e + 1].to_broadcast([NE, P]), e_row[0:NE, :], start=True, stop=True) \
                        .then_inc(sem("e_spread"), 1)
                pe.wait_ge(sem("e_select"), 1)
                rep = ar(16880, 4096).rearrange("p (t e c) -> p t e c", t=TT, c=P)
                for e in range(NE):
                    for tt in range(TT):
                        last = mm(half(0, e)[:, tt * P:(tt + 1) * P], rep[:, tt, e, :], e_diag[:, tt * NE + e, :],
                                  start=True, stop=True)
                    if e % 2:
                        last.then_inc(sem("e_backs"), 1)
                for kt in range(KT):
                    pe.wait_ge(sem("e_back"), kt + 1)
                    for tt in range(TT):
                        last = mm(ps[:, kt, :], e_h[:, tt, kt * P:(kt + 1) * P],
                                  e_sel[:, tt, :, :].rearrange("p e c -> p (e c)"), start=tt == 0, stop=tt == 1)
                    last.then_inc(sem("e_gathers"), 1)
                pe.wait_ge(sem("e_gather"), KT)

            def experts():
                open_banks(4)
                with pe.Fori(0, NE) as e:
                    def weights(j):
                        pe.wait_ge(sem(f"ring_landed{j % NRING}"), 16 * (PER_EXPERT // NRING) * e
                                   + 16 * ((SEQ_MOE + j) // NRING + 1))
                        return slot(SEQ_MOE + j)

                    pe.wait_ge(sem("moe_x"), e + 1)
                    for part in range(2):
                        for kt in range(KT):
                            w = weights(8 * part + kt)
                            for n in range(4):
                                last = mm(ps[32 * n:32 * n + 32, part, :], e_xe[:, kt, :], w[:, n * 512:(n + 1) * 512],
                                          start=kt == 0, stop=kt == KT - 1, skip_group_check=True)
                            last.then_inc(sem("moe_slot"), 1)
                    pe.wait_ge(sem("moe_h"), e + 1)
                    for i in range(4):
                        last = tr(ps[:, 2, i * P:(i + 1) * P], e_h2[:, i * P:(i + 1) * P], ident)
                    last.then_inc(sem("moe_turned"), 1)
                    pe.wait_ge(sem("moe_hT"), e + 1)
                    for j in range(8):
                        w = weights(16 + j)
                        for t2 in range(2):
                            n, i = (2 * j + t2) // 4, (2 * j + t2) % 4
                            for nn in range(2):
                                q = 64 * nn + 32 * t2
                                last = mm(ps[q:q + 32, 3, :], e_hT[:, i, 32 * n:32 * n + 32],
                                          w[:, t2 * D + nn * 512:t2 * D + (nn + 1) * 512],
                                          start=j == 0, stop=j == 7, skip_group_check=True)
                        last.then_inc(sem("moe_slot"), 1)
                    pe.wait_ge(sem("moe_y"), e + 1)
                    for i in range(4):
                        for nn in range(2):
                            r = slice(64 * nn, 64 * nn + 64)
                            last = mm(half(4, 4 * nn + i), e_y[r, i * P:(i + 1) * P], e_bk[r, :],
                                      start=False, stop=True, skip_group_check=True)
                    last.then_inc(sem("moe_o"), 1)

            pe.wait_ge(sem("zeros"), 1)
            open_banks(2, ("gate_used", "gate_up_ready", "down_used"))
            pe.wait_ge(sem("start_landed"), 64)
            norm(0)
            ffn(0, 1)
            norm(1)
            mla()
            norm(2)
            ffn(1, 3)
            norm(3)
            ffn(2, 4)
            norm(4)
            rwkv()
            norm(5)
            ffn(3, 6)
            filters()
            norm(6)
            norm(7)
            norm(8)
            b2_in()
            hgrn()
            hyena()
            norm(9)
            routing()
            experts()
            norm(10)
            pe.wait_ge(sem("h_ready"), 10)
            for tt in range(TT):
                for kt in range(KT):
                    last = tr(ps[:, 2 * tt + kt // 4, (kt % 4) * P:(kt % 4 + 1) * P], h3[:, kt, tt * P:(tt + 1) * P], ident)
            last.then_inc(sem("row_turned"), 1)

        @block.scalar
        def _(act):
            f = nc.scalar.activation

            def copy(dst, src):
                return f(dst, src, ACT.Copy)

            def two(ap):
                return ap.rearrange("p b (h t) -> p (b h) t", t=T)

            n_root = [0]

            def root(buf):
                n_root[0] += 1
                act.wait_ge(sem("root_in"), n_root[0])
                f(buf, buf, ACT.Sqrt).then_inc(sem("root_out"), 1)

            def squares(i, src):
                if i >= 1:
                    act.wait_ge(sem("norm_sum"), i)
                f(sq3, src, ACT.Square).then_inc(sem("squares"), 1)
                root(rstd[:, :])

            def norm(i, ready):
                act.wait_ge(sem("x_ready"), ready)
                squares(i, x3)

            def ffn(n):
                with act.Fori(0, NG) as g:
                    t = g + NG * n
                    for ft in range(2):
                        act.wait_ge(sem("gate_up_ready"), 2 * t + ft + 2)
                        f(sil3[:, ft, :], ps[:, ft, 0:T], ACT.Silu).then_inc(sem("silu_ready"), 1)

            def mla():
                for b in range(3):
                    act.wait_ge(sem("mla_in"), 2 * b + 2)
                    copy(m_c[:, 2 * b:2 * b + 2, :], ps[:, b, :].rearrange("p (h t) -> p h t", t=T)).then_inc(sem("mla_c"), 1)
                act.wait_ge(sem("mla_c"), 3)
                act.wait_ge(sem("norm_sum"), 2)
                f(sq3[:, 0:5, :], m_c[:, 0:5, :], ACT.Square).then_inc(sem("mla_c"), 1)
                root(m_rope)
                for b in range(8):
                    act.wait_ge(sem("mla_q"), b + 1)
                    copy(m_q[0:64, 2 * b:2 * b + 2, :], ps[0:64, b, :].rearrange("p (h t) -> p h t", t=T)) \
                        .then_inc(sem("mla_q_nope"), 1)
                for b in range(4):
                    act.wait_ge(sem("mla_kv"), b + 1)
                    for o in range(2):
                        copy(m_k[0:64, 4 * b + o:4 * b + o + 3:2, :],
                             ps[64 * o:64 * o + 64, b, :].rearrange("p (h t) -> p h t", t=T)).then_inc(sem("mla_k_nope"), 1)
                for b in range(4):
                    s, st = 3 * (b % 2), m_st[:, 32 * (b % 2):32 * (b % 2) + 32]
                    act.wait_ge(sem("mla_max"), b + 1)
                    if b >= 1:
                        act.wait_ge(sem("mla_turned"), b)
                    for hh in range(4):
                        f(m_p0[:, hh, :], ps[:, s, hh * P:(hh + 1) * P], ACT.Exp, bias=st[:, 8 + hh:9 + hh],
                          scale=QK ** -0.5, accum_out=st[:, 16 + hh:17 + hh]).then_inc(sem("mla_exp"), 1)
                        f(m_p1[:, hh, :], half(s + 1, hh), ACT.Exp, bias=st[:, 12 + hh:13 + hh],
                          scale=QK ** -0.5, accum_out=st[:, 20 + hh:21 + hh]).then_inc(sem("mla_exp"), 1)
                    act.wait_ge(sem("mla_turned"), b + 1)
                    copy(m_t0, two(ps[:, 6:8, :])).then_inc(sem("mla_t0"), 1)
                    act.wait_ge(sem("mla_pv"), b + 1)
                    copy(m_o[:, 2 * b:2 * b + 2, :], ps[:, s + 1, :].rearrange("p (h t) -> p h t", t=T)) \
                        .then_inc(sem("mla_o"), 1)

            def eight(b):
                return ps[:, b:b + 2, :].rearrange("p b (k s) -> p (b k) s", s=P)

            def rwkv():
                act.wait_ge(sem("rwkv_low1"), 1)
                f(hid3[0:64, 0, :], ps[0:64, 6, 0:T], ACT.Tanh).then_inc(sem("rwkv_low"), 1)
                act.wait_ge(sem("rwkv_low1"), 2)
                copy(hid3[0:64, 1, :], ps[0:64, 5, 0:T]).then_inc(sem("rwkv_low"), 1)
                act.wait_ge(sem("rwkv_low1"), 3)
                act.wait_ge(sem("zeros"), 2)
                f(sil3[0:32, 1, :], ps[0:32, 7, T:2 * T], ACT.Sigmoid)
                f(sil3[:, 0, :], ps[:, 7, 0:T], ACT.Sigmoid).then_inc(sem("rwkv_low"), 1)
                for n, (dst, bias) in enumerate(((r_w, "w0"), (r_a, "a0"))):
                    act.wait_ge(sem("rwkv_low2"), n + 1)
                    for m in range(KT):
                        last = f(dst[:, m, :], half(0, m), ACT.Sigmoid, bias=v(bias, m))
                    last.then_inc(sem("rwkv_sig"), 1)
                act.wait_ge(sem("rwkv_low2"), 3)
                copy(r_o, two(ps[:, 0:4, :])).then_inc(sem("rwkv_sig"), 1)
                act.wait_ge(sem("rkv_slot"), 4)
                copy(r_r, two(ps[:, 4:8, :])).then_inc(sem("rwkv_rkv"), 1)
                act.wait_ge(sem("rkv_slot"), 8)
                copy(r_k, two(ps[:, 0:4, :]))
                act.wait_ge(sem("rwkv_mix"), 6)
                for m in range(KT):
                    last = f(r_x[:, m, :], half(0, m), ACT.Copy, scale=v("k_k", m))
                last.then_inc(sem("rwkv_rkv"), 1)
                act.wait_ge(sem("rkv_slot"), 12)
                copy(r_v, two(ps[:, 4:8, :])).then_inc(sem("rwkv_rkv"), 1)
                act.wait_ge(sem("rwkv_rkv"), 3)
                f(sq3, r_x, ACT.Square).then_inc(sem("rwkv_kk2"), 1)
                root(sq3)
                act.wait_ge(sem("rwkv_G"), 1)
                f(r_dec, r_g[:, :, CH - 1::CH], ACT.Exp)
                f(r_e1, r_g, ACT.Exp).then_inc(sem("rwkv_E"), 1)
                f(r_e2, r_g, ACT.Exp, scale=-1.0).then_inc(sem("rwkv_E"), 1)
                act.wait_ge(sem("rwkv_Gp"), 1)
                f(r_e3, r_w, ACT.Exp).then_inc(sem("rwkv_E"), 1)
                for c in range(NCH):
                    act.wait_ge(sem("rw_ak"), c + 1)
                    copy(c_vs, ps[:, 4, :].rearrange("p (k s) -> p k s", s=HD)).then_inc(sem("rw_vs"), 1)
                    for lev in range(6):
                        act.wait_ge(sem("rw_Y"), 6 * c + lev + 1)
                        copy(c_y, eight(0)).then_inc(sem("rw_Ys"), 1)
                    act.wait_ge(sem("rw_turned"), 2 * c + 1)
                    copy(c_bt, eight(5)).then_inc(sem("rw_tok"), 1)
                    act.wait_ge(sem("rw_rhs"), c + 1)
                    copy(c_rhs, ps[:, 4, :].rearrange("p (k s) -> p k s", s=HD)).then_inc(sem("rw_rhs_s"), 1)
                    act.wait_ge(sem("rw_u"), c + 1)
                    copy(c_u, ps[:, 7, :].rearrange("p (k s) -> p k s", s=HD)).then_inc(sem("rw_u_s"), 1)
                    act.wait_ge(sem("rw_turned"), 2 * c + 2)
                    copy(c_kt, eight(0)).then_inc(sem("rw_tok"), 1)
                    root(c_st[:, 8:16])
                    act.wait_ge(sem("rw_out"), c + 1)
                    copy(r_w[:, :, c * CH:(c + 1) * CH], ps[:, 5, :].rearrange("p (k s) -> p k s", s=CH)) \
                        .then_inc(sem("rw_y"), 1)

            def filters():
                act.wait_ge(sem("hg_lb_in"), 1)
                f(small[:, 168:184], small[:, 168:184], ACT.Exp).then_inc(sem("hg_lb_exp"), 1)
                for n in range(2):
                    act.wait_ge(sem("filter_arg"), n + 1)
                    f(f_in[0:64, 0, 0:T], f_in[0:64, 0, T:2 * T], ACT.Sin).then_inc(sem("filter_sin"), 1)
                sides = sq[:, :].rearrange("p (t s c) -> p t s c", t=TT, c=HYW)
                act.wait_ge(sem("filter_h"), 8)
                for o in range(2):
                    if o == 1:
                        act.wait_ge(sem("filter_l1"), 1)
                    for tt in range(TT):
                        last = f(sides[:, tt, :, :], f_h[:, tt, 2 * o:2 * o + 2, :], ACT.Abs)
                    last.then_inc(sem("filter_abs"), 1)

            def b2_in():
                for u, (s, what, context) in enumerate(B2_UNITS):
                    act.wait_ge(sem("b2_unit"), u + 1)
                    src = ps[:, u % 7, :]
                    src2 = src.rearrange("p (h t) -> p h t", t=T)
                    j = (s - 6) % 2
                    if what == "hy":
                        last = copy(hy_p[:, 2 * s:2 * s + 2, :], src2)
                    elif what == "q":
                        last = f(g_q[:, 2 * j:2 * j + 2, :], src2, ACT.Silu)
                    elif what == "i":
                        last = copy((x_v if context else g_v)[:, :, j * T:(j + 1) * T], src2)
                    elif what == "g":
                        last = f(g_g[:, 2 * j:2 * j + 2, :], src2, ACT.Silu)
                    else:
                        d = 0 if what == "zf" else 1
                        last = f((x_f if context else g_f)[:, d, 2 * j:2 * j + 2, :], src2, ACT.Sigmoid)
                    last.then_inc(sem("b2_evac"), 1)

            def hgrn():
                for i in range(4):
                    act.wait_ge(sem("hg_ctx_t"), i + 1)
                    copy(x_kt[:, i // 2, i % 2, :], ps[:, i, :]).then_inc(sem("hg_ctx_kt"), 1)
                act.wait_ge(sem("hg_state"), 2)
                for d in range(2):
                    copy(g_S[d], ps[:, 4 + d, :].rearrange("p (h s) -> p h s", s=P)).then_inc(sem("hg_state_s"), 1)
                act.wait_ge(sem("hg_cross"), 1)
                copy(g_X, ps[:, 0:2, :].rearrange("p d (h s) -> p d h s", s=P)).then_inc(sem("hg_cross_s"), 1)
                act.wait_ge(sem("hg_out"), 1)
                copy(g_F[:, 0], two(ps[:, 2:4, :])).then_inc(sem("hg_os"), 1)
                act.wait_ge(sem("hg_os"), 1)
                f(sq3[:, 0:4, :], g_F[:, 0], ACT.Square).then_inc(sem("hg_os"), 1)
                root(g_F[:, 1])

            def hyena():
                act.wait_ge(sem("hg_mixed"), 1)
                for m in range(12):
                    f(y_c[:, m, :], hy_p[:, m, :], ACT.Identity, scale=v("conv_w", 12 + m), bias=v("conv_b", m)) \
                        .then_inc(sem("hy_middle"), 1)
                for i in range(6):
                    act.wait_ge(sem("hy_turned"), i + 1)
                    copy(y_t[:, i // 3, (i % 3) * HYW:(i % 3 + 1) * HYW], ps[:, i, :]).then_inc(sem("hy_rows"), 1)
                act.wait_ge(sem("hy_z"), 2)
                for tt in range(TT):
                    f(sq[:, tt * HYW:(tt + 1) * HYW], y_m[:, tt, :], ACT.Square, accum_out=small[:, 208 + tt:209 + tt]) \
                        .then_inc(sem("hy_square"), 1)
                root(small[:, 208:210])
                for m in range(4):
                    act.wait_ge(sem("hy_back"), m + 1)
                    f(mix3[:, m, :], ps[:, m, 0:T], ACT.Copy, scale=v("hy_norm_g", m)).then_inc(sem("hy_mixed"), 1)

            def routing():
                act.wait_ge(sem("e_turned"), 1)
                copy(e_h, ps[:, 0:4, :].rearrange("p (t b) c -> p t (b c)", t=TT)).then_inc(sem("e_rows"), 1)
                act.wait_ge(sem("e_aff"), 1)
                f(e_aff, e_aff, ACT.Exp).then_inc(sem("e_rows"), 1)
                act.wait_ge(sem("e_aff_t"), 1)
                copy(e_row[0:NE, :], ps[0:NE, 5, 0:T]).then_inc(sem("e_rows"), 1)
                for b in range(8):
                    act.wait_ge(sem("e_backs"), b + 1)
                    copy(e_back[:, 2 * b:2 * b + 2, :], ps[:, b, :].rearrange("p (h t) -> p h t", t=T)).then_inc(sem("e_back"), 1)
                for kt in range(KT):
                    act.wait_ge(sem("e_gathers"), kt + 1)
                    copy(e_x[:, kt, :], ps[:, kt, :]).then_inc(sem("e_gather"), 1)

            def experts():
                with act.Fori(0, NE) as e:
                    act.wait_ge(sem("moe_slot"), PER_EXPERT * e + 8)
                    f(e_s, ps[:, 0, :], ACT.Silu).then_inc(sem("moe_silu"), 1)
                    act.wait_ge(sem("moe_turned"), e + 1)
                    copy(e_hT, ps[:, 2, :].rearrange("p (i c) -> p i c", c=P)).then_inc(sem("moe_hT"), 1)
                    act.wait_ge(sem("moe_slot"), PER_EXPERT * e + PER_EXPERT)
                    copy(e_y, ps[:, 3, :]).then_inc(sem("moe_y"), 1)

            act.wait_ge(sem("start_landed"), 64)
            f(c_rows, c_rows, ACT.Silu).then_inc(sem("c_ready"), 1)
            squares(0, x3)
            ffn(0)
            norm(1, 1)
            mla()
            norm(2, 2)
            ffn(1)
            norm(3, 3)
            ffn(2)
            norm(4, 4)
            rwkv()
            norm(5, 5)
            ffn(3)
            filters()
            act.wait_ge(sem("filter_done"), 2)
            norm(6, 6)
            norm(7, 7)
            act.wait_ge(sem("ctx_landed"), 16)
            squares(8, ctx3)
            b2_in()
            hgrn()
            hyena()
            norm(9, 8)
            routing()
            experts()
            norm(10, 9)
            act.wait_ge(sem("row_turned"), 1)
            copy(o_row, ps[:, 0:4, :].rearrange("p (t b) c -> p t (b c)", t=TT)).then_inc(sem("row_ready"), 1)

        @block.gpsimd
        def _(pool):
            nc.gpsimd.memset(zeros[:, :], 0.0).then_inc(sem("zeros"), 1)
            n_block = 0
            for c in range(NCH):
                cut = slice(c * CH, (c + 1) * CH)
                pool.wait_ge(sem("rwkv_prep"), 1)
                if c >= 1:
                    pool.wait_ge(sem("rw_out"), c)
                for dst, src in ((c_k, r_k), (c_v, r_v)):
                    for o in (0, 64):
                        if n_block:
                            pool.wait_ge(sem("rw_blocks_k"), n_block)
                        nc.gpsimd.tensor_copy(dst[o:o + 64, :, o:o + 64], src[o:o + 64, :, cut]).then_inc(sem("rw_blocks_k"), 1)
                        n_block += 1
                for dst in (c_t, c_tt):
                    pool.wait_ge(sem("rw_blocks_k"), n_block)
                    nc.gpsimd.tensor_copy(dst, bcm(ident, KT)).then_inc(sem("rw_blocks_k"), 1)
                    n_block += 1

        @block.vector
        def _(dve):
            n_order = [0]

            def done(ins):
                n_order[0] += 1
                ins.then_inc(sem("dve_order"), 1)
                dve.wait_ge(sem("dve_order"), n_order[0])

            tt_, ts, stt, cp = (nc.vector.tensor_tensor, nc.vector.tensor_scalar, nc.vector.scalar_tensor_tensor,
                                nc.vector.tensor_copy)
            red = nc.vector.tensor_reduce

            def two(ap):
                return ap.rearrange("p b (h t) -> p (b h) t", t=T)

            n_root = [0]

            def inverse_root(ins, buf):
                n_root[0] += 1
                ins.then_inc(sem("root_in"), 1)
                dve.wait_ge(sem("root_out"), n_root[0])
                done(nc.vector.reciprocal(buf, buf))

            def norm(i, src, dst, scale, shift=None, name="h_ready"):
                dve.wait_ge(sem("norm_sum"), i + 1)
                inverse_root(ts(rstd[:, :], ps[:, 7, 0:T], 1.0 / D, EPS, ALU.mult, ALU.add), rstd[:, :])
                done(tt_(dst, src, bcm(rstd[:, :], KT), ALU.mult))
                for m in range(KT):
                    if shift is None:
                        last = ts(dst[:, m, :], dst[:, m, :], scale[:, m:m + 1], None, ALU.mult)
                    else:
                        last = ts(dst[:, m, :], dst[:, m, :], scale[:, m:m + 1], shift[:, m:m + 1], ALU.mult, ALU.add)
                last.then_inc(sem(name), 1)

            def scale_of(at, g, src=mods, to=0):
                done(stt(out=coef[:, to:to + 8], in0=src[:, at:at + 8], scalar=1.0, in1=g, op0=ALU.add, op1=ALU.mult))

            def gate_of(at, factor):
                done(ts(coef[:, 8:16], mods[:, at:at + 8], factor, None, ALU.mult))

            def residual(src=None):
                for m in range(KT):
                    last = stt(out=x3[:, m, :], in0=acc(m) if src is None else src(m), scalar=coef[:, 8 + m:9 + m],
                               in1=x3[:, m, :], op0=ALU.mult, op1=ALU.add)
                last.then_inc(sem("x_ready"), 1)

            def ada_round(r, row, context=False, junk=sq):
                def dot(w, which, col, out_at, buf, done_sem):
                    nc.vector.tensor_tensor_reduce(buf[:, out_at * D:(out_at + 1) * D], w, c_rows[:, which * D:(which + 1) * D],
                                                   1.0, 0.0, ALU.mult, ALU.add, dots[:, col:col + 1]).then_inc(sem(done_sem), 1)

                dve.wait_ge(sem("ada_kept"), r)
                for j in range(NADA):
                    dve.wait_ge(sem(f"ada_landed{j}"), 16 * r + 16)
                    w = ada_slot(j)
                    if context:
                        dve.wait_ge(sem("ada_context"), 9 * (r - 18) + 2 * j)
                        for i in range(2):
                            dot(w[:, i, :], 2, 8 + 2 * j + i, i, ar(0, 2 * D), "ada_context")
                    dve.wait_ge(sem("ada_first"), 4 * r + j)
                    dot(w[:, 0, :], row, 2 * j, 0, junk, "ada_first")
                    dve.wait_ge(sem("ada_used"), 4 * r + j)
                    dot(w[:, 1, :], row, 2 * j + 1, 1, junk, "ada_used")
                dve.wait_ge(sem("ada_first"), 4 * r + 4)
                dve.wait_ge(sem("ada_used"), 4 * r + 4)
                cp(mods[:, bass.ds(8 * r, 8)], dots[:, 0:8]).then_inc(sem("ada_kept"), 1)
                if context:
                    dve.wait_ge(sem("ada_context"), 9 * (r - 18) + 8)
                    cp(cmods[:, bass.ds(8 * (r - 18), 8)], dots[:, 8:16]).then_inc(sem("ada_context"), 1)

            def hidden(t):
                for ft in range(2):
                    dve.wait_ge(sem("silu_ready"), 2 * t + ft + 1)
                    tt_(hid3[:, ft, :], sil3[:, ft, :], ps[:, ft, T:2 * T], ALU.mult).then_inc(sem("hid_ready"), 1)

            def ffn(n):
                for lo, hi, row, context in {0: [(0, NG, 0, False)], 1: [(0, 5, 0, False), (5, 7, 1, True), (7, NG, 1, False)]} \
                        .get(n, [(0, NG, None, False)]):
                    if context:
                        for t in range(NG * n + lo, NG * n + hi):
                            hidden(t)
                            ada_round(t + ADA_FIRST, row, True)
                        continue
                    with dve.Fori(lo, hi) as g:
                        t = g + NG * n
                        hidden(t)
                        if row is not None:
                            ada_round(t + ADA_FIRST, row)
                dve.wait_ge(sem("down_used"), NG * (n + 1) + 1)
                residual()

            def ada_bias(lo, hi, kept):
                dve.wait_ge(sem("ada_kept"), kept)
                done(tt_(mods[:, lo:hi], mods[:, lo:hi], v("ada_b", lo, hi - lo), ALU.add))

            def mixed(n):
                dve.wait_ge(sem("proj_slot"), 4 * n + 4)
                residual()

            def mla():
                dve.wait_ge(sem("mla_in"), 7)
                r2 = m_rope
                done(ts(r2[:, 0, :], ps[:, 3, 0:T], 1.0 / 384, EPS, ALU.mult, ALU.add))
                inverse_root(ts(r2[:, 1, :], ps[:, 3, T:2 * T], 1.0 / 256, EPS, ALU.mult, ALU.add), r2)
                for m in range(5):
                    g = v("q_norm", m) if m < 3 else v("kv_norm", m - 3)
                    last = stt(out=m_c[:, m, :], in0=m_c[:, m, :], scalar=g, in1=r2[:, 0 if m < 3 else 1, :],
                               op0=ALU.mult, op1=ALU.mult)
                last.then_inc(sem("mla_normed"), 1)
                dve.wait_ge(sem("mla_normed"), 1)
                rope = k("rope")
                done(tt_(m_k[64:96, 0, :], m_c[64:96, 5, :], rope[64:96, :], ALU.mult))
                done(tt_(m_rope[64:96, 0, :], m_c[96:128, 5, :], rope[96:128, :], ALU.mult))
                done(tt_(m_k[64:96, 0, :], m_k[64:96, 0, :], m_rope[64:96, 0, :], ALU.add))
                cp(m_k[64:96, 1:HEADS, :], bcm(m_k[64:96, 0, :], HEADS - 1)).then_inc(sem("mla_k_rope"), 1)
                for b in range(8):
                    dve.wait_ge(sem("mla_q"), b + 1)
                    q, src = m_q[:, 2 * b:2 * b + 2, :], ps[:, b, :].rearrange("p (h t) -> p h t", t=T)
                    done(tt_(q[64:96], src[64:96], bcm(rope[64:96, :], 2), ALU.mult))
                    done(tt_(m_rope[64:96], src[96:128], bcm(rope[96:128, :], 2), ALU.mult))
                    tt_(q[64:96], q[64:96], m_rope[64:96], ALU.add).then_inc(sem("mla_q_rope"), 1)
                    dve.wait_ge(sem("mla_q_rope"), b + 1)
                for i in range(4):
                    dve.wait_ge(sem("mla_kv"), 5 + i)
                    cp(m_v[:, i // 2, (i % 2) * 512:(i % 2 + 1) * 512], ps[:, 4 + i, :]).then_inc(sem("mla_v"), 1)
                for b in range(4):
                    s, st = 3 * (b % 2), m_st[:, 32 * (b % 2):32 * (b % 2) + 32]
                    s0, s1 = ps[:, s, :].rearrange("p (h t) -> p h t", t=P), two(ps[:, s + 1:s + 3, :])
                    dve.wait_ge(sem("mla_scores"), b + 1)
                    done(tt_(s0, s0, bcm(k("causal"), 4), ALU.add))
                    done(tt_(s1[:, :, P:T], s1[:, :, P:T], bcm(k("causal"), 4), ALU.add))
                    done(red(st[:, 0:4], s0, AXX, ALU.max))
                    done(red(st[:, 4:8], s1, AXX, ALU.max))
                    ts(st[:, 8:16], st[:, 0:8], -(QK ** -0.5), None, ALU.mult).then_inc(sem("mla_max"), 1)
                    dve.wait_ge(sem("mla_exp"), 8 * b + 8)
                    done(nc.vector.reciprocal(st[:, 24:32], st[:, 16:24]))
                    done(tt_(m_p0, m_p0, bc(st[:, 24:28], P), ALU.mult))
                    tt_(m_p1, m_p1, bc(st[:, 28:32], T), ALU.mult).then_inc(sem("mla_probs"), 1)
                    dve.wait_ge(sem("mla_turned"), b + 1)
                    cp(m_t1, s0).then_inc(sem("mla_t1"), 1)

            def eight(b):
                return ps[:, b:b + 2, :].rearrange("p b (k s) -> p (b k) s", s=P)

            def rwkv():
                dve.wait_ge(sem("h_ready"), 5)
                nc.vector.memset(sil3[:, 1, :], 0.0).then_inc(sem("zeros"), 1)
                done(tt_(r_x[:, :, 1:T], h3[:, :, 0:T - 1], h3[:, :, 1:T], ALU.subtract))
                done(ts(r_x[:, :, 0:1], h3[:, :, 0:1], -1.0, None, ALU.mult))
                for n, part in enumerate((3, 4, 5, 0, 1, 2)):
                    dst = r_b if n % 2 else r_g
                    if n in (2, 3):
                        dve.wait_ge(sem("rwkv_low1"), n - 1)
                    elif n == 4:
                        dve.wait_ge(sem("rwkv_low1"), 3)
                    elif n == 5:
                        dve.wait_ge(sem("rkv_slot"), 4)
                    for m in range(KT):
                        last = stt(out=dst[:, m, :], in0=r_x[:, m, :], scalar=v("mu", 8 * part + m), in1=h3[:, m, :],
                                   op0=ALU.mult, op1=ALU.add)
                    last.then_inc(sem("rwkv_mix"), 1)
                dve.wait_ge(sem("rwkv_sig"), 2)
                done(ts(r_w, r_w, -float(np.exp(-0.5)), None, ALU.mult))
                dve.wait_ge(sem("rwkv_rkv"), 2)
                for m in range(KT):
                    last = ts(r_g[:, m, :], r_a[:, m, :], -1.0, v("k_a", m), ALU.add, ALU.mult)
                done(last)
                done(stt(out=r_k, in0=r_g, scalar=1.0, in1=r_k, op0=ALU.add, op1=ALU.mult))
                dve.wait_ge(sem("rwkv_rkv"), 3)
                for m in range(KT):
                    last = stt(out=r_b[:, m, :], in0=r_r[:, m, :], scalar=v("r_k", m), in1=r_k[:, m, :],
                               op0=ALU.mult, op1=ALU.mult)
                last.then_inc(sem("rwkv_prod"), 1)
                for m in range(KT):
                    last = nc.vector.tensor_tensor_scan(r_g[:, m, :], k("keep"), r_w[:, m, :], 0.0, ALU.mult, ALU.add)
                last.then_inc(sem("rwkv_G"), 1)
                dve.wait_ge(sem("rwkv_G"), 1)
                tt_(r_w, r_g, r_w, ALU.subtract).then_inc(sem("rwkv_Gp"), 1)
                dve.wait_ge(sem("rwkv_sums"), 1)
                inverse_root(ts(sq3, two(ps[:, 0:4, :]), 1e-24, None, ALU.max), sq3)
                done(tt_(r_x, r_x, sq3, ALU.mult))
                dve.wait_ge(sem("rwkv_sums"), 2)
                done(tt_(r_b, two(ps[:, 4:8, :]), r_v, ALU.mult))
                done(tt_(r_a, r_a, r_x, ALU.mult))
                dve.wait_ge(sem("rwkv_E"), 3)
                done(tt_(r_r, r_r, r_e1, ALU.mult))
                done(tt_(r_a, r_a, r_e2, ALU.mult))
                done(tt_(r_k, r_k, r_e2, ALU.mult))
                done(stt(out=r_x, in0=r_x, scalar=-1.0, in1=r_e3, op0=ALU.mult, op1=ALU.mult))
                for blocks in (c_r, c_a, c_b, c_k, c_y):
                    done(nc.vector.memset(blocks, 0.0))
                nc.vector.memset(c_s, 0.0).then_inc(sem("rwkv_prep"), 1)
                dve.wait_ge(sem("rwkv_prep"), 1)
                for c in range(NCH):
                    cut = slice(c * CH, (c + 1) * CH)
                    if c >= 1:
                        dve.wait_ge(sem("rw_out"), c)
                    for dst, src in ((c_b, r_a), (c_a, r_x), (c_r, r_r)):
                        for o in (0, 64):
                            last = cp(dst[o:o + 64, :, o:o + 64], src[o:o + 64, :, cut])
                    last.then_inc(sem("rw_blocks"), 1)
                    dve.wait_ge(sem("rw_ab"), c + 1)
                    tt_(c_ab, eight(0), bcm(k("before"), KT), ALU.mult).then_inc(sem("rw_m"), 1)
                    dve.wait_ge(sem("rw_ak"), c + 1)
                    tt_(c_ak, eight(2), bcm(k("before"), KT), ALU.mult).then_inc(sem("rw_m"), 1)
                    for lev in range(6):
                        n = 6 * c + lev
                        dve.wait_ge(sem("rw_Z"), n + 1)
                        done(nc.vector.copy_predicated(c_t, bcm(k("low", lev * P, P).bitcast(U32), KT), eight(2)))
                        nc.vector.copy_predicated(c_tt, bcm(k("up", lev * P, P).bitcast(U32), KT), eight(5)) \
                            .then_inc(sem("rw_T"), 1)
                    dve.wait_ge(sem("rw_rb"), 2 * c + 1)
                    tt_(c_rb, eight(0), bcm(k("upto"), KT), ALU.mult).then_inc(sem("rw_m_rb"), 1)
                    dve.wait_ge(sem("rw_rb"), 2 * c + 2)
                    tt_(c_rk, eight(2), bcm(k("upto"), KT), ALU.mult).then_inc(sem("rw_m_rb"), 1)
                    dve.wait_ge(sem("rw_ds"), c + 1)
                    done(tt_(c_s, c_s, ps[:, 7, :].rearrange("p (k s) -> p k s", s=HD), ALU.add))
                    tt_(c_s, c_s, bc(r_dec[:, :, c], HD), ALU.mult).then_inc(sem("rw_S"), 1)
                    o3 = ps[:, 4, :].rearrange("p (k s) -> p k s", s=HD)
                    dve.wait_ge(sem("rw_o"), c + 1)
                    done(red(c_st[:, 0:8], o3, AXX, ALU.add))
                    done(ts(c_st[:, 0:8], c_st[:, 0:8], 1.0 / HD, None, ALU.mult))
                    done(tt_(c_rhs, o3, bc(c_st[:, 0:8], HD), ALU.subtract))
                    done(tt_(c_u, c_rhs, c_rhs, ALU.mult))
                    done(red(c_st[:, 8:16], c_u, AXX, ALU.add))
                    inverse_root(ts(c_st[:, 8:16], c_st[:, 8:16], 1.0 / HD, GN_EPS, ALU.mult, ALU.add), c_st[:, 8:16])
                    for o in (0, 64):
                        last = tt_(c_yb[o:o + 64, :, o:o + 64], c_rhs[o:o + 64], bc(c_st[o:o + 64, 8:16], HD), ALU.mult)
                    last.then_inc(sem("rw_yb"), 1)
                dve.wait_ge(sem("rw_y"), NCH)
                for m in range(KT):
                    last = ts(r_w[:, m, :], r_w[:, m, :], v("gn_w", m), v("gn_b", m), ALU.mult, ALU.add)
                done(last)
                done(tt_(r_w, r_w, r_b, ALU.add))
                tt_(r_w, r_w, r_o, ALU.mult).then_inc(sem("rwkv_y"), 1)

            def filters():
                lb0, lb1 = v("hg_lb", 0, 8), v("hg_lb", 8, 8)
                done(tt_(small[:, 160:168], lb0, lb1, ALU.max))
                done(tt_(small[:, 168:176], lb0, small[:, 160:168], ALU.subtract))
                tt_(small[:, 176:184], lb1, small[:, 160:168], ALU.subtract).then_inc(sem("hg_lb_in"), 1)
                dve.wait_ge(sem("hg_lb_exp"), 1)
                done(tt_(small[:, 184:192], small[:, 168:176], small[:, 176:184], ALU.add))
                done(nc.vector.reciprocal(small[:, 184:192], small[:, 184:192]))
                done(tt_(small[:, 192:200], small[:, 168:176], small[:, 184:192], ALU.mult))
                done(ts(small[:, 200:208], small[:, 192:200], -1.0, 1.0, ALU.mult, ALU.add))
                arg, turns = f_in[0:64, 0, T:2 * T], f_in[0:64, 1, 0:T]
                magic = 1.5 * 2.0 ** 23
                c1 = 6.28125
                c2 = float(np.floor((2 * np.pi - c1) * 2.0 ** 22) / 2.0 ** 22)
                c3 = 2 * np.pi - c1 - c2
                for n, (b, fr) in enumerate((("pos_b1", "freq1"), ("pos_b2", "freq2"))):
                    dve.wait_ge(sem("filter_mm"), n + 1)
                    done(ts(arg, ps[0:64, n, 0:T], v(b)[0:64], v(fr)[0:64], ALU.add, ALU.mult))
                    done(ts(turns, arg, 1.0 / (2 * np.pi), magic, ALU.mult, ALU.add))
                    done(ts(turns, turns, magic, None, ALU.subtract))
                    for part in (c1, c2, c3):
                        done(stt(out=arg, in0=turns, scalar=-part, in1=arg, op0=ALU.mult, op1=ALU.add))
                    ts(arg, arg, 3.1415925, -3.1415925, ALU.min, ALU.max).then_inc(sem("filter_arg"), 1)
                win = f_win[:, 0:TT * 2 * HYW].rearrange("p (t s c) -> p t s c", t=TT, c=HYW)
                for i in range(8):
                    dve.wait_ge(sem("filter_mm"), 3 + i)
                    tt_(f_h[:, i // 4, i % 4, :], ps[:, i, :], win[:, i // 4, i % 2, :], ALU.mult).then_inc(sem("filter_h"), 1)
                for o in range(2):
                    dve.wait_ge(sem("filter_l1"), o + 1)
                    done(ts(f_rn[:, o, :], ps[:, o, :], EPS, None, ALU.add))
                    done(nc.vector.reciprocal(f_rn[:, o, :], f_rn[:, o, :]))
                for o in range(2):
                    done(tt_(f_sum, f_h[:, :, 2 * o, :], f_h[:, :, 2 * o + 1, :], ALU.add))
                    tt_(f_dif, f_h[:, :, 2 * o, :], f_h[:, :, 2 * o + 1, :], ALU.subtract).then_inc(sem("filter_sides"), 1)
                    dve.wait_ge(sem("filter_freq"), o + 1)
                    rn, bias = f_rn[:, o, :], f_bias[:, o, :]
                    done(tt_(f_A[o], ps[:, 2:4, :], bcm(rn, 2), ALU.mult))
                    done(tt_(f_A[o], f_A[o], bcm(bias, 2), ALU.add))
                    done(tt_(f_D[o], ps[:, 6, :], rn, ALU.mult))
                    done(tt_(f_D[o], f_D[o], bias, ALU.add))
                    tt_(f_B[o], ps[:, 4:6, :], bcm(rn, 2), ALU.mult).then_inc(sem("filter_done"), 1)

            def gates(f_, k_):
                for d in range(2):
                    for h in range(HGH):
                        i = 4 * d + h
                        last = ts(f_[:, d, h, :], f_[:, d, h, :], small[:, 200 + i:201 + i], small[:, 192 + i:193 + i],
                                  ALU.mult, ALU.add)
                done(last)
                done(ts(k_, f_, -1.0, 1.0, ALU.mult, ALU.add))

            def hgrn():
                dve.wait_ge(sem("b2_evac"), len(B2_UNITS))
                done(nc.vector.memset(rstd[:, :], 0.0))
                gates(x_f, x_k)
                done(nc.vector.memset(x_E[:, 0, :, T - 1:T], 1.0))
                done(nc.vector.memset(x_E[:, 1, :, 0:1], 1.0))
                for h in range(HGH):
                    nc.vector.tensor_tensor_scan(x_E[:, 0, h, 0:T - 1][:, ::-1], x_f[:, 0, h, 1:T][:, ::-1], rstd[:, 0:T - 1],
                                                 1.0, ALU.mult, ALU.add)
                    last = nc.vector.tensor_tensor_scan(x_E[:, 1, h, 1:T], x_f[:, 1, h, 0:T - 1], rstd[:, 0:T - 1],
                                                        1.0, ALU.mult, ALU.add)
                done(last)
                tt_(x_k, x_k, x_E, ALU.mult).then_inc(sem("hg_gates"), 1)
                gates(g_f, g_k)
                ts(g_q, g_q, float(P) ** -0.5, None, ALU.mult).then_inc(sem("hg_gates"), 1)
                dve.wait_ge(sem("hg_gates"), 2)
                dve.wait_ge(sem("hg_state"), 2)
                cp(g_F, g_f)
                done(nc.vector.memset(g_E, 1.0))
                for lev in range(NLEV + 2):
                    hb = 1 << lev
                    if lev <= NLEV:
                        if lev >= 1:
                            dve.wait_ge(sem("hg_level"), lev + 1)
                        for d in range(2):
                            late, early = (1, 0) if d == 0 else (0, 1)

                            def cut(ap, side):
                                return ap.rearrange("p h (b s t) -> p (h b) s t", s=2, t=hb)[:, :, side, :]

                            tt_(cut(g_Q[:, d], late), cut(g_q, late), cut(g_F[:, d], late), ALU.mult)
                            last = tt_(cut(g_K[:, d], early), cut(g_k[:, d], early), cut(g_E[:, d], early), ALU.mult)
                        last.then_inc(sem("hg_scaled"), 1)
                        dve.wait_ge(sem("hg_scaled"), lev + 1)
                        for d in range(2):
                            late, early = (1, 0) if d == 0 else (0, 1)
                            end = hb - 1 if d == 0 else 0
                            edge_l = cut(g_F[:, d], late)[:, :, end:end + 1].to_broadcast([P, HGH * T // (2 * hb), hb])
                            edge_e = cut(g_F[:, d], early)[:, :, end:end + 1].to_broadcast([P, HGH * T // (2 * hb), hb])
                            done(tt_(cut(g_E[:, d], early), cut(g_E[:, d], early), edge_l, ALU.mult))
                            done(tt_(cut(g_F[:, d], late), cut(g_F[:, d], late), edge_e, ALU.mult))
                    else:
                        dve.wait_ge(sem("hg_cross"), 1)
                        for d in range(2):
                            last = tt_(g_Q[:, d], g_q, g_F[:, d], ALU.mult)
                        last.then_inc(sem("hg_scaled"), 1)
                    if lev <= NLEV:
                        dve.wait_ge(sem("hg_level"), lev + 1)
                        for d in range(2):
                            for tt in range(TT):
                                src = ps[:, 4 * (lev % 2) + 2 * d + tt, :].rearrange("p (h s) -> p h s", s=P)
                                if lev == 0:
                                    last = tt_(g_A[:, d, tt], src, bcm(ident, HGH), ALU.mult)
                                else:
                                    mask = k("up" if d == 0 else "low", (lev - 1) * P, P).bitcast(U32)
                                    last = nc.vector.copy_predicated(g_A[:, d, tt], bcm(mask, HGH), src)
                        last.then_inc(sem("hg_taken"), 1)
                dve.wait_ge(sem("hg_out"), 2)
                o, r = g_F[:, 0], g_F[:, 1]
                inverse_root(ts(r, two(ps[:, 4:6, :]), 1.0 / P, EPS, ALU.mult, ALU.add), r)
                done(stt(out=o, in0=o, scalar=v("hg_norm_g"), in1=r, op0=ALU.mult, op1=ALU.mult))
                tt_(mix3[:, 4:8, :], o, g_g, ALU.mult).then_inc(sem("hg_mixed"), 1)

            def hyena():
                rows = T // GRID
                for m in range(12):
                    dve.wait_ge(sem("hy_middle"), m + 1)
                    y = y_c[:, m, :].rearrange("p (r g) -> p r g", g=GRID)
                    p_ = hy_p[:, m, :].rearrange("p (r g) -> p r g", g=GRID)
                    done(stt(out=y[:, :, 1:GRID], in0=p_[:, :, 0:GRID - 1], scalar=v("conv_w", m), in1=y[:, :, 1:GRID],
                             op0=ALU.mult, op1=ALU.add))
                    last = stt(out=y[:, :, 0:GRID - 1], in0=p_[:, :, 1:GRID], scalar=v("conv_w", 24 + m),
                               in1=y[:, :, 0:GRID - 1], op0=ALU.mult, op1=ALU.add)
                last.then_inc(sem("hy_conv"), 1)
                for o in range(2):
                    dve.wait_ge(sem("hy_u"), o + 1)
                    tmp = sq[:, 1024:1536]
                    for ft in range(2):
                        uc, us = ps[:, ft, :], ps[:, 2 + ft, :]
                        A, B, Dd = f_A[o][:, ft, :], f_B[o][:, ft, :], (f_D[o] if ft == 0 else f_A[o][:, 1, :])
                        done(tt_(y_cc[:, ft, :], uc, A, ALU.mult))
                        done(tt_(tmp, us, B, ALU.mult))
                        done(tt_(y_cc[:, ft, :], y_cc[:, ft, :], tmp, ALU.subtract))
                        done(tt_(y_ss[:, ft, :], uc, B, ALU.mult))
                        done(tt_(tmp, us, Dd, ALU.mult))
                        last = tt_(y_ss[:, ft, :], y_ss[:, ft, :], tmp, ALU.add)
                    last.then_inc(sem("hy_y"), 1)
                    dve.wait_ge(sem("hy_v"), o + 1)
                    for tt in range(TT):
                        last = tt_((y_m if o else y_z)[:, tt, :], ps[:, 4 + tt, :], y_t[:, tt, HYW * (o + 1):HYW * (o + 2)], ALU.mult)
                    last.then_inc(sem("hy_z"), 1)
                dve.wait_ge(sem("hy_square"), 2)
                inverse_root(ts(small[:, 208:210], small[:, 208:210], 1.0 / HYW, EPS, ALU.mult, ALU.add), small[:, 208:210])
                tt_(y_m, y_m, bc(small[:, 208:210], HYW), ALU.mult).then_inc(sem("hy_normed"), 1)

            def routing():
                dve.wait_ge(sem("e_turned"), 2)
                lg = ps[:, 4, 0:TT * NE].rearrange("p (t e) -> p t e", t=TT)
                done(red(e_st[:, 0:2], lg, AXX, ALU.max))
                tt_(e_aff, lg, bc(e_st[:, 0:2], NE), ALU.subtract).then_inc(sem("e_aff"), 1)
                dve.wait_ge(sem("e_rows"), 2)
                done(red(e_st[:, 2:4], e_aff, AXX, ALU.add))
                done(nc.vector.reciprocal(e_st[:, 4:6], e_st[:, 2:4]))
                tt_(e_aff, e_aff, bc(e_st[:, 4:6], NE), ALU.mult).then_inc(sem("e_aff"), 1)
                dve.wait_ge(sem("e_aff"), 2)
                unit = e_s[:, 0:T]
                done(nc.vector.memset(unit, 1.0))
                for tt in range(TT):
                    done(tt_(e_diag[:, tt * NE:(tt + 1) * NE, :], bcm(ident, NE), bc(e_aff[:, tt, :], P), ALU.mult))
                dve.wait_ge(sem("early_landed"), 16)
                before = n_order[0]
                for e in range(NE):
                    dve.wait_ge(sem("e_spread"), 2 * (e // 2) + 2)
                    if e >= 2:
                        dve.wait_ge(sem("dve_order"), before + e - 1)
                    for tt in range(TT):
                        cmp = e_cmp[:, 4 * (e % 2) + 2 * tt:4 * (e % 2) + 2 * tt + 2, :]
                        stt(out=cmp[:, 0, :], in0=half(0, e), scalar=e_aff[:, tt, e:e + 1], in1=unit, op0=ALU.is_gt,
                            op1=ALU.mult, accum_out=e_rank[:, tt, e:e + 1])
                        last = stt(out=cmp[:, 1, :], in0=half(0, e), scalar=e_aff[:, tt, e:e + 1], in1=e_early[:, tt, :],
                                   op0=ALU.is_equal, op1=ALU.mult, accum_out=e_tie[:, tt, e:e + 1])
                    last.then_inc(sem("dve_order"), 1)
                n_order[0] += NE
                dve.wait_ge(sem("dve_order"), n_order[0])
                done(tt_(e_rank, e_rank, e_tie, ALU.add))
                for tt in range(TT):
                    done(tt_(e_sel[:, tt], bcm(k("iota"), NE), bc(e_rank[:, tt, :], CAP), ALU.is_equal))
                rep = ar(16880, 4096).rearrange("p (t e r c) -> p (t e) r c", t=TT, r=4, c=CAP)
                flat = e_sel.rearrange("p t e c -> p (t e) c")
                for r in range(4):
                    last = cp(rep[:, :, r, :], flat)
                last.then_inc(sem("e_select"), 1)
                dve.wait_ge(sem("e_gather"), KT)

            def experts():
                def tokens(at):
                    cp(e_xe, e_x[:, :, at]).then_inc(sem("moe_x"), 1)

                back = e_back.rearrange("p a b -> p (a b)")

                def gated(e):
                    dve.wait_ge(sem("moe_slot"), PER_EXPERT * e + 8)
                    cp(e_bk, back[:, bass.ds(T * e, T)])
                    dve.wait_ge(sem("moe_slot"), PER_EXPERT * e + 16)
                    dve.wait_ge(sem("moe_silu"), e + 1)
                    tt_(e_h2, e_s, ps[:, 1, :], ALU.mult).then_inc(sem("moe_h"), 1)

                tokens(slice(0, CAP))
                with dve.Fori(0, NE - 1) as e:
                    gated(e)
                    tokens(bass.ds(CAP * e + CAP, CAP))
                gated(NE - 1)

            def site(layer, s):
                return 72 * layer + 24 * s

            def modulated(i, layer, s, factor):
                at = site(layer, s)
                scale_of(at + 8, v("norm_g", 8 * (3 * layer + s), 8))
                norm(i, x3, h3, coef[:, 0:8], mods[:, at:at + 8])

            dve.wait_ge(sem("c_ready"), 1)
            for r in range(ADA_FIRST):
                ada_round(r, 0, junk=hT)
            ada_bias(0, 16, ADA_FIRST)
            modulated(0, 0, 0, 0.5)
            with dve.Fori(0, NG) as g:
                hidden(g)
                ada_round(g + ADA_FIRST, 0)
            ada_bias(16, 8 * (ADA_FIRST + NG), ADA_FIRST + NG)
            gate_of(site(0, 0) + 16, 0.5)
            dve.wait_ge(sem("down_used"), NG + 1)
            residual()
            modulated(1, 0, 1, 1.0)
            mla()
            gate_of(site(0, 1) + 16, 1.0)
            mixed(0)
            modulated(2, 0, 2, 0.5)
            gate_of(site(0, 2) + 16, 0.5)
            ffn(1)
            ada_bias(8 * (ADA_FIRST + NG), N_MODS, ADA_FIRST + 2 * NG)
            dve.wait_ge(sem("ada_context"), 18)
            done(tt_(cmods[:, :], cmods[:, :], v("ada_b", 144, 16), ALU.add))
            modulated(3, 1, 0, 0.5)
            gate_of(site(1, 0) + 16, 0.5)
            ffn(2)
            modulated(4, 1, 1, 1.0)
            rwkv()
            gate_of(site(1, 1) + 16, 1.0)
            mixed(1)
            modulated(5, 1, 2, 0.5)
            gate_of(site(1, 2) + 16, 0.5)
            ffn(3)
            filters()
            norm(6, x3, x3, v("final_g", 0, 8), name="x_ready")
            scale_of(144 + 8, v("norm1_g", 0, 8))
            norm(7, x3, h3, coef[:, 0:8], mods[:, 144:152])
            scale_of(8, v("norm1_g", 0, 8), src=cmods, to=16)
            norm(8, ctx3, hc3, coef[:, 16:24], cmods[:, 0:8])
            hgrn()
            hyena()
            gate_of(144 + 16, 1.0)
            mixed(2)
            scale_of(144 + 32, v("norm2_g", 0, 8))
            norm(9, x3, h3, coef[:, 0:8], mods[:, 144 + 24:144 + 32])
            routing()
            experts()
            gate_of(144 + 40, 1.0)
            dve.wait_ge(sem("moe_o"), NE)
            residual(lambda m: half(4, m))
            norm(10, x3, h3, v("final_g2", 0, 8))


INPUTS = ("con", "big", "win", "earlier", "vec", "xT", "ctxT", "c_rows", "ada", "ffn_gate", "ffn_up", "ffn_down",
          "ring_w", "w1", "w3", "w2", "pos_w", "hy_bias")


def kernel(**inputs):
    import concourse.bacc as bacc
    from concourse.bass_utils import run_bass_kernel_spmd

    laid = lay_out(inputs)
    nc = bacc.Bacc("TRN2", target_bir_lowering=False, num_devices=1)
    arrays, args = {}, {}
    for name in INPUTS:
        arrays[f"in_{name}"] = np.ascontiguousarray(laid[name])
        args[name] = nc.dram_tensor(f"in_{name}", arrays[f"in_{name}"].shape, F32, kind="ExternalInput").ap()
    out = nc.dram_tensor("out_0", (T, D), F32, kind="ExternalOutput").ap()
    build(nc, args, out)
    r = run_bass_kernel_spmd(nc, [arrays], core_ids=[0])
    return r.results[0]["out_0"].reshape(1, T, D)
```

```python
from contextlib import ExitStack

import numpy as np

import concourse.bass as bass
from concourse import mybir

P = 128
D = 1024
KT = D // P
T = 256
TT = T // P
FF = 2816
FG = 256
NG = FF // FG
NFFN = 4
SLOT = 2048
NRING = 4
NADA = 4
EPS = 1e-6

HEADS = 16
NOPE, ROPE = 64, 32
QK = NOPE + ROPE
HD = 64
CH = 64
NCH = T // CH
GN_EPS = 64e-5

HYW = 512
HGH = 4
GRID = 64
NE = 16
CAP = 2 * T // NE
EFF = 2048

SEQ_MLA = 0
SEQ_RWKV = 12
SEQ_B2 = 32
SEQ_MOE = 52
PER_EXPERT = 24

ADA_FIRST = 2
N_MODS = 72 + 72 + 48

F32 = mybir.dt.float32
BF16 = mybir.dt.bfloat16
U32 = mybir.dt.uint32
ALU = mybir.AluOpType
ACT = mybir.ActivationFunctionType
AXX = mybir.AxisListType.X


def layout(sizes):
    at, out = 0, {}
    for name, n in sizes:
        out[name] = (at, n)
        at += n
    return out, at


VEC, NVEC = layout([
    ("norm_g", 48), ("final_g", 8), ("ada_b", N_MODS), ("q_norm", 3), ("kv_norm", 2),
    ("mu", 48), ("w0", 8), ("a0", 8), ("k_k", 8), ("k_a", 8), ("r_k", 8), ("gn_w", 8), ("gn_b", 8),
    ("norm1_g", 8), ("conv_w", 36), ("conv_b", 12), ("pos_b1", 1), ("freq1", 1), ("pos_b2", 1),
    ("freq2", 1), ("hy_norm_g", 4), ("hg_lb", 16), ("hg_norm_g", 1), ("norm2_g", 8), ("final_g2", 8),
    ("rw", KT * NE),
])
NLEV = 7
CON, NCON = layout([
    ("ident", P), ("ones", P), ("blk", P), ("causal", P), ("before", HD), ("upto", HD),
    ("low", NLEV * P), ("up", NLEV * P), ("low64", 6 * HD), ("up64", 6 * HD), ("i64", HD), ("i32", CAP), ("iota", CAP), ("rope", T), ("keep", T),
])
BIG, NBIG = layout([
    ("cos", 2 * T), ("sin", 2 * T), ("sinq", 2 * T), ("cosq", 2 * P), ("inv", 4 * T),
])
WIN, NWIN = layout([("win", TT * 2 * HYW), ("zT", T)])


def shape_constants():
    con = np.zeros((P, NCON), np.float32)

    def put(name, a):
        o, n = CON[name]
        con[:, o:o + n] = np.asarray(a).reshape(P, n)

    i = np.arange(P)
    put("ident", np.eye(P))
    put("ones", np.ones((P, P)))
    same = (i[:, None] // HD) == (i[None, :] // HD)
    put("blk", same)
    put("causal", np.where(i[None, :] <= i[:, None], 0.0, -1e30))
    j = np.arange(HD)
    put("before", np.concatenate([j[:, None] < j[None, :]] * 2))
    put("upto", np.concatenate([j[:, None] <= j[None, :]] * 2))
    low = np.zeros((P, NLEV, P), np.float32)
    for lev in range(NLEV):
        h = 1 << lev
        low[:, lev, :] = ((i[:, None] // (2 * h)) == (i[None, :] // (2 * h))) \
            & ((i[:, None] // h) % 2 == 1) & ((i[None, :] // h) % 2 == 0)
    put("low", low)
    put("up", low.transpose(2, 1, 0))
    put("low64", np.concatenate([low[:HD, :6, :HD]] * 2))
    put("up64", np.concatenate([low.transpose(2, 1, 0)[:HD, :6, :HD]] * 2))
    put("i64", np.concatenate([np.eye(HD)] * 2))
    put("i32", np.concatenate([np.eye(CAP)] * 4))
    put("iota", np.broadcast_to(np.arange(CAP), (P, CAP)))
    inv = (np.float32(10000.0) ** (-np.arange(0, ROPE, 2, dtype=np.float32) / np.float32(ROPE))).astype(np.float32)
    ang = (np.arange(T, dtype=np.float32)[:, None] * inv[None, :]).astype(np.float64)
    rope = np.zeros((P, T))
    rope[64:96] = np.concatenate([np.cos(ang), np.cos(ang)], 1).T
    rope[96:128] = np.concatenate([-np.sin(ang), np.sin(ang)], 1).T
    put("rope", rope)
    put("keep", np.broadcast_to(np.arange(T) % CH != 0, (P, T)))

    big = np.zeros((P, NBIG), np.float32)

    def put_big(name, a):
        o, n = BIG[name]
        big[:, o:o + n] = np.asarray(a).reshape(P, n)

    t = np.arange(T)
    f = np.arange(T)
    turn = 2 * np.pi * ((t[:, None] * f[None, :]) % (2 * T)) / (2 * T)
    alt = 1.0 - 2.0 * (t % 2)
    cos, sin = np.cos(turn), np.sin(turn)
    sinq, cosq = sin.copy(), cos.copy()
    sinq[:, 0] = alt
    cosq[:, 0] = alt

    def by_tile(a):
        return a.reshape(TT, P, -1).transpose(1, 0, 2)

    put_big("cos", by_tile(cos))
    put_big("sin", by_tile(sin))
    put_big("sinq", by_tile(sinq))
    put_big("cosq", by_tile(cosq[:, :P]))
    ci, si = cos.T / T, sin.T / T
    ci[0] = 1.0 / (2 * T)
    si[0] = alt / (2 * T)
    put_big("inv", np.concatenate([ci, si]).reshape(4, P, T).transpose(1, 0, 2))

    pos = np.linspace(0.0, 1.0, T, dtype=np.float32)
    first, last = np.log(1e-2) / 1.5, np.log(1e-2) / 0.3
    deltas = np.abs(np.linspace(first, last, HYW, dtype=np.float32))
    window = np.exp(-pos[:, None].astype(np.float64) * deltas[None, :]) + 0.05
    both = np.stack([window, window], 1)
    both[0, 1, :] = 0.0
    omega = 2.0 * np.pi * t[:, None] / T
    band = np.linspace(1e-4, 15, 16, dtype=np.float32)[None, :].astype(np.float64)
    z = np.concatenate([pos[:, None], np.cos(band * omega), -np.sin(band * omega)], 1)
    win = np.zeros((P, NWIN), np.float32)
    o, n = WIN["win"]
    win[:, o:o + n] = both.reshape(TT, P, 2 * HYW).transpose(1, 0, 2).reshape(P, n)
    o, n = WIN["zT"]
    win[:33, o:o + n] = z.T
    lt = (np.arange(T)[None, :] < t[:, None]).astype(np.float32)
    lt = lt.reshape(TT, P, T).transpose(1, 0, 2).reshape(P, TT * T)
    return {"con": con, "big": big, "win": win, "earlier": lt}


def cols(a):
    a = np.asarray(a).reshape(-1)
    return a.reshape(-1, P).T


def k_major(w):
    k = w.shape[0] // P
    return w.reshape(k, P, -1).transpose(1, 0, 2).reshape(P, -1)


def slots(w):
    n = -(-w.shape[1] // SLOT)
    out = np.zeros((P, n * SLOT), np.float32)
    out[:, :w.shape[1]] = w
    return out.reshape(P, n, SLOT).transpose(1, 0, 2)


def lay_out(i):
    out = dict(shape_constants())
    vec = np.zeros((P, NVEC), np.float32)

    def put(name, a):
        o, n = VEC[name]
        a = np.asarray(a)
        vec[:a.shape[0], o:o + n] = a

    put("norm_g", cols(i["norm_g"]))
    put("final_g", cols(i["final_g"]))
    put("ada_b", np.concatenate([cols(i["ada_b"]), cols(i["ada_b_2"])], 1))
    put("q_norm", cols(i["mla_q_norm"]))
    put("kv_norm", cols(i["mla_kv_norm"]))
    put("mu", cols(i["rwkv_mu"]))
    for name, key in (("w0", "rwkv_w0"), ("a0", "rwkv_a0"), ("k_k", "rwkv_k_k"), ("k_a", "rwkv_k_a"),
                      ("r_k", "rwkv_r_k"), ("gn_w", "rwkv_gn_w"), ("gn_b", "rwkv_gn_b"),
                      ("norm1_g", "norm1_g_2"), ("conv_w", "hy_conv_w_2"), ("conv_b", "hy_conv_b_2"),
                      ("hy_norm_g", "hy_norm_g_2"), ("hg_lb", "hg_lb_2"), ("hg_norm_g", "hg_norm_g_2"),
                      ("norm2_g", "norm2_g_2"), ("final_g2", "final_g_2")):
        put(name, cols(i[key]))
    for name, key in (("pos_b1", "hy_pos_b1_2"), ("freq1", "hy_freq1_2"), ("pos_b2", "hy_pos_b2_2"),
                      ("freq2", "hy_freq2_2")):
        put(name, np.asarray(i[key]).reshape(-1, 1))
    put("rw", k_major(np.asarray(i["router_w_2"])[0]))
    out["vec"] = vec

    out["xT"] = k_major(np.asarray(i["x"])[0].T)
    out["ctxT"] = k_major(np.asarray(i["ctx_2"])[0].T)
    out["c_rows"] = np.broadcast_to(np.concatenate([np.asarray(i[k]).reshape(1, D) for k in ("c", "c_2", "c_ctx_2")], 1),
                                    (P, 3 * D))
    ada = np.concatenate([np.asarray(i["ada_w"])[0].T, np.asarray(i["ada_w"])[1].T, np.asarray(i["ada_w_2"])[0].T])
    out["ada"] = ada.reshape(-1, 2, P, D).transpose(0, 2, 1, 3).reshape(-1, P, 2 * D)

    w_in = np.asarray(i["ffn_w_in"]).reshape(NFFN, KT, P, 2, NG, FG).transpose(3, 0, 4, 2, 1, 5)
    out["ffn_gate"] = w_in[0].reshape(NFFN * NG, P, SLOT)
    out["ffn_up"] = w_in[1].reshape(NFFN * NG, P, SLOT)
    out["ffn_down"] = np.asarray(i["ffn_w_out"]).reshape(NFFN * NG, 2, P, D).transpose(0, 2, 1, 3).reshape(NFFN * NG, P, SLOT)

    w = np.asarray(i["mla_w_in"])[0]
    kr = w[:, 640:672]
    w = np.concatenate([w[:, :640], kr, kr, kr, kr[:, 16:], kr[:, :16]], 1)
    uq = np.asarray(i["mla_w_uq"])[0].reshape(384, HEADS, QK)
    uq = np.concatenate([uq, uq[:, :, 80:], uq[:, :, 64:80]], 2).reshape(384, HEADS * P)
    ukv = np.asarray(i["mla_w_ukv"])[0].reshape(256, HEADS, P)
    ukv = np.concatenate([ukv[:, :, :NOPE].reshape(256, D), ukv[:, :, NOPE:].reshape(256, D)], 1)
    mla = [slots(k_major(w)), slots(k_major(uq)), slots(k_major(ukv)), slots(k_major(np.asarray(i["mla_w_out"])[0]))]

    low = np.zeros((4, P, SLOT), np.float32)
    dw = np.concatenate([np.asarray(i["rwkv_wd1"])[0], np.asarray(i["rwkv_wa1"])[0]], 1)
    low[0, :, :D] = k_major(dw)
    low[0, :64, D:] = np.asarray(i["rwkv_wd2"])[0]
    low[1, :, :KT * 160] = k_major(np.asarray(i["rwkv_wg1"])[0])
    low[2, :64, :D] = np.asarray(i["rwkv_wa2"])[0]
    low[2, :, D:] = np.asarray(i["rwkv_wg2"])[0][:P]
    low[3, :32, :D] = np.asarray(i["rwkv_wg2"])[0][P:]
    rwkv = [low] + [slots(k_major(np.asarray(i["rwkv_w_rkv"])[0, n])) for n in range(3)] \
        + [slots(k_major(np.asarray(i["rwkv_w_out"])[0]))]

    w = np.asarray(i["w_in_2"])[0].reshape(KT, P, 16, 256).transpose(2, 1, 0, 3).reshape(16, P, SLOT)
    out["ring_w"] = np.concatenate(mla + rwkv + [w, slots(k_major(np.asarray(i["w_out_2"])[0]))])
    out["w1"] = np.asarray(i["exp_w1_2"])[0].reshape(NE * KT, P, EFF)
    out["w3"] = np.asarray(i["exp_w3_2"])[0].reshape(NE * KT, P, EFF)
    out["w2"] = np.asarray(i["exp_w2_2"])[0].reshape(NE * 8, 2, P, D)
    pos = np.zeros((P, P + HYW * 4), np.float32)
    pos[:33, :64] = np.asarray(i["hy_pos_w1_2"])[0]
    pos[:64, 64:128] = np.asarray(i["hy_pos_w2_2"])[0]
    pos[:64, 128:] = np.asarray(i["hy_pos_w3_2"])[0]
    out["pos_w"] = pos
    out["hy_bias"] = np.broadcast_to(np.asarray(i["hy_bias_2"]).reshape(1, 2 * HYW), (P, 2 * HYW))
    return out


def build(nc, a, out):
    with ExitStack() as ctx:
        def sb(name, n, dt=F32):
            return ctx.enter_context(nc.sbuf_tensor(name, [P, n], dt))

        sems = {}

        def sem(name):
            if name not in sems:
                sems[name] = ctx.enter_context(nc.semaphore(name))
            return sems[name]

        ring = sb("ring", NRING * SLOT)
        xT = sb("xT", KT * T)
        hT = sb("hT", KT * T)
        sq = sb("sq", KT * T)
        vec = sb("vec", NVEC)
        con = sb("con", NCON)
        mods = sb("mods", N_MODS)
        cmods = sb("cmods", 16)
        dots = sb("dots", 16)
        coef = sb("coef", 64)
        rstd = sb("rstd", T)
        sil = sb("sil", 2 * T)
        hid = sb("hid", 2 * T)
        small = sb("small", 256)
        zeros = sb("zeros", 512, BF16)
        ARENA = 32368
        arena = sb("arena", ARENA)
        FFN0 = ARENA - 3 * SLOT
        ADA0 = FFN0 - NADA * SLOT - 3 * D
        gate_w, up_w, down_w = (arena[:, FFN0 + i * SLOT:FFN0 + (i + 1) * SLOT] for i in range(3))
        c_rows = arena[:, FFN0 - 3 * D:FFN0]
        ps = ctx.enter_context(nc.psum_tensor("ps", [P, 8, 512], F32))

        def v(name, i=0, n=1):
            o, _ = VEC[name]
            return vec[:, o + i:o + i + n]

        def k(name, i=0, n=None):
            o, m = CON[name]
            return con[:, o + i:o + i + (m if n is None else n)]

        def ar(off, n):
            assert off + n <= ARENA, (off, n)
            return arena[:, off:off + n]

        def tiles(ap, b=T):
            return ap.rearrange("p (a b) -> p a b", b=b)

        x3, h3, sq3 = (tiles(t[:, :]) for t in (xT, hT, sq))
        gate3, up3 = tiles(gate_w[:, :], FG), tiles(up_w[:, :], FG)
        down3 = tiles(down_w[:, :], D)
        sil3, hid3 = tiles(sil[:, :]), tiles(hid[:, :])
        ident, ones, blk = k("ident"), k("ones"), k("blk")

        def slot(seq):
            s = seq % NRING
            return ring[:, s * SLOT:(s + 1) * SLOT]

        def ada_slot(j):
            return tiles(ar(ADA0 + j * SLOT, SLOT), D)

        def acc(m):
            return ps[:, 2 + m // 2, (m % 2) * T:(m % 2 + 1) * T]

        def half(bank, m):
            return ps[:, bank + m // 2, (m % 2) * T:(m % 2 + 1) * T]

        def norm_sums(i):
            return ps[:, 0 if i == 10 else 7, 0:T]

        def bc(ap, n):
            return ap.unsqueeze(2).to_broadcast([ap.shape[0], ap.shape[1], n])

        def bcm(ap, n):
            return ap.unsqueeze(1).to_broadcast([ap.shape[0], n, ap.shape[1]])

        m_c = tiles(ar(0, 6 * T))
        m_q = tiles(ar(1536, HEADS * T))
        m_k = tiles(ar(5632, HEADS * T))
        m_v = tiles(ar(9728, TT * D), D)
        m_p0 = tiles(ar(11776, 4 * P), P)
        m_p1 = tiles(ar(12288, 4 * T))
        m_t0 = tiles(ar(13312, 4 * T))
        m_t1 = tiles(ar(14336, 4 * P), P)
        m_rope = hid3
        m_st = small[:, 0:64]
        m_o = h3

        r_x = tiles(ar(0, 2048))
        r_g = tiles(ar(2048, 2048))
        r_b = tiles(ar(4096, 2048))
        r_r, r_k, r_v, r_a = (tiles(ar(6144 + 2048 * n, 2048)) for n in range(4))
        r_w = tiles(ar(14336, 2048))
        r_o = tiles(ar(16384, 2048))
        c_room = [ar(18432 + 512 * n, 512) for n in range(27)] \
            + [buf[:, 512 * n:512 * (n + 1)] for buf in (ar(2048, 2048), hT, sq) for n in range(4)] + [hid[:, :]]
        c_room = [tiles(buf, HD) for buf in c_room]
        c_ab, c_ak, c_rb, c_rk, c_vs, c_bt, c_kt, c_y, c_t, c_tt = (
            [c_room[(27 + 4 * n + c) % 40] for c in range(NCH)]
            for n in range(10))
        c_s = tiles(sil[:, :], HD)
        r_dec = small[:, 0:KT * NCH].rearrange("p (a b) -> p a b", b=NCH)
        r_e1, r_e2, r_e3 = (tiles(ar(18432 + 2048 * n, 2048)) for n in range(3))
        c_st = [small[:, 32 + 16 * c:48 + 16 * c] for c in range(NCH)]
        c_first = (("ab", r_a, r_x), ("m", r_x, r_a), ("vs", r_v, None), ("ak", r_k, r_x), ("bt", r_a, None), ("rb", r_a, r_r),
                   ("kt", r_k, None), ("rk", r_k, r_r))

        f_A = [tiles(ar(0 + 2560 * o, 1024), HYW) for o in range(2)]
        f_B = [tiles(ar(1024 + 2560 * o, 1024), HYW) for o in range(2)]
        f_D = [ar(2048 + 2560 * o, 512) for o in range(2)]
        big = ar(5120, NBIG)
        B0 = 5120 + NBIG
        hy_p = tiles(ar(B0, 3072))
        B1 = B0 + 3072
        f_win = ar(B1, NWIN)
        f_h = ar(B1 + NWIN, 4096).rearrange("p (t s c) -> p t s c", t=TT, c=HYW)
        f_pos = ar(B1 + NWIN + 4096, P + 2048)
        f_abs = ar(B1 + NWIN + 8320, 512)
        f_rn = tiles(ar(B1 + NWIN + 8832, 1024), HYW)
        f_sum = tiles(sq[:, 0:1024], HYW)
        f_dif = tiles(sq[:, 1024:2048], HYW)
        f_in = f_rn
        f_bias = tiles(ar(B1 + NWIN + 9856, 1024), HYW)

        def bigt(name, n):
            o, m = BIG[name]
            return big[:, o:o + m].rearrange("p (a b) -> p a b", b=n)

        g_q = tiles(ar(B1, 1024))
        g_g = tiles(ar(B1 + 1024, 1024))
        g_f = ar(B1 + 2048, 2048).rearrange("p (d h t) -> p d h t", d=2, t=T)
        g_k = ar(B1 + 4096, 2048).rearrange("p (d h t) -> p d h t", d=2, t=T)
        g_F = ar(B1 + 6144, 2048).rearrange("p (d h t) -> p d h t", d=2, t=T)
        g_E = ar(B1 + 8192, 2048).rearrange("p (d h t) -> p d h t", d=2, t=T)
        g_Q = ar(B1 + 10240, 2048).rearrange("p (d h t) -> p d h t", d=2, t=T)
        g_K = ar(B1 + 12288, 2048).rearrange("p (d h t) -> p d h t", d=2, t=T)
        g_v = tiles(ar(B1 + 14336, 1024), HYW)
        g_A = ar(B1 + 15360, 2048).rearrange("p (d t h s) -> p d t h s", d=2, t=TT, s=P)
        g_X = ar(B1 + 17408, 1024).rearrange("p (d h s) -> p d h s", d=2, s=P)
        g_S = sil[:, :].rearrange("p (h s) -> p h s", s=P), hid[:, :].rearrange("p (h s) -> p h s", s=P)
        x_f, x_k, x_E = g_F, g_E, g_Q
        x_kt = ar(B1 + 12288, 2048).rearrange("p (d t c) -> p d t c", d=2, t=TT)
        x_v = tiles(ar(B1 + 15360, 1024), HYW)
        ctx3 = tiles(ar(B1 + 6144, 2048))
        hc3 = tiles(ar(B1 + 17408, 2048))
        mix3 = h3

        y_c = tiles(ar(B1, 3072))
        y_t = ar(B1 + 3072, 3072).rearrange("p (t c) -> p t c", t=TT)
        y_cc = tiles(ar(B1 + 6144, 1024), HYW)
        y_ss = tiles(ar(B1 + 7168, 1024), HYW)
        y_z = tiles(ar(B1 + 8192, 1024), HYW)
        y_m = tiles(ar(B1 + 9216, 1024), HYW)

        e_h = tiles(ar(0, TT * D), D)
        e_aff = ar(2048, TT * NE).rearrange("p (t e) -> p t e", t=TT)
        e_rank = ar(2080, TT * NE).rearrange("p (t e) -> p t e", t=TT)
        e_tie = ar(2112, TT * NE).rearrange("p (t e) -> p t e", t=TT)
        e_row = ar(2144, T)
        e_st = ar(2400, 16)
        e_cmp = tiles(ar(8432, 8 * T))
        e_early = tiles(ar(2672, TT * T))
        e_sel = ar(3184, TT * NE * CAP).rearrange("p (t e c) -> p t e c", t=TT, c=CAP)
        e_rep = ar(4208, P)
        e_diag = tiles(ar(4336, TT * NE * P), P)
        e_back = tiles(ar(8432, NE * T))
        e_x = tiles(ar(12528, KT * NE * CAP), NE * CAP)
        e_xe = tiles(ar(16624, KT * CAP), CAP)
        e_s = ar(20976, 512)
        e_h2 = ar(21488, 512)
        e_hT = tiles(ar(22000, 512), P)
        e_y = ar(22512, 512)
        e_bk = ar(25088, T)
        o_row = tiles(ar(23024, TT * D), D)

        block = ctx.enter_context(nc.Block())

        def slot_done(seq):
            if seq < 3:
                return "mla_in", 6
            if seq < 6:
                return "mla_q", 8
            if seq < 8:
                return "mla_kv", 8
            if seq < SEQ_RWKV:
                return "proj_slot", seq - 8 + 1
            if seq < 16:
                return "rwkv_low2", 3
            if seq < 28:
                return "rkv_slot", seq - 16 + 1
            if seq < SEQ_B2:
                return "proj_slot", 4 + seq - 28 + 1
            if seq < 48:
                return "b2_unit", B2_LAST[seq - SEQ_B2] + 1
            return "proj_slot", 8 + seq - 48 + 1

        B2_UNITS = []
        for s in range(16):
            what = "hy" if s < 6 else ("q", "i", "zf", "zb", "g")[(s - 6) // 2]
            B2_UNITS.append((s, what, False))
            if what in ("i", "zf", "zb"):
                B2_UNITS.append((s, what, True))
        B2_LAST = [max(u for u, unit in enumerate(B2_UNITS) if unit[0] == s) for s in range(16)]

        @block.sync
        def _(sp):
            for dst, name in ((con, "con"), (vec, "vec"), (xT, "xT")):
                sp.dma_start(dst[:, :], a[name]).then_inc(sem("start_landed"), 16)
            sp.dma_start(c_rows, a["c_rows"]).then_inc(sem("start_landed"), 16)

            def ada_round(r, wait):
                for j in range(NADA):
                    if wait:
                        sp.wait_ge(sem("ada_used"), 4 * r - 3 + j)
                    sp.dma_start(ada_slot(j).rearrange("p a b -> p (a b)"), a["ada"][4 * r + j, :, :]) \
                        .then_inc(sem(f"ada_landed{j}"), 16)

            def ffn(n):
                with sp.Fori(0, NG) as g:
                    t = g + NG * n
                    sp.wait_ge(sem("gate_used"), t + 1)
                    sp.dma_start(gate_w[:, :], a["ffn_gate"][t, :, :]).then_inc(sem("gate_landed"), 16)
                    sp.wait_ge(sem("gate_up_ready"), 2 * t + 1)
                    sp.dma_start(up_w[:, :], a["ffn_up"][t, :, :]).then_inc(sem("up_landed"), 16)
                    sp.wait_ge(sem("down_used"), t + 1)
                    sp.dma_start(down_w[:, :], a["ffn_down"][t, :, :]).then_inc(sem("down_landed"), 16)
                    if n < 2:
                        ada_round(t + ADA_FIRST, True)

            def load(seq):
                if seq >= NRING:
                    name, n = slot_done(seq - NRING)
                    sp.wait_ge(sem(name), n)
                sp.dma_start(slot(seq), a["ring_w"][seq, :, :]).then_inc(sem(f"ring_landed{seq % NRING}"), 16)

            def expert_load(e, j):
                dst = slot(SEQ_MOE + j)
                if j < 8:
                    d = sp.dma_start(dst, a["w1"][8 * e + j, :, :])
                elif j < 16:
                    d = sp.dma_start(dst, a["w3"][8 * e + (j - 8), :, :])
                else:
                    d = sp.dma_start(tiles(dst, D), a["w2"][8 * e + (j - 16), :, :, :].rearrange("t p n -> p t n"))
                d.then_inc(sem(f"ring_landed{j % NRING}"), 16)

            for r in range(ADA_FIRST):
                ada_round(r, r > 0)
            ffn(0)
            for seq in range(SEQ_MLA, SEQ_RWKV):
                load(seq)
            ffn(1)
            ffn(2)
            for seq in range(SEQ_RWKV, SEQ_B2):
                load(seq)
            sp.wait_ge(sem("x_ready"), 5 * KT)
            for dst, name in ((big, "big"), (f_win, "win"), (f_pos, "pos_w"), (f_bias.rearrange("p a b -> p (a b)"), "hy_bias")):
                sp.dma_start(dst, a[name]).then_inc(sem("filter_landed"), 16)
            ffn(3)
            for seq in range(SEQ_B2, SEQ_B2 + NRING):
                load(seq)
            sp.wait_ge(sem("filter_done"), 2)
            sp.dma_start(ctx3.rearrange("p a b -> p (a b)"), a["ctxT"]).then_inc(sem("ctx_landed"), 16)
            for seq in range(SEQ_B2 + NRING, SEQ_MOE):
                load(seq)
            for j in range(NRING):
                sp.wait_ge(sem("proj_slot"), 8 + j + 1)
                expert_load(0, j)
            sp.wait_ge(sem("x_ready"), 8 * KT)
            sp.dma_start(e_early.rearrange("p a b -> p (a b)"), a["earlier"]).then_inc(sem("early_landed"), 16)
            with sp.Fori(0, NE - 1) as e:
                for j in range(NRING, PER_EXPERT):
                    sp.wait_ge(sem("moe_slot"), PER_EXPERT * e + (j - NRING + 1))
                    expert_load(e, j)
                for j in range(NRING):
                    sp.wait_ge(sem("moe_slot"), PER_EXPERT * e + (PER_EXPERT - NRING + j + 1))
                    expert_load(e + 1, j)
            for j in range(NRING, PER_EXPERT):
                sp.wait_ge(sem("moe_slot"), PER_EXPERT * (NE - 1) + j - NRING + 1)
                expert_load(NE - 1, j)
            sp.wait_ge(sem("row_ready"), 1)
            sp.dma_start(out.rearrange("(t p) n -> p t n", p=P), o_row).then_inc(sem("out_stored"), 16)
            sp.wait_ge(sem("out_stored"), 16)

        @block.tensor
        def _(pe):
            mm, tr = nc.tensor.matmul, nc.tensor.transpose

            def landed(seq):
                pe.wait_ge(sem(f"ring_landed{seq % NRING}"), 16 * (seq // NRING + 1))

            def norm(i):
                for kt in range(KT):
                    pe.wait_ge(sem("squares"), 4 * i + kt // 2 + 1)
                    last = mm(norm_sums(i), ones, sq3[:, kt, :], start=kt == 0, stop=kt == KT - 1)
                last.then_inc(sem("norm_sum"), 1)

            def h_part(i, kt):
                pe.wait_ge(sem("h_ready"), KT * (i - 1) + kt + 1)

            def open_banks(b0, signals=()):
                for b in range(4):
                    mm_ = mm(ps[:, b0 + b, :], zeros[:, 0:P], zeros[:, :], start=True, stop=False, skip_group_check=True)
                    if b < len(signals):
                        mm_.then_inc(sem(signals[b]), 1)

            def ffn(n, ready):
                if n > 0:
                    h_part(ready, 0)
                    open_banks(2)
                with pe.Fori(0, NG) as g:
                    t = g + NG * n
                    for ft in range(2):
                        if ft == 0:
                            pe.wait_ge(sem("gate_landed"), 16 * t + 16)
                        for kt in range(KT):
                            if ft == 0:
                                h_part(ready, kt)
                            last = mm(ps[:, ft, 0:T], gate3[:, kt, ft * P:(ft + 1) * P], h3[:, kt, :],
                                      start=kt == 0, stop=kt == KT - 1)
                        if ft == 1:
                            last.then_inc(sem("gate_used"), 1)
                        else:
                            pe.wait_ge(sem("up_landed"), 16 * t + 16)
                        for kt in range(KT):
                            last = mm(ps[:, ft, T:2 * T], up3[:, kt, ft * P:(ft + 1) * P], h3[:, kt, :],
                                      start=kt == 0, stop=kt == KT - 1)
                        last.then_inc(sem("gate_up_ready"), 1)
                    pe.wait_ge(sem("down_landed"), 16 * t + 16)
                    for ft in range(2):
                        pe.wait_ge(sem("hid_ready"), 2 * t + ft + 1)
                        for m in range(KT):
                            last = mm(acc(m), down3[:, ft, m * P:(m + 1) * P], hid3[:, ft, :],
                                      start=False, stop=True, skip_group_check=True)
                    last.then_inc(sem("down_used"), 1)

            def k_outer(out_of, seq0, rhs3, done):
                for kt in range(KT):
                    if kt % 2 == 0:
                        landed(seq0 + kt // 2)
                    for m in range(KT):
                        last = mm(out_of(m), slot(seq0 + kt // 2)[:, (kt % 2) * D + m * P:(kt % 2) * D + (m + 1) * P],
                                  rhs3[:, kt, :], start=(kt == 0 and m % 2 == 0), stop=kt == KT - 1,
                                  skip_group_check=True)
                    if kt % 2 == 1:
                        last.then_inc(sem(done), 1)

            def mla():
                for s in range(3):
                    landed(s)
                for m in range(6):
                    for kt in range(KT):
                        if m == 0:
                            h_part(2, kt)
                        last = mm(half(0, m), ring[:, kt * 768 + m * P:kt * 768 + (m + 1) * P], h3[:, kt, :],
                                  start=kt == 0, stop=kt == KT - 1)
                    last.then_inc(sem("mla_in"), 1)
                pe.wait_ge(sem("mla_c"), 4)
                for o, k0, k1 in ((0, 0, 3), (T, 3, 5)):
                    for kt in range(k0, k1):
                        last = mm(ps[:, 3, o:o + T], ones, sq3[:, kt, :], start=kt == k0, stop=kt == k1 - 1)
                last.then_inc(sem("mla_in"), 1)
                pe.wait_ge(sem("mla_normed"), 1)
                for s in range(3, 6):
                    landed(s)
                for h in range(HEADS):
                    for kt in range(3):
                        last = mm(half(0, h), slot(3 + kt)[:, h * P:(h + 1) * P], m_c[:, kt, :],
                                  start=kt == 0, stop=kt == 2)
                    if h % 2:
                        last.then_inc(sem("mla_q"), 1)
                for s in (6, 7):
                    landed(s)
                pe.wait_ge(sem("mla_q_nope"), 8)
                pe.wait_ge(sem("mla_q_rope"), 8)
                for i in range(8):
                    for kt in range(2):
                        last = mm(half(0, i), slot(6 + kt)[:, i * P:(i + 1) * P], m_c[:, 3 + kt, :],
                                  start=kt == 0, stop=kt == 1)
                    if i % 2:
                        last.then_inc(sem("mla_kv"), 1)
                for i in range(4):
                    tt, hb = i // 2, i % 2
                    for kt in range(2):
                        last = mm(ps[:, 4 + i, :], m_c[:, 3 + kt, tt * P:(tt + 1) * P],
                                  slot(6 + kt)[:, D + hb * 512:D + (hb + 1) * 512], start=kt == 0, stop=kt == 1)
                    last.then_inc(sem("mla_kv"), 1)

                def scores(b):
                    s = 3 * (b % 2)
                    if b == 0:
                        pe.wait_ge(sem("mla_k_nope"), 8)
                        pe.wait_ge(sem("mla_k_rope"), 1)
                        pe.wait_ge(sem("mla_v"), 4)
                    if b >= 2:
                        pe.wait_ge(sem("mla_o"), b - 1)
                    for hh in range(4):
                        h = 4 * b + hh
                        mm(ps[:, s, hh * P:(hh + 1) * P], m_q[0:QK, h, 0:P], m_k[0:QK, h, 0:P], start=True, stop=True)
                        last = mm(half(s + 1, hh), m_q[0:QK, h, P:T], m_k[0:QK, h, :], start=True, stop=True)
                    last.then_inc(sem("mla_scores"), 1)

                scores(0)
                for b in range(4):
                    s = 3 * (b % 2)
                    if b < 3:
                        scores(b + 1)
                    pe.wait_ge(sem("mla_probs"), b + 1)
                    if b >= 1:
                        pe.wait_ge(sem("mla_t0"), b)
                    for hh in range(4):
                        o = (hh % 2) * T
                        tr(ps[:, 6 + hh // 2, o:o + P], m_p0[:, hh, :], ident)
                        tr(ps[:, 6 + hh // 2, o + P:o + T], m_p1[:, hh, 0:P], ident)
                        last = tr(ps[:, s, hh * P:(hh + 1) * P], m_p1[:, hh, P:T], ident)
                    last.then_inc(sem("mla_turned"), 1)
                    pe.wait_ge(sem("mla_t0"), b + 1)
                    pe.wait_ge(sem("mla_t1"), b + 1)
                    for hh in range(4):
                        h, r, o = 4 * b + hh, 64 * (hh % 2), (hh // 2) * T
                        mm(ps[r:r + 64, s + 1, o:o + T], m_v[:, 0, h * 64:h * 64 + 64], m_t0[:, hh, :],
                           start=True, stop=False, skip_group_check=True)
                        last = mm(ps[r:r + 64, s + 1, o + P:o + T], m_v[:, 1, h * 64:h * 64 + 64], m_t1[:, hh, :],
                                  start=False, stop=True, skip_group_check=True)
                    last.then_inc(sem("mla_pv"), 1)
                pe.wait_ge(sem("mla_o"), 4)
                k_outer(acc, 8, m_o, "proj_slot")

            def heads(bank, lhs, rhs, start=True, stop=True):
                for kt in range(KT):
                    for r in (slice(0, 64), slice(64, 128)):
                        last = mm(ps[r, bank, kt * HD:(kt + 1) * HD], lhs[r, kt, :], rhs[r, :] if len(rhs.shape) == 2 else rhs[r, kt, :],
                                  start=start and (stop or kt == 0), stop=stop, skip_group_check=True)
                return last

            def rwkv():
                pe.wait_ge(sem("rwkv_mix"), 1)
                landed(12)
                for n, (buf, o) in enumerate(((r_g, 0), (r_b, 64))):
                    pe.wait_ge(sem("rwkv_mix"), n + 1)
                    for kt in range(KT):
                        last = mm(ps[0:64, 6 - n, 0:T], slot(12)[:, kt * P + o:kt * P + o + 64], buf[:, kt, :],
                                  start=kt == 0, stop=kt == KT - 1)
                    last.then_inc(sem("rwkv_low1"), 1)
                pe.wait_ge(sem("rwkv_mix"), 3)
                landed(13)
                for o, w in ((0, P), (P, 32)):
                    for kt in range(KT):
                        last = mm(ps[0:w, 7, 2 * o:2 * o + T], slot(13)[:, kt * 160 + o:kt * 160 + o + w], r_g[:, kt, :],
                                  start=kt == 0, stop=kt == KT - 1)
                last.then_inc(sem("rwkv_low1"), 1)
                pe.wait_ge(sem("rwkv_low"), 1)
                for m in range(KT):
                    last = mm(half(0, m), slot(12)[0:64, D + m * P:D + (m + 1) * P], hid3[0:64, 0, :], start=True, stop=True)
                last.then_inc(sem("rwkv_low2"), 1)
                landed(14)
                pe.wait_ge(sem("rwkv_low"), 2)
                pe.wait_ge(sem("rwkv_sig"), 1)
                for m in range(KT):
                    last = mm(half(0, m), slot(14)[0:64, m * P:(m + 1) * P], hid3[0:64, 1, :], start=True, stop=True)
                last.then_inc(sem("rwkv_low2"), 1)
                landed(15)
                pe.wait_ge(sem("rwkv_low"), 3)
                pe.wait_ge(sem("rwkv_sig"), 2)
                for m in range(KT):
                    mm(half(0, m), slot(14)[:, D + m * P:D + (m + 1) * P], sil3[:, 0, :], start=True, stop=False)
                    last = mm(half(0, m), slot(15)[:, m * P:(m + 1) * P], sil3[:, 1, :], start=False, stop=True)
                last.then_inc(sem("rwkv_low2"), 1)
                pe.wait_ge(sem("rwkv_mix"), 4)
                k_outer(lambda m: half(4, m), 16, r_b, "rkv_slot")
                pe.wait_ge(sem("rwkv_sig"), 3)
                pe.wait_ge(sem("rwkv_mix"), 5)
                k_outer(lambda m: half(0, m), 20, r_g, "rkv_slot")
                pe.wait_ge(sem("rwkv_rkv"), 1)
                pe.wait_ge(sem("rwkv_mix"), 6)
                k_outer(lambda m: half(4, m), 24, r_b, "rkv_slot")
                pe.wait_ge(sem("rwkv_kk2"), 1)
                for b in range(4):
                    last = mm(ps[:, b, :], blk, sq[:, b * 512:(b + 1) * 512], start=True, stop=True)
                last.then_inc(sem("rwkv_sums"), 1)
                pe.wait_ge(sem("rwkv_prod"), 1)
                for b in range(4):
                    last = mm(ps[:, 4 + b, :], blk, r_b[:, 2 * b:2 * b + 2, :].rearrange("p a b -> p (a b)"),
                              start=True, stop=True)
                last.then_inc(sem("rwkv_sums"), 1)
                pe.wait_ge(sem("rwkv_prep"), 1)
                for p, (name, left, right) in enumerate(c_first):
                    for c in range(NCH):
                        cut = slice(c * CH, (c + 1) * CH)
                        if p >= 2:
                            n = {2: 0, 3: 1, 5: 2, 7: 3}.get(p)
                            if n is None:
                                pe.wait_ge(sem("rw_first_a"), 4 * (0 if p == 4 else 1) + c + 1)
                            else:
                                pe.wait_ge(sem("rw_first_d"), 4 * n + c + 1)
                        heads((4 * p + c) % 8, left[:, :, cut], k("i64") if right is None else right[:, :, cut]) \
                            .then_inc(sem("rw_first"), 1)
                for lev in range(1, 6):
                    n = 4 * (lev - 1)
                    for c in range(NCH):
                        pe.wait_ge(sem("rw_T"), n + c + 1)
                        if lev == 1:
                            pe.wait_ge(sem("rw_first_a"), 9 + c)
                        heads(c, c_ab[c], c_t[c]).then_inc(sem("rw_Y"), 1)
                    for c in range(NCH):
                        pe.wait_ge(sem("rw_Ys"), n + c + 1)
                        if lev == 1:
                            pe.wait_ge(sem("rw_first_d"), 17 + c)
                        if lev < 5:
                            heads(c, c_tt[c], c_y[c])
                        heads(4 + c, c_y[c], c_tt[c]).then_inc(sem("rw_Z"), 1)
                pe.wait_ge(sem("rw_T"), 6 * NCH)
                for c in range(NCH + 1):
                    cut = slice(c * CH, (c + 1) * CH)
                    if c < NCH:
                        o = 2 + c % 2
                        heads(0, c_ak[c], c_vs[c], stop=c == 0)
                        if c >= 2:
                            pe.wait_ge(sem("rw_yb"), c - 1)
                        last = heads(o, c_rk[c], c_vs[c], stop=False)
                        if c > 0:
                            pe.wait_ge(sem("rw_S"), c)
                            last = heads(0, r_x[:, :, cut], c_s, start=False)
                        last.then_inc(sem("rw_rhs"), 1)
                        if c < NCH - 1:
                            heads(4, c_kt[c], c_vs[c], stop=False)
                        if c > 0:
                            heads(o, r_r[:, :, cut], c_s, start=False, stop=False)
                        pe.wait_ge(sem("rw_rhs_s"), c + 1)
                        heads(1, c_tt[c], c_y[c]).then_inc(sem("rw_u"), 1)
                        pe.wait_ge(sem("rw_u_s"), c + 1)
                        if c < NCH - 1:
                            heads(4, c_bt[c], c_t[c], start=False).then_inc(sem("rw_ds"), 1)
                        heads(o, c_rb[c], c_t[c], start=False).then_inc(sem("rw_o"), 1)
                    if c > 0:
                        pe.wait_ge(sem("rw_yb"), c)
                        if c >= 3:
                            pe.wait_ge(sem("rw_y"), c - 2)
                        heads(5 + (c - 1) % 2, c_ab[c - 1], k("i64")).then_inc(sem("rw_out"), 1)
                pe.wait_ge(sem("rwkv_y"), 1)
                k_outer(acc, 28, r_w, "proj_slot")

            def filters():
                pe.wait_ge(sem("filter_landed"), 64)
                pe.wait_ge(sem("x_ready"), 6 * KT)
                zT = f_win[0:33, WIN["zT"][0]:WIN["zT"][0] + T]
                mm(ps[0:64, 0, 0:T], f_pos[0:33, 0:64], zT, start=True, stop=True).then_inc(sem("filter_mm"), 1)
                pe.wait_ge(sem("filter_sin"), 1)
                mm(ps[0:64, 1, 0:T], f_pos[0:64, 64:128], f_in[0:64, 0, 0:T], start=True, stop=True) \
                    .then_inc(sem("filter_mm"), 1)
                pe.wait_ge(sem("filter_sin"), 2)
                for tt in range(TT):
                    for q in range(4):
                        mm(ps[:, 4 * tt + q, :], f_in[0:64, 0, tt * P:(tt + 1) * P],
                           f_pos[0:64, P + q * HYW:P + (q + 1) * HYW], start=True, stop=True).then_inc(sem("filter_mm"), 1)
                for o in range(2):
                    pe.wait_ge(sem("filter_abs"), o + 1)
                    for n in range(4):
                        last = mm(ps[:, o, :], ones, sq[:, n * HYW:(n + 1) * HYW], start=n == 0, stop=n == 3)
                    last.then_inc(sem("filter_l1"), 1)
                cos, sin, cosq = bigt("cos", T), bigt("sin", T), bigt("cosq", P)
                for o in range(2):
                    pe.wait_ge(sem("filter_sides"), o + 1)
                    if o == 1:
                        pe.wait_ge(sem("filter_done"), 1)
                    for ft in range(2):
                        for tt in range(TT):
                            mm(ps[:, 2 + ft, :], cos[:, tt, ft * P:(ft + 1) * P], f_sum[:, tt, :], start=tt == 0, stop=tt == 1)
                        for tt in range(TT):
                            mm(ps[:, 4 + ft, :], sin[:, tt, ft * P:(ft + 1) * P], f_dif[:, tt, :], start=tt == 0, stop=tt == 1)
                    for tt in range(TT):
                        last = mm(ps[:, 6, :], cosq[:, tt, :], f_sum[:, tt, :], start=tt == 0, stop=tt == 1)
                    last.then_inc(sem("filter_freq"), 1)

            def b2_in():
                h_part(7, KT - 1)
                for u, (s, what, context) in enumerate(B2_UNITS):
                    if context:
                        h_part(8, KT - 1)
                    src = hc3 if context else h3
                    landed(SEQ_B2 + s)
                    if u >= 7:
                        pe.wait_ge(sem("b2_evac"), u - 6)
                    w = tiles(slot(SEQ_B2 + s), 256)
                    for j in range(2):
                        o = ps[:, u % 7, j * T:(j + 1) * T]
                        for kt in range(KT):
                            if what == "i":
                                last = mm(o, src[:, kt, j * P:(j + 1) * P], w[:, kt, :], start=kt == 0, stop=kt == KT - 1)
                            else:
                                last = mm(o, w[:, kt, j * P:(j + 1) * P], src[:, kt, :], start=kt == 0, stop=kt == KT - 1)
                    last.then_inc(sem("b2_unit"), 1)

            def hgrn():
                pe.wait_ge(sem("hg_gates"), 1)
                pe.wait_ge(sem("b2_evac"), len(B2_UNITS))
                for d in range(2):
                    for tt in range(TT):
                        for h in range(HGH):
                            last = tr(ps[:, 2 * d + tt, h * P:(h + 1) * P], x_k[:, d, h, tt * P:(tt + 1) * P], ident)
                        last.then_inc(sem("hg_ctx_t"), 1)
                pe.wait_ge(sem("hg_ctx_kt"), 4)
                for d in range(2):
                    for h in range(HGH):
                        for tt in range(TT):
                            last = mm(ps[:, 4 + d, h * P:(h + 1) * P], x_kt[:, d, tt, h * P:(h + 1) * P],
                                      x_v[:, tt, h * P:(h + 1) * P], start=tt == 0, stop=tt == 1)
                    last.then_inc(sem("hg_state"), 1)

                def level(n, kk, qq):
                    for d in range(2):
                        for tt in range(TT):
                            for h in range(HGH):
                                last = mm(ps[:, 4 * (n % 2) + 2 * d + tt, h * P:(h + 1) * P],
                                          kk(d)[:, h, tt * P:(tt + 1) * P], qq(d)[:, h, tt * P:(tt + 1) * P],
                                          start=True, stop=True)
                    last.then_inc(sem("hg_level"), 1)

                pe.wait_ge(sem("hg_gates"), 2)
                level(0, lambda d: g_k[:, d], lambda d: g_q)
                pe.wait_ge(sem("hg_state_s"), 2)
                for lev in range(NLEV):
                    pe.wait_ge(sem("hg_scaled"), lev + 1)
                    if lev >= 1:
                        pe.wait_ge(sem("hg_taken"), lev)
                    level(lev + 1, lambda d: g_K[:, d], lambda d: g_Q[:, d])
                pe.wait_ge(sem("hg_scaled"), NLEV + 1)
                pe.wait_ge(sem("hg_taken"), NLEV)
                for d in range(2):
                    for h in range(HGH):
                        last = mm(ps[:, d, h * P:(h + 1) * P], g_K[:, d, h, d * P:(d + 1) * P],
                                  g_Q[:, d, h, (1 - d) * P:(2 - d) * P], start=True, stop=True)
                last.then_inc(sem("hg_cross"), 1)
                pe.wait_ge(sem("hg_cross_s"), 1)
                pe.wait_ge(sem("hg_taken"), NLEV + 1)
                pe.wait_ge(sem("hg_scaled"), NLEV + 2)
                for h in range(HGH):
                    o, e0 = half(2, h), slice(h * P, (h + 1) * P)
                    mm(o, g_S[0][:, h, :], g_Q[:, 0, h, :], start=True, stop=False, skip_group_check=True)
                    mm(o, g_S[1][:, h, :], g_Q[:, 1, h, :], start=False, stop=False, skip_group_check=True)
                    for d in range(2):
                        for tt in range(TT):
                            mm(o[:, tt * P:(tt + 1) * P], g_v[:, tt, e0], g_A[:, d, tt, h, :],
                               start=False, stop=False, skip_group_check=True)
                        last = mm(o[:, (1 - d) * P:(2 - d) * P], g_v[:, d, e0], g_X[:, d, h, :],
                                  start=False, stop=d == 1, skip_group_check=True)
                last.then_inc(sem("hg_out"), 1)
                pe.wait_ge(sem("hg_os"), 2)
                for b in range(2):
                    last = mm(ps[:, 4 + b, :], ones, sq[:, b * 512:(b + 1) * 512], start=True, stop=True)
                last.then_inc(sem("hg_out"), 1)

            def hyena():
                pe.wait_ge(sem("hy_conv"), 1)
                for tt in range(TT):
                    for w in range(3):
                        for j in range(4):
                            last = tr(ps[:, 3 * tt + w, j * P:(j + 1) * P], y_c[:, 4 * w + j, tt * P:(tt + 1) * P], ident)
                        last.then_inc(sem("hy_turned"), 1)
                cos, sinq, inv = bigt("cos", T), bigt("sinq", T), bigt("inv", T)
                for o in range(2):
                    if o == 0:
                        pe.wait_ge(sem("hy_rows"), 6)
                    else:
                        pe.wait_ge(sem("hy_z"), 1)
                    for ft in range(2):
                        for b, table in ((0, cos), (2, sinq)):
                            for tt in range(TT):
                                u = y_t[:, tt, 0:HYW] if o == 0 else y_z[:, tt, :]
                                last = mm(ps[:, b + ft, :], table[:, tt, ft * P:(ft + 1) * P], u, start=tt == 0, stop=tt == 1)
                    last.then_inc(sem("hy_u"), 1)
                    pe.wait_ge(sem("hy_y"), o + 1)
                    for tt in range(TT):
                        for f in range(4):
                            y = y_cc[:, f, :] if f < 2 else y_ss[:, f - 2, :]
                            last = mm(ps[:, 4 + tt, :], inv[:, f, tt * P:(tt + 1) * P], y, start=f == 0, stop=f == 3)
                    last.then_inc(sem("hy_v"), 1)
                pe.wait_ge(sem("hy_normed"), 1)
                for m in range(4):
                    for tt in range(TT):
                        last = tr(ps[:, m, tt * P:(tt + 1) * P],
                                  y_m[:, tt, m * P:(m + 1) * P], ident)
                    last.then_inc(sem("hy_back"), 1)
                pe.wait_ge(sem("hy_mixed"), 4)
                pe.wait_ge(sem("hg_mixed"), 1)
                k_outer(acc, 48, mix3, "proj_slot")

            def routing():
                for tt in range(TT):
                    for kt in range(KT):
                        h_part(9, kt)
                        last = tr(ps[:, 2 * tt + kt // 4, (kt % 4) * P:(kt % 4 + 1) * P], h3[:, kt, tt * P:(tt + 1) * P], ident)
                last.then_inc(sem("e_turned"), 1)
                for tt in range(TT):
                    for kt in range(KT):
                        last = mm(ps[:, 4, tt * NE:(tt + 1) * NE], h3[:, kt, tt * P:(tt + 1) * P], v("rw", kt * NE, NE),
                                  start=kt == 0, stop=kt == KT - 1)
                last.then_inc(sem("e_turned"), 1)
                pe.wait_ge(sem("e_aff"), 2)
                for tt in range(TT):
                    last = tr(ps[0:NE, 5, tt * P:(tt + 1) * P], e_aff[:, tt, :], ident)
                last.then_inc(sem("e_aff_t"), 1)
                pe.wait_ge(sem("e_rows"), 3)
                for e in range(NE):
                    mm(half(0, e), ident[0:NE, e:e + 1].to_broadcast([NE, P]), e_row[0:NE, :], start=True, stop=True) \
                        .then_inc(sem("e_spread"), 1)
                pe.wait_ge(sem("e_select"), 1)
                rep = ar(16880, 4096).rearrange("p (t e c) -> p t e c", t=TT, c=P)
                for e in range(NE):
                    for tt in range(TT):
                        last = mm(half(0, e)[:, tt * P:(tt + 1) * P], rep[:, tt, e, :], e_diag[:, tt * NE + e, :],
                                  start=True, stop=True)
                    if e % 2:
                        last.then_inc(sem("e_backs"), 1)
                for kt in range(KT):
                    pe.wait_ge(sem("e_back"), kt + 1)
                    for tt in range(TT):
                        last = mm(ps[:, kt, :], e_h[:, tt, kt * P:(kt + 1) * P],
                                  e_sel[:, tt, :, :].rearrange("p e c -> p (e c)"), start=tt == 0, stop=tt == 1)
                    last.then_inc(sem("e_gathers"), 1)
                pe.wait_ge(sem("e_gather"), KT)

            def experts():
                open_banks(4)
                with pe.Fori(0, NE) as e:
                    def weights(j):
                        pe.wait_ge(sem(f"ring_landed{j % NRING}"), 16 * (PER_EXPERT // NRING) * e
                                   + 16 * ((SEQ_MOE + j) // NRING + 1))
                        return slot(SEQ_MOE + j)

                    pe.wait_ge(sem("moe_x"), e + 1)
                    for part in range(2):
                        for kt in range(KT):
                            w = weights(8 * part + kt)
                            for n in range(4):
                                last = mm(ps[32 * n:32 * n + 32, part, :], e_xe[:, kt, :], w[:, n * 512:(n + 1) * 512],
                                          start=kt == 0, stop=kt == KT - 1, skip_group_check=True)
                            last.then_inc(sem("moe_slot"), 1)
                    pe.wait_ge(sem("moe_h"), e + 1)
                    for i in range(4):
                        last = tr(ps[:, 2, i * P:(i + 1) * P], e_h2[:, i * P:(i + 1) * P], ident)
                    last.then_inc(sem("moe_turned"), 1)
                    pe.wait_ge(sem("moe_hT"), e + 1)
                    for j in range(8):
                        w = weights(16 + j)
                        for t2 in range(2):
                            n, i = (2 * j + t2) // 4, (2 * j + t2) % 4
                            for nn in range(2):
                                q = 64 * nn + 32 * t2
                                last = mm(ps[q:q + 32, 3, :], e_hT[:, i, 32 * n:32 * n + 32],
                                          w[:, t2 * D + nn * 512:t2 * D + (nn + 1) * 512],
                                          start=j == 0, stop=j == 7, skip_group_check=True)
                        last.then_inc(sem("moe_slot"), 1)
                    pe.wait_ge(sem("moe_y"), e + 1)
                    for i in range(4):
                        for nn in range(2):
                            r = slice(64 * nn, 64 * nn + 64)
                            last = mm(half(4, 4 * nn + i), e_y[r, i * P:(i + 1) * P], e_bk[r, :],
                                      start=False, stop=True, skip_group_check=True)
                    last.then_inc(sem("moe_o"), 1)

            pe.wait_ge(sem("zeros"), 1)
            open_banks(2, ("gate_used", "gate_up_ready", "down_used"))
            pe.wait_ge(sem("start_landed"), 64)
            norm(0)
            ffn(0, 1)
            norm(1)
            mla()
            norm(2)
            ffn(1, 3)
            norm(3)
            ffn(2, 4)
            norm(4)
            rwkv()
            norm(5)
            ffn(3, 6)
            filters()
            norm(6)
            norm(7)
            norm(8)
            b2_in()
            hgrn()
            hyena()
            norm(9)
            routing()
            experts()
            norm(10)
            for tt in range(TT):
                for kt in range(KT):
                    h_part(10, kt)
                    last = tr(ps[:, 2 * tt + kt // 4, (kt % 4) * P:(kt % 4 + 1) * P], h3[:, kt, tt * P:(tt + 1) * P], ident)
            last.then_inc(sem("row_turned"), 1)

        @block.scalar
        def _(act):
            f = nc.scalar.activation

            def copy(dst, src):
                return f(dst, src, ACT.Copy)

            def two(ap):
                return ap.rearrange("p b (h t) -> p (b h) t", t=T)

            n_root = [0]

            def root(buf):
                n_root[0] += 1
                act.wait_ge(sem("root_in"), n_root[0])
                f(buf, buf, ACT.Sqrt).then_inc(sem("root_out"), 1)

            n_shift = [0]

            def norm(i, ready, src=x3, dst=h3, shift=None):
                if i >= 1:
                    act.wait_ge(sem("norm_sum"), i)
                for b in range(4):
                    if ready is not None:
                        act.wait_ge(sem("x_ready"), KT * (ready - 1) + 2 * b + 2)
                    f(sq3[:, 2 * b:2 * b + 2, :], src[:, 2 * b:2 * b + 2, :], ACT.Square).then_inc(sem("squares"), 1)
                root(rstd[:, :])
                if shift is not None:
                    for m in range(KT):
                        act.wait_ge(sem("h_scaled"), KT * n_shift[0] + m + 1)
                        f(dst[:, m, :], dst[:, m, :], ACT.Identity, bias=shift[:, m:m + 1]).then_inc(sem("h_ready"), 1)
                    n_shift[0] += 1

            def modulated(i, ready, layer, s):
                at = 72 * layer + 24 * s
                norm(i, ready, shift=mods[:, at:at + 8])

            def ffn(n):
                with act.Fori(0, NG) as g:
                    t = g + NG * n
                    for ft in range(2):
                        act.wait_ge(sem("gate_up_ready"), 2 * t + ft + 2)
                        f(sil3[:, ft, :], ps[:, ft, 0:T], ACT.Silu).then_inc(sem("silu_ready"), 1)

            def mla():
                for b in range(3):
                    act.wait_ge(sem("mla_in"), 2 * b + 2)
                    copy(m_c[:, 2 * b:2 * b + 2, :], ps[:, b, :].rearrange("p (h t) -> p h t", t=T)).then_inc(sem("mla_c"), 1)
                act.wait_ge(sem("mla_c"), 3)
                act.wait_ge(sem("norm_sum"), 2)
                f(sq3[:, 0:5, :], m_c[:, 0:5, :], ACT.Square).then_inc(sem("mla_c"), 1)
                root(m_rope)
                for b in range(8):
                    act.wait_ge(sem("mla_q"), b + 1)
                    copy(m_q[0:64, 2 * b:2 * b + 2, :], ps[0:64, b, :].rearrange("p (h t) -> p h t", t=T)) \
                        .then_inc(sem("mla_q_nope"), 1)
                for b in range(4):
                    act.wait_ge(sem("mla_kv"), b + 1)
                    for o in range(2):
                        copy(m_k[0:64, 4 * b + o:4 * b + o + 3:2, :],
                             ps[64 * o:64 * o + 64, b, :].rearrange("p (h t) -> p h t", t=T)).then_inc(sem("mla_k_nope"), 1)
                for b in range(4):
                    s, st = 3 * (b % 2), m_st[:, 32 * (b % 2):32 * (b % 2) + 32]
                    act.wait_ge(sem("mla_max"), b + 1)
                    if b >= 1:
                        act.wait_ge(sem("mla_turned"), b)
                    for hh in range(4):
                        f(m_p0[:, hh, :], ps[:, s, hh * P:(hh + 1) * P], ACT.Exp, bias=st[:, 8 + hh:9 + hh],
                          scale=QK ** -0.5, accum_out=st[:, 16 + hh:17 + hh]).then_inc(sem("mla_exp"), 1)
                        f(m_p1[:, hh, :], half(s + 1, hh), ACT.Exp, bias=st[:, 12 + hh:13 + hh],
                          scale=QK ** -0.5, accum_out=st[:, 20 + hh:21 + hh]).then_inc(sem("mla_exp"), 1)
                    act.wait_ge(sem("mla_turned"), b + 1)
                    copy(m_t0, two(ps[:, 6:8, :])).then_inc(sem("mla_t0"), 1)
                    act.wait_ge(sem("mla_pv"), b + 1)
                    copy(m_o[:, 2 * b:2 * b + 2, :], ps[:, s + 1, :].rearrange("p (h t) -> p h t", t=T)) \
                        .then_inc(sem("mla_o"), 1)

            def heads(bank):
                return tiles(ps[:, bank, :], HD)

            def rwkv():
                act.wait_ge(sem("rwkv_low1"), 1)
                f(hid3[0:64, 0, :], ps[0:64, 6, 0:T], ACT.Tanh).then_inc(sem("rwkv_low"), 1)
                act.wait_ge(sem("rwkv_low1"), 2)
                copy(hid3[0:64, 1, :], ps[0:64, 5, 0:T]).then_inc(sem("rwkv_low"), 1)
                act.wait_ge(sem("rwkv_low1"), 3)
                act.wait_ge(sem("zeros"), 2)
                f(sil3[0:32, 1, :], ps[0:32, 7, T:2 * T], ACT.Sigmoid)
                f(sil3[:, 0, :], ps[:, 7, 0:T], ACT.Sigmoid).then_inc(sem("rwkv_low"), 1)
                for n, (dst, bias) in enumerate(((r_w, "w0"), (r_a, "a0"))):
                    act.wait_ge(sem("rwkv_low2"), n + 1)
                    for m in range(KT):
                        last = f(dst[:, m, :], half(0, m), ACT.Sigmoid, bias=v(bias, m))
                    last.then_inc(sem("rwkv_sig"), 1)
                act.wait_ge(sem("rwkv_low2"), 3)
                copy(r_o, two(ps[:, 0:4, :])).then_inc(sem("rwkv_sig"), 1)
                act.wait_ge(sem("rkv_slot"), 4)
                copy(r_r, two(ps[:, 4:8, :])).then_inc(sem("rwkv_rkv"), 1)
                act.wait_ge(sem("rkv_slot"), 8)
                copy(r_k, two(ps[:, 0:4, :]))
                act.wait_ge(sem("rwkv_mix"), 6)
                for m in range(KT):
                    last = f(r_x[:, m, :], half(0, m), ACT.Copy, scale=v("k_k", m))
                last.then_inc(sem("rwkv_rkv"), 1)
                act.wait_ge(sem("rkv_slot"), 12)
                copy(r_v, two(ps[:, 4:8, :])).then_inc(sem("rwkv_rkv"), 1)
                act.wait_ge(sem("rwkv_rkv"), 3)
                f(sq3, r_x, ACT.Square).then_inc(sem("rwkv_kk2"), 1)
                root(sq3)
                act.wait_ge(sem("rwkv_G"), 1)
                f(r_dec, r_g[:, :, CH - 1::CH], ACT.Exp)
                f(r_e1, r_g, ACT.Exp).then_inc(sem("rwkv_E"), 1)
                f(r_e2, r_g, ACT.Exp, scale=-1.0).then_inc(sem("rwkv_E"), 1)
                act.wait_ge(sem("rwkv_Gp"), 1)
                f(r_e3, r_w, ACT.Exp).then_inc(sem("rwkv_E"), 1)
                for p, (name, left, right) in enumerate(c_first):
                    if right is None:
                        for c in range(NCH):
                            act.wait_ge(sem("rw_first"), 4 * p + c + 1)
                            copy({"vs": c_vs, "bt": c_bt, "kt": c_kt}[name][c], heads((4 * p + c) % 8)).then_inc(sem("rw_first_a"), 1)
                for n in range(5 * NCH):
                    act.wait_ge(sem("rw_Y"), n + 1)
                    copy(c_y[n % NCH], heads(n % NCH)).then_inc(sem("rw_Ys"), 1)
                for c in range(NCH + 1):
                    if c < NCH:
                        act.wait_ge(sem("rw_rhs"), c + 1)
                        copy(c_y[c], heads(0)).then_inc(sem("rw_rhs_s"), 1)
                        act.wait_ge(sem("rw_u"), c + 1)
                        copy(c_t[c], heads(1)).then_inc(sem("rw_u_s"), 1)
                    if c > 0:
                        root(c_st[c - 1][:, 8:16])
                        act.wait_ge(sem("rw_out"), c)
                        copy(r_w[:, :, (c - 1) * CH:c * CH], heads(5 + (c - 1) % 2)).then_inc(sem("rw_y"), 1)

            def filters():
                act.wait_ge(sem("hg_lb_in"), 1)
                f(small[:, 168:184], small[:, 168:184], ACT.Exp).then_inc(sem("hg_lb_exp"), 1)
                for n in range(2):
                    act.wait_ge(sem("filter_arg"), n + 1)
                    f(f_in[0:64, 0, 0:T], f_in[0:64, 0, T:2 * T], ACT.Sin).then_inc(sem("filter_sin"), 1)
                sides = sq[:, :].rearrange("p (t s c) -> p t s c", t=TT, c=HYW)
                act.wait_ge(sem("filter_h"), 8)
                for o in range(2):
                    if o == 1:
                        act.wait_ge(sem("filter_l1"), 1)
                    for tt in range(TT):
                        last = f(sides[:, tt, :, :], f_h[:, tt, 2 * o:2 * o + 2, :], ACT.Abs)
                    last.then_inc(sem("filter_abs"), 1)

            def b2_in():
                for u, (s, what, context) in enumerate(B2_UNITS):
                    act.wait_ge(sem("b2_unit"), u + 1)
                    src = ps[:, u % 7, :]
                    src2 = src.rearrange("p (h t) -> p h t", t=T)
                    j = (s - 6) % 2
                    if what == "hy":
                        last = copy(hy_p[:, 2 * s:2 * s + 2, :], src2)
                    elif what == "q":
                        last = f(g_q[:, 2 * j:2 * j + 2, :], src2, ACT.Silu)
                    elif what == "i":
                        last = copy((x_v if context else g_v)[:, :, j * T:(j + 1) * T], src2)
                    elif what == "g":
                        last = f(g_g[:, 2 * j:2 * j + 2, :], src2, ACT.Silu)
                    else:
                        d = 0 if what == "zf" else 1
                        last = f((x_f if context else g_f)[:, d, 2 * j:2 * j + 2, :], src2, ACT.Sigmoid)
                    last.then_inc(sem("b2_evac"), 1)

            def hgrn():
                for i in range(4):
                    act.wait_ge(sem("hg_ctx_t"), i + 1)
                    copy(x_kt[:, i // 2, i % 2, :], ps[:, i, :]).then_inc(sem("hg_ctx_kt"), 1)
                act.wait_ge(sem("hg_state"), 2)
                for d in range(2):
                    copy(g_S[d], ps[:, 4 + d, :].rearrange("p (h s) -> p h s", s=P)).then_inc(sem("hg_state_s"), 1)
                act.wait_ge(sem("hg_cross"), 1)
                copy(g_X, ps[:, 0:2, :].rearrange("p d (h s) -> p d h s", s=P)).then_inc(sem("hg_cross_s"), 1)
                act.wait_ge(sem("hg_out"), 1)
                copy(g_F[:, 0], two(ps[:, 2:4, :])).then_inc(sem("hg_os"), 1)
                act.wait_ge(sem("hg_os"), 1)
                f(sq3[:, 0:4, :], g_F[:, 0], ACT.Square).then_inc(sem("hg_os"), 1)
                root(g_F[:, 1])

            def hyena():
                act.wait_ge(sem("hg_mixed"), 1)
                for m in range(12):
                    f(y_c[:, m, :], hy_p[:, m, :], ACT.Identity, scale=v("conv_w", 12 + m), bias=v("conv_b", m)) \
                        .then_inc(sem("hy_middle"), 1)
                for i in range(6):
                    act.wait_ge(sem("hy_turned"), i + 1)
                    copy(y_t[:, i // 3, (i % 3) * HYW:(i % 3 + 1) * HYW], ps[:, i, :]).then_inc(sem("hy_rows"), 1)
                act.wait_ge(sem("hy_z"), 2)
                for tt in range(TT):
                    f(sq[:, tt * HYW:(tt + 1) * HYW], y_m[:, tt, :], ACT.Square, accum_out=small[:, 208 + tt:209 + tt]) \
                        .then_inc(sem("hy_square"), 1)
                root(small[:, 208:210])
                for m in range(4):
                    act.wait_ge(sem("hy_back"), m + 1)
                    f(mix3[:, m, :], ps[:, m, 0:T], ACT.Copy, scale=v("hy_norm_g", m)).then_inc(sem("hy_mixed"), 1)

            def routing():
                act.wait_ge(sem("e_turned"), 1)
                copy(e_h, ps[:, 0:4, :].rearrange("p (t b) c -> p t (b c)", t=TT)).then_inc(sem("e_rows"), 1)
                act.wait_ge(sem("e_aff"), 1)
                f(e_aff, e_aff, ACT.Exp).then_inc(sem("e_rows"), 1)
                act.wait_ge(sem("e_aff_t"), 1)
                copy(e_row[0:NE, :], ps[0:NE, 5, 0:T]).then_inc(sem("e_rows"), 1)
                for b in range(8):
                    act.wait_ge(sem("e_backs"), b + 1)
                    copy(e_back[:, 2 * b:2 * b + 2, :], ps[:, b, :].rearrange("p (h t) -> p h t", t=T)).then_inc(sem("e_back"), 1)
                for kt in range(KT):
                    act.wait_ge(sem("e_gathers"), kt + 1)
                    copy(e_x[:, kt, :], ps[:, kt, :]).then_inc(sem("e_gather"), 1)

            def experts():
                with act.Fori(0, NE) as e:
                    act.wait_ge(sem("moe_slot"), PER_EXPERT * e + 8)
                    f(e_s, ps[:, 0, :], ACT.Silu).then_inc(sem("moe_silu"), 1)
                    act.wait_ge(sem("moe_turned"), e + 1)
                    copy(e_hT, ps[:, 2, :].rearrange("p (i c) -> p i c", c=P)).then_inc(sem("moe_hT"), 1)
                    act.wait_ge(sem("moe_slot"), PER_EXPERT * e + PER_EXPERT)
                    copy(e_y, ps[:, 3, :]).then_inc(sem("moe_y"), 1)

            act.wait_ge(sem("start_landed"), 64)
            f(c_rows, c_rows, ACT.Silu).then_inc(sem("c_ready"), 1)
            modulated(0, None, 0, 0)
            ffn(0)
            modulated(1, 1, 0, 1)
            mla()
            modulated(2, 2, 0, 2)
            ffn(1)
            modulated(3, 3, 1, 0)
            ffn(2)
            modulated(4, 4, 1, 1)
            rwkv()
            modulated(5, 5, 1, 2)
            ffn(3)
            filters()
            act.wait_ge(sem("filter_done"), 2)
            norm(6, 6)
            norm(7, 7, shift=mods[:, 144:152])
            act.wait_ge(sem("ctx_landed"), 16)
            norm(8, None, ctx3, hc3, shift=cmods[:, 0:8])
            b2_in()
            hgrn()
            hyena()
            norm(9, 8, shift=mods[:, 144 + 24:144 + 32])
            routing()
            experts()
            norm(10, 9)
            act.wait_ge(sem("row_turned"), 1)
            copy(o_row, ps[:, 0:4, :].rearrange("p (t b) c -> p t (b c)", t=TT)).then_inc(sem("row_ready"), 1)

        @block.gpsimd
        def _(pool):
            nc.gpsimd.memset(zeros[:, :], 0.0).then_inc(sem("zeros"), 1)
            pool.wait_ge(sem("h_ready"), 5 * KT)
            for c in range(NCH):
                for buf in (c_t[c], c_tt[c]):
                    nc.gpsimd.tensor_copy(buf, bcm(k("i64"), KT)).then_inc(sem("rw_ident"), 1)

        @block.vector
        def _(dve):
            n_order = [0]

            def done(ins):
                n_order[0] += 1
                ins.then_inc(sem("dve_order"), 1)
                dve.wait_ge(sem("dve_order"), n_order[0])

            tt_, ts, stt, cp = (nc.vector.tensor_tensor, nc.vector.tensor_scalar, nc.vector.scalar_tensor_tensor,
                                nc.vector.tensor_copy)
            red = nc.vector.tensor_reduce

            def two(ap):
                return ap.rearrange("p b (h t) -> p (b h) t", t=T)

            n_root = [0]

            def inverse_root(ins, buf):
                n_root[0] += 1
                ins.then_inc(sem("root_in"), 1)
                dve.wait_ge(sem("root_out"), n_root[0])
                done(nc.vector.reciprocal(buf, buf))

            def norm(i, src, dst, scale, name="h_scaled"):
                dve.wait_ge(sem("norm_sum"), i + 1)
                inverse_root(ts(rstd[:, :], norm_sums(i), 1.0 / D, EPS, ALU.mult, ALU.add), rstd[:, :])
                for m in range(KT):
                    stt(out=dst[:, m, :], in0=src[:, m, :], scalar=scale[:, m:m + 1], in1=rstd[:, :], op0=ALU.mult, op1=ALU.mult) \
                        .then_inc(sem(name), 1)

            def scale_of(at, g, src=mods, to=0):
                done(stt(out=coef[:, to:to + 8], in0=src[:, at:at + 8], scalar=1.0, in1=g, op0=ALU.add, op1=ALU.mult))

            def gate_of(at, factor):
                done(ts(coef[:, 8:16], mods[:, at:at + 8], factor, None, ALU.mult))

            def residual(src=None):
                for m in range(KT):
                    stt(out=x3[:, m, :], in0=acc(m) if src is None else src(m), scalar=coef[:, 8 + m:9 + m],
                        in1=x3[:, m, :], op0=ALU.mult, op1=ALU.add).then_inc(sem("x_ready"), 1)

            def ada_round(r, row, context=False, junk=sq):
                def dot(w, which, col, out_at, buf, done_sem):
                    nc.vector.tensor_tensor_reduce(buf[:, out_at * D:(out_at + 1) * D], w, c_rows[:, which * D:(which + 1) * D],
                                                   1.0, 0.0, ALU.mult, ALU.add, dots[:, col:col + 1]).then_inc(sem(done_sem), 1)

                dve.wait_ge(sem("ada_kept"), r)
                for j in range(NADA):
                    dve.wait_ge(sem(f"ada_landed{j}"), 16 * r + 16)
                    w = ada_slot(j)
                    if context:
                        dve.wait_ge(sem("ada_context"), 9 * (r - 18) + 2 * j)
                        for i in range(2):
                            dot(w[:, i, :], 2, 8 + 2 * j + i, i, ar(0, 2 * D), "ada_context")
                    dve.wait_ge(sem("ada_first"), 4 * r + j)
                    dot(w[:, 0, :], row, 2 * j, 0, junk, "ada_first")
                    dve.wait_ge(sem("ada_used"), 4 * r + j)
                    dot(w[:, 1, :], row, 2 * j + 1, 1, junk, "ada_used")
                dve.wait_ge(sem("ada_first"), 4 * r + 4)
                dve.wait_ge(sem("ada_used"), 4 * r + 4)
                cp(mods[:, bass.ds(8 * r, 8)], dots[:, 0:8]).then_inc(sem("ada_kept"), 1)
                if context:
                    dve.wait_ge(sem("ada_context"), 9 * (r - 18) + 8)
                    cp(cmods[:, bass.ds(8 * (r - 18), 8)], dots[:, 8:16]).then_inc(sem("ada_context"), 1)

            def hidden(t):
                for ft in range(2):
                    dve.wait_ge(sem("silu_ready"), 2 * t + ft + 1)
                    tt_(hid3[:, ft, :], sil3[:, ft, :], ps[:, ft, T:2 * T], ALU.mult).then_inc(sem("hid_ready"), 1)

            def ffn(n):
                for lo, hi, row, context in {0: [(0, NG, 0, False)], 1: [(0, 5, 0, False), (5, 7, 1, True), (7, NG, 1, False)]} \
                        .get(n, [(0, NG, None, False)]):
                    if context:
                        for t in range(NG * n + lo, NG * n + hi):
                            hidden(t)
                            ada_round(t + ADA_FIRST, row, True)
                        continue
                    with dve.Fori(lo, hi) as g:
                        t = g + NG * n
                        hidden(t)
                        if row is not None:
                            ada_round(t + ADA_FIRST, row)
                dve.wait_ge(sem("down_used"), NG * (n + 1) + 1)
                residual()

            def ada_bias(lo, hi, kept):
                dve.wait_ge(sem("ada_kept"), kept)
                done(tt_(mods[:, lo:hi], mods[:, lo:hi], v("ada_b", lo, hi - lo), ALU.add))

            def mixed(n):
                dve.wait_ge(sem("proj_slot"), 4 * n + 4)
                residual()

            def mla():
                dve.wait_ge(sem("mla_in"), 7)
                r2 = m_rope
                done(ts(r2[:, 0, :], ps[:, 3, 0:T], 1.0 / 384, EPS, ALU.mult, ALU.add))
                inverse_root(ts(r2[:, 1, :], ps[:, 3, T:2 * T], 1.0 / 256, EPS, ALU.mult, ALU.add), r2)
                for m in range(5):
                    g = v("q_norm", m) if m < 3 else v("kv_norm", m - 3)
                    last = stt(out=m_c[:, m, :], in0=m_c[:, m, :], scalar=g, in1=r2[:, 0 if m < 3 else 1, :],
                               op0=ALU.mult, op1=ALU.mult)
                last.then_inc(sem("mla_normed"), 1)
                dve.wait_ge(sem("mla_normed"), 1)
                rope = k("rope")
                done(tt_(m_k[64:96, 0, :], m_c[64:96, 5, :], rope[64:96, :], ALU.mult))
                done(tt_(m_rope[64:96, 0, :], m_c[96:128, 5, :], rope[96:128, :], ALU.mult))
                done(tt_(m_k[64:96, 0, :], m_k[64:96, 0, :], m_rope[64:96, 0, :], ALU.add))
                cp(m_k[64:96, 1:HEADS, :], bcm(m_k[64:96, 0, :], HEADS - 1)).then_inc(sem("mla_k_rope"), 1)
                for b in range(8):
                    dve.wait_ge(sem("mla_q"), b + 1)
                    q, src = m_q[:, 2 * b:2 * b + 2, :], ps[:, b, :].rearrange("p (h t) -> p h t", t=T)
                    done(tt_(q[64:96], src[64:96], bcm(rope[64:96, :], 2), ALU.mult))
                    done(tt_(m_rope[64:96], src[96:128], bcm(rope[96:128, :], 2), ALU.mult))
                    tt_(q[64:96], q[64:96], m_rope[64:96], ALU.add).then_inc(sem("mla_q_rope"), 1)
                    dve.wait_ge(sem("mla_q_rope"), b + 1)
                for i in range(4):
                    dve.wait_ge(sem("mla_kv"), 5 + i)
                    cp(m_v[:, i // 2, (i % 2) * 512:(i % 2 + 1) * 512], ps[:, 4 + i, :]).then_inc(sem("mla_v"), 1)
                for b in range(4):
                    s, st = 3 * (b % 2), m_st[:, 32 * (b % 2):32 * (b % 2) + 32]
                    s0, s1 = ps[:, s, :].rearrange("p (h t) -> p h t", t=P), two(ps[:, s + 1:s + 3, :])
                    dve.wait_ge(sem("mla_scores"), b + 1)
                    done(tt_(s0, s0, bcm(k("causal"), 4), ALU.add))
                    done(tt_(s1[:, :, P:T], s1[:, :, P:T], bcm(k("causal"), 4), ALU.add))
                    done(red(st[:, 0:4], s0, AXX, ALU.max))
                    done(red(st[:, 4:8], s1, AXX, ALU.max))
                    ts(st[:, 8:16], st[:, 0:8], -(QK ** -0.5), None, ALU.mult).then_inc(sem("mla_max"), 1)
                    dve.wait_ge(sem("mla_exp"), 8 * b + 8)
                    done(nc.vector.reciprocal(st[:, 24:32], st[:, 16:24]))
                    done(tt_(m_p0, m_p0, bc(st[:, 24:28], P), ALU.mult))
                    tt_(m_p1, m_p1, bc(st[:, 28:32], T), ALU.mult).then_inc(sem("mla_probs"), 1)
                    dve.wait_ge(sem("mla_turned"), b + 1)
                    cp(m_t1, s0).then_inc(sem("mla_t1"), 1)

            def heads(bank):
                return tiles(ps[:, bank, :], HD)

            def rwkv():
                dve.wait_ge(sem("h_ready"), 5 * KT)
                nc.vector.memset(sil3[:, 1, :], 0.0).then_inc(sem("zeros"), 1)
                done(tt_(r_x[:, :, 1:T], h3[:, :, 0:T - 1], h3[:, :, 1:T], ALU.subtract))
                done(ts(r_x[:, :, 0:1], h3[:, :, 0:1], -1.0, None, ALU.mult))
                for n, part in enumerate((3, 4, 5, 0, 1, 2)):
                    dst = r_b if n % 2 else r_g
                    if n in (2, 3):
                        dve.wait_ge(sem("rwkv_low1"), n - 1)
                    elif n == 4:
                        dve.wait_ge(sem("rwkv_low1"), 3)
                    elif n == 5:
                        dve.wait_ge(sem("rkv_slot"), 4)
                    for m in range(KT):
                        last = stt(out=dst[:, m, :], in0=r_x[:, m, :], scalar=v("mu", 8 * part + m), in1=h3[:, m, :],
                                   op0=ALU.mult, op1=ALU.add)
                    last.then_inc(sem("rwkv_mix"), 1)
                dve.wait_ge(sem("rwkv_sig"), 2)
                done(ts(r_w, r_w, -float(np.exp(-0.5)), None, ALU.mult))
                dve.wait_ge(sem("rwkv_rkv"), 2)
                for m in range(KT):
                    last = ts(r_g[:, m, :], r_a[:, m, :], -1.0, v("k_a", m), ALU.add, ALU.mult)
                done(last)
                done(stt(out=r_k, in0=r_g, scalar=1.0, in1=r_k, op0=ALU.add, op1=ALU.mult))
                dve.wait_ge(sem("rwkv_rkv"), 3)
                for m in range(KT):
                    last = stt(out=r_b[:, m, :], in0=r_r[:, m, :], scalar=v("r_k", m), in1=r_k[:, m, :],
                               op0=ALU.mult, op1=ALU.mult)
                last.then_inc(sem("rwkv_prod"), 1)
                for m in range(KT):
                    last = nc.vector.tensor_tensor_scan(r_g[:, m, :], k("keep"), r_w[:, m, :], 0.0, ALU.mult, ALU.add)
                last.then_inc(sem("rwkv_G"), 1)
                dve.wait_ge(sem("rwkv_G"), 1)
                tt_(r_w, r_g, r_w, ALU.subtract).then_inc(sem("rwkv_Gp"), 1)
                dve.wait_ge(sem("rwkv_sums"), 1)
                n_root[0] += 1
                ts(sq3, two(ps[:, 0:4, :]), 1e-24, None, ALU.max).then_inc(sem("root_in"), 1)
                dve.wait_ge(sem("root_out"), n_root[0])
                nc.vector.reciprocal(sq3, sq3)
                dve.wait_ge(sem("rwkv_sums"), 2)
                tt_(r_b, two(ps[:, 4:8, :]), r_v, ALU.mult)
                dve.wait_ge(sem("rwkv_E"), 2)
                tt_(r_r, r_r, r_e1, ALU.mult)
                done(tt_(r_k, r_k, r_e2, ALU.mult))
                done(tt_(r_x, r_x, sq3, ALU.mult))
                done(tt_(r_a, r_a, r_x, ALU.mult))
                dve.wait_ge(sem("rwkv_E"), 3)
                stt(out=r_x, in0=r_x, scalar=-1.0, in1=r_e3, op0=ALU.mult, op1=ALU.mult)
                tt_(r_a, r_a, r_e2, ALU.mult).then_inc(sem("rwkv_prep"), 1)
                dve.wait_ge(sem("rwkv_prep"), 1)
                dve.wait_ge(sem("rw_ident"), 2 * NCH)
                low, up = (k(name).bitcast(U32) for name in ("low64", "up64"))
                n = 0
                for p, (name, left, right) in enumerate(c_first):
                    if right is not None:
                        for c in range(NCH):
                            src = heads((4 * p + c) % 8)
                            n += 1
                            dve.wait_ge(sem("rw_first"), 4 * p + c + 1)
                            if name == "m":
                                nc.vector.copy_predicated(c_t[c], bcm(low[:, 0:HD], KT), src).then_inc(sem("rw_first_d"), 1)
                                dve.wait_ge(sem("rw_first_d"), n)
                                nc.vector.copy_predicated(c_tt[c], bcm(up[:, 0:HD], KT), c_ab[c]).then_inc(sem("rw_T"), 1)
                            else:
                                dst = {"ab": c_ab, "ak": c_ak, "rb": c_rb, "rk": c_rk}[name][c]
                                tt_(dst, src, bcm(k("before" if name in ("ab", "ak") else "upto"), KT), ALU.mult) \
                                    .then_inc(sem("rw_first_d"), 1)
                for lev in range(1, 6):
                    for c in range(NCH):
                        dve.wait_ge(sem("rw_Z"), 4 * (lev - 1) + c + 1)
                        dve.wait_ge(sem("rw_T"), 4 * (lev - 1) + c + 1)
                        at = slice(lev * HD, (lev + 1) * HD)
                        if lev < 5:
                            nc.vector.copy_predicated(c_t[c], bcm(low[:, at], KT), heads(c))
                        nc.vector.copy_predicated(c_tt[c], bcm(up[:, at], KT), heads(4 + c)).then_inc(sem("rw_T"), 1)
                for c in range(NCH):
                    if c < NCH - 1:
                        dve.wait_ge(sem("rw_ds"), c + 1)
                        ds_ = heads(4)
                        if c > 0:
                            done(tt_(c_s, c_s, ds_, ALU.add))
                            ds_ = c_s
                        tt_(c_s, ds_, bc(r_dec[:, :, c], HD), ALU.mult).then_inc(sem("rw_S"), 1)
                    st, mid, square = c_st[c], c_tt[c], c_y[c]
                    dve.wait_ge(sem("rw_o"), c + 1)
                    done(red(st[:, 0:8], heads(2 + c % 2), AXX, ALU.add))
                    done(ts(st[:, 0:8], st[:, 0:8], 1.0 / HD, None, ALU.mult))
                    done(tt_(mid, heads(2 + c % 2), bc(st[:, 0:8], HD), ALU.subtract))
                    done(tt_(square, mid, mid, ALU.mult))
                    done(red(st[:, 8:16], square, AXX, ALU.add))
                    inverse_root(ts(st[:, 8:16], st[:, 8:16], 1.0 / HD, GN_EPS, ALU.mult, ALU.add), st[:, 8:16])
                    tt_(c_ab[c], mid, bc(st[:, 8:16], HD), ALU.mult).then_inc(sem("rw_yb"), 1)
                dve.wait_ge(sem("rw_y"), NCH)
                for m in range(KT):
                    last = ts(r_w[:, m, :], r_w[:, m, :], v("gn_w", m), v("gn_b", m), ALU.mult, ALU.add)
                done(last)
                done(tt_(r_w, r_w, r_b, ALU.add))
                tt_(r_w, r_w, r_o, ALU.mult).then_inc(sem("rwkv_y"), 1)

            def filters():
                lb0, lb1 = v("hg_lb", 0, 8), v("hg_lb", 8, 8)
                done(tt_(small[:, 160:168], lb0, lb1, ALU.max))
                done(tt_(small[:, 168:176], lb0, small[:, 160:168], ALU.subtract))
                tt_(small[:, 176:184], lb1, small[:, 160:168], ALU.subtract).then_inc(sem("hg_lb_in"), 1)
                dve.wait_ge(sem("hg_lb_exp"), 1)
                done(tt_(small[:, 184:192], small[:, 168:176], small[:, 176:184], ALU.add))
                done(nc.vector.reciprocal(small[:, 184:192], small[:, 184:192]))
                done(tt_(small[:, 192:200], small[:, 168:176], small[:, 184:192], ALU.mult))
                done(ts(small[:, 200:208], small[:, 192:200], -1.0, 1.0, ALU.mult, ALU.add))
                arg, turns = f_in[0:64, 0, T:2 * T], f_in[0:64, 1, 0:T]
                magic = 1.5 * 2.0 ** 23
                c1 = 6.28125
                c2 = float(np.floor((2 * np.pi - c1) * 2.0 ** 22) / 2.0 ** 22)
                c3 = 2 * np.pi - c1 - c2
                for n, (b, fr) in enumerate((("pos_b1", "freq1"), ("pos_b2", "freq2"))):
                    dve.wait_ge(sem("filter_mm"), n + 1)
                    done(ts(arg, ps[0:64, n, 0:T], v(b)[0:64], v(fr)[0:64], ALU.add, ALU.mult))
                    done(ts(turns, arg, 1.0 / (2 * np.pi), magic, ALU.mult, ALU.add))
                    done(ts(turns, turns, magic, None, ALU.subtract))
                    for part in (c1, c2, c3):
                        done(stt(out=arg, in0=turns, scalar=-part, in1=arg, op0=ALU.mult, op1=ALU.add))
                    ts(arg, arg, 3.1415925, -3.1415925, ALU.min, ALU.max).then_inc(sem("filter_arg"), 1)
                win = f_win[:, 0:TT * 2 * HYW].rearrange("p (t s c) -> p t s c", t=TT, c=HYW)
                for i in range(8):
                    dve.wait_ge(sem("filter_mm"), 3 + i)
                    tt_(f_h[:, i // 4, i % 4, :], ps[:, i, :], win[:, i // 4, i % 2, :], ALU.mult).then_inc(sem("filter_h"), 1)
                for o in range(2):
                    dve.wait_ge(sem("filter_l1"), o + 1)
                    done(ts(f_rn[:, o, :], ps[:, o, :], EPS, None, ALU.add))
                    done(nc.vector.reciprocal(f_rn[:, o, :], f_rn[:, o, :]))
                for o in range(2):
                    done(tt_(f_sum, f_h[:, :, 2 * o, :], f_h[:, :, 2 * o + 1, :], ALU.add))
                    tt_(f_dif, f_h[:, :, 2 * o, :], f_h[:, :, 2 * o + 1, :], ALU.subtract).then_inc(sem("filter_sides"), 1)
                    dve.wait_ge(sem("filter_freq"), o + 1)
                    rn, bias = f_rn[:, o, :], f_bias[:, o, :]
                    done(tt_(f_A[o], ps[:, 2:4, :], bcm(rn, 2), ALU.mult))
                    done(tt_(f_A[o], f_A[o], bcm(bias, 2), ALU.add))
                    done(tt_(f_D[o], ps[:, 6, :], rn, ALU.mult))
                    done(tt_(f_D[o], f_D[o], bias, ALU.add))
                    tt_(f_B[o], ps[:, 4:6, :], bcm(rn, 2), ALU.mult).then_inc(sem("filter_done"), 1)

            def gates(f_, k_):
                for d in range(2):
                    for h in range(HGH):
                        i = 4 * d + h
                        last = ts(f_[:, d, h, :], f_[:, d, h, :], small[:, 200 + i:201 + i], small[:, 192 + i:193 + i],
                                  ALU.mult, ALU.add)
                done(last)
                done(ts(k_, f_, -1.0, 1.0, ALU.mult, ALU.add))

            def hgrn():
                dve.wait_ge(sem("b2_evac"), len(B2_UNITS))
                done(nc.vector.memset(rstd[:, :], 0.0))
                gates(x_f, x_k)
                done(nc.vector.memset(x_E[:, 0, :, T - 1:T], 1.0))
                done(nc.vector.memset(x_E[:, 1, :, 0:1], 1.0))
                for h in range(HGH):
                    nc.vector.tensor_tensor_scan(x_E[:, 0, h, 0:T - 1][:, ::-1], x_f[:, 0, h, 1:T][:, ::-1], rstd[:, 0:T - 1],
                                                 1.0, ALU.mult, ALU.add)
                    last = nc.vector.tensor_tensor_scan(x_E[:, 1, h, 1:T], x_f[:, 1, h, 0:T - 1], rstd[:, 0:T - 1],
                                                        1.0, ALU.mult, ALU.add)
                done(last)
                tt_(x_k, x_k, x_E, ALU.mult).then_inc(sem("hg_gates"), 1)
                gates(g_f, g_k)
                ts(g_q, g_q, float(P) ** -0.5, None, ALU.mult).then_inc(sem("hg_gates"), 1)
                dve.wait_ge(sem("hg_gates"), 2)
                dve.wait_ge(sem("hg_state"), 2)
                cp(g_F, g_f)
                done(nc.vector.memset(g_E, 1.0))
                for lev in range(NLEV + 2):
                    hb = 1 << lev
                    if lev <= NLEV:
                        if lev >= 1:
                            dve.wait_ge(sem("hg_level"), lev + 1)
                        for d in range(2):
                            late, early = (1, 0) if d == 0 else (0, 1)

                            def cut(ap, side):
                                return ap.rearrange("p h (b s t) -> p (h b) s t", s=2, t=hb)[:, :, side, :]

                            tt_(cut(g_Q[:, d], late), cut(g_q, late), cut(g_F[:, d], late), ALU.mult)
                            last = tt_(cut(g_K[:, d], early), cut(g_k[:, d], early), cut(g_E[:, d], early), ALU.mult)
                        last.then_inc(sem("hg_scaled"), 1)
                        dve.wait_ge(sem("hg_scaled"), lev + 1)
                        for d in range(2):
                            late, early = (1, 0) if d == 0 else (0, 1)
                            end = hb - 1 if d == 0 else 0
                            edge_l = cut(g_F[:, d], late)[:, :, end:end + 1].to_broadcast([P, HGH * T // (2 * hb), hb])
                            edge_e = cut(g_F[:, d], early)[:, :, end:end + 1].to_broadcast([P, HGH * T // (2 * hb), hb])
                            done(tt_(cut(g_E[:, d], early), cut(g_E[:, d], early), edge_l, ALU.mult))
                            done(tt_(cut(g_F[:, d], late), cut(g_F[:, d], late), edge_e, ALU.mult))
                    else:
                        dve.wait_ge(sem("hg_cross"), 1)
                        for d in range(2):
                            last = tt_(g_Q[:, d], g_q, g_F[:, d], ALU.mult)
                        last.then_inc(sem("hg_scaled"), 1)
                    if lev <= NLEV:
                        dve.wait_ge(sem("hg_level"), lev + 1)
                        for d in range(2):
                            for tt in range(TT):
                                src = ps[:, 4 * (lev % 2) + 2 * d + tt, :].rearrange("p (h s) -> p h s", s=P)
                                if lev == 0:
                                    last = tt_(g_A[:, d, tt], src, bcm(ident, HGH), ALU.mult)
                                else:
                                    mask = k("up" if d == 0 else "low", (lev - 1) * P, P).bitcast(U32)
                                    last = nc.vector.copy_predicated(g_A[:, d, tt], bcm(mask, HGH), src)
                        last.then_inc(sem("hg_taken"), 1)
                dve.wait_ge(sem("hg_out"), 2)
                o, r = g_F[:, 0], g_F[:, 1]
                inverse_root(ts(r, two(ps[:, 4:6, :]), 1.0 / P, EPS, ALU.mult, ALU.add), r)
                done(stt(out=o, in0=o, scalar=v("hg_norm_g"), in1=r, op0=ALU.mult, op1=ALU.mult))
                tt_(mix3[:, 4:8, :], o, g_g, ALU.mult).then_inc(sem("hg_mixed"), 1)

            def hyena():
                rows = T // GRID
                for m in range(12):
                    dve.wait_ge(sem("hy_middle"), m + 1)
                    y = y_c[:, m, :].rearrange("p (r g) -> p r g", g=GRID)
                    p_ = hy_p[:, m, :].rearrange("p (r g) -> p r g", g=GRID)
                    done(stt(out=y[:, :, 1:GRID], in0=p_[:, :, 0:GRID - 1], scalar=v("conv_w", m), in1=y[:, :, 1:GRID],
                             op0=ALU.mult, op1=ALU.add))
                    last = stt(out=y[:, :, 0:GRID - 1], in0=p_[:, :, 1:GRID], scalar=v("conv_w", 24 + m),
                               in1=y[:, :, 0:GRID - 1], op0=ALU.mult, op1=ALU.add)
                last.then_inc(sem("hy_conv"), 1)
                for o in range(2):
                    dve.wait_ge(sem("hy_u"), o + 1)
                    tmp = sq[:, 1024:1536]
                    for ft in range(2):
                        uc, us = ps[:, ft, :], ps[:, 2 + ft, :]
                        A, B, Dd = f_A[o][:, ft, :], f_B[o][:, ft, :], (f_D[o] if ft == 0 else f_A[o][:, 1, :])
                        done(tt_(y_cc[:, ft, :], uc, A, ALU.mult))
                        done(tt_(tmp, us, B, ALU.mult))
                        done(tt_(y_cc[:, ft, :], y_cc[:, ft, :], tmp, ALU.subtract))
                        done(tt_(y_ss[:, ft, :], uc, B, ALU.mult))
                        done(tt_(tmp, us, Dd, ALU.mult))
                        last = tt_(y_ss[:, ft, :], y_ss[:, ft, :], tmp, ALU.add)
                    last.then_inc(sem("hy_y"), 1)
                    dve.wait_ge(sem("hy_v"), o + 1)
                    for tt in range(TT):
                        last = tt_((y_m if o else y_z)[:, tt, :], ps[:, 4 + tt, :], y_t[:, tt, HYW * (o + 1):HYW * (o + 2)], ALU.mult)
                    last.then_inc(sem("hy_z"), 1)
                dve.wait_ge(sem("hy_square"), 2)
                inverse_root(ts(small[:, 208:210], small[:, 208:210], 1.0 / HYW, EPS, ALU.mult, ALU.add), small[:, 208:210])
                tt_(y_m, y_m, bc(small[:, 208:210], HYW), ALU.mult).then_inc(sem("hy_normed"), 1)

            def routing():
                dve.wait_ge(sem("e_turned"), 2)
                lg = ps[:, 4, 0:TT * NE].rearrange("p (t e) -> p t e", t=TT)
                done(red(e_st[:, 0:2], lg, AXX, ALU.max))
                tt_(e_aff, lg, bc(e_st[:, 0:2], NE), ALU.subtract).then_inc(sem("e_aff"), 1)
                dve.wait_ge(sem("e_rows"), 2)
                done(red(e_st[:, 2:4], e_aff, AXX, ALU.add))
                done(nc.vector.reciprocal(e_st[:, 4:6], e_st[:, 2:4]))
                tt_(e_aff, e_aff, bc(e_st[:, 4:6], NE), ALU.mult).then_inc(sem("e_aff"), 1)
                dve.wait_ge(sem("e_aff"), 2)
                unit = e_s[:, 0:T]
                done(nc.vector.memset(unit, 1.0))
                for tt in range(TT):
                    done(tt_(e_diag[:, tt * NE:(tt + 1) * NE, :], bcm(ident, NE), bc(e_aff[:, tt, :], P), ALU.mult))
                dve.wait_ge(sem("early_landed"), 16)
                before = n_order[0]
                for e in range(NE):
                    dve.wait_ge(sem("e_spread"), 2 * (e // 2) + 2)
                    if e >= 2:
                        dve.wait_ge(sem("dve_order"), before + e - 1)
                    for tt in range(TT):
                        cmp = e_cmp[:, 4 * (e % 2) + 2 * tt:4 * (e % 2) + 2 * tt + 2, :]
                        stt(out=cmp[:, 0, :], in0=half(0, e), scalar=e_aff[:, tt, e:e + 1], in1=unit, op0=ALU.is_gt,
                            op1=ALU.mult, accum_out=e_rank[:, tt, e:e + 1])
                        last = stt(out=cmp[:, 1, :], in0=half(0, e), scalar=e_aff[:, tt, e:e + 1], in1=e_early[:, tt, :],
                                   op0=ALU.is_equal, op1=ALU.mult, accum_out=e_tie[:, tt, e:e + 1])
                    last.then_inc(sem("dve_order"), 1)
                n_order[0] += NE
                dve.wait_ge(sem("dve_order"), n_order[0])
                done(tt_(e_rank, e_rank, e_tie, ALU.add))
                for tt in range(TT):
                    done(tt_(e_sel[:, tt], bcm(k("iota"), NE), bc(e_rank[:, tt, :], CAP), ALU.is_equal))
                rep = ar(16880, 4096).rearrange("p (t e r c) -> p (t e) r c", t=TT, r=4, c=CAP)
                flat = e_sel.rearrange("p t e c -> p (t e) c")
                for r in range(4):
                    last = cp(rep[:, :, r, :], flat)
                last.then_inc(sem("e_select"), 1)
                dve.wait_ge(sem("e_gather"), KT)

            def experts():
                def tokens(at):
                    cp(e_xe, e_x[:, :, at]).then_inc(sem("moe_x"), 1)

                back = e_back.rearrange("p a b -> p (a b)")

                def gated(e):
                    dve.wait_ge(sem("moe_slot"), PER_EXPERT * e + 8)
                    cp(e_bk, back[:, bass.ds(T * e, T)])
                    dve.wait_ge(sem("moe_slot"), PER_EXPERT * e + 16)
                    dve.wait_ge(sem("moe_silu"), e + 1)
                    tt_(e_h2, e_s, ps[:, 1, :], ALU.mult).then_inc(sem("moe_h"), 1)

                tokens(slice(0, CAP))
                with dve.Fori(0, NE - 1) as e:
                    gated(e)
                    tokens(bass.ds(CAP * e + CAP, CAP))
                gated(NE - 1)

            def site(layer, s):
                return 72 * layer + 24 * s

            def modulated(i, layer, s, factor):
                at = site(layer, s)
                scale_of(at + 8, v("norm_g", 8 * (3 * layer + s), 8))
                norm(i, x3, h3, coef[:, 0:8])

            dve.wait_ge(sem("c_ready"), 1)
            for r in range(ADA_FIRST):
                ada_round(r, 0, junk=hT)
            ada_bias(0, 16, ADA_FIRST)
            modulated(0, 0, 0, 0.5)
            with dve.Fori(0, NG) as g:
                hidden(g)
                ada_round(g + ADA_FIRST, 0)
            ada_bias(16, 8 * (ADA_FIRST + NG), ADA_FIRST + NG)
            gate_of(site(0, 0) + 16, 0.5)
            dve.wait_ge(sem("down_used"), NG + 1)
            residual()
            modulated(1, 0, 1, 1.0)
            mla()
            gate_of(site(0, 1) + 16, 1.0)
            mixed(0)
            modulated(2, 0, 2, 0.5)
            gate_of(site(0, 2) + 16, 0.5)
            ffn(1)
            ada_bias(8 * (ADA_FIRST + NG), N_MODS, ADA_FIRST + 2 * NG)
            dve.wait_ge(sem("ada_context"), 18)
            done(tt_(cmods[:, :], cmods[:, :], v("ada_b", 144, 16), ALU.add))
            modulated(3, 1, 0, 0.5)
            gate_of(site(1, 0) + 16, 0.5)
            ffn(2)
            modulated(4, 1, 1, 1.0)
            rwkv()
            gate_of(site(1, 1) + 16, 1.0)
            mixed(1)
            modulated(5, 1, 2, 0.5)
            gate_of(site(1, 2) + 16, 0.5)
            ffn(3)
            filters()
            norm(6, x3, x3, v("final_g", 0, 8), name="x_ready")
            scale_of(144 + 8, v("norm1_g", 0, 8))
            norm(7, x3, h3, coef[:, 0:8])
            scale_of(8, v("norm1_g", 0, 8), src=cmods, to=16)
            norm(8, ctx3, hc3, coef[:, 16:24])
            hgrn()
            hyena()
            gate_of(144 + 16, 1.0)
            mixed(2)
            scale_of(144 + 32, v("norm2_g", 0, 8))
            norm(9, x3, h3, coef[:, 0:8])
            routing()
            experts()
            gate_of(144 + 40, 1.0)
            dve.wait_ge(sem("moe_o"), NE)
            residual(lambda m: half(4, m))
            norm(10, x3, h3, v("final_g2", 0, 8), name="h_ready")


INPUTS = ("con", "big", "win", "earlier", "vec", "xT", "ctxT", "c_rows", "ada", "ffn_gate", "ffn_up", "ffn_down",
          "ring_w", "w1", "w3", "w2", "pos_w", "hy_bias")


def kernel(**inputs):
    import concourse.bacc as bacc
    from concourse.bass_utils import run_bass_kernel_spmd

    laid = lay_out(inputs)
    nc = bacc.Bacc("TRN2", target_bir_lowering=False, num_devices=1)
    arrays, args = {}, {}
    for name in INPUTS:
        arrays[f"in_{name}"] = np.ascontiguousarray(laid[name])
        args[name] = nc.dram_tensor(f"in_{name}", arrays[f"in_{name}"].shape, F32, kind="ExternalInput").ap()
    out = nc.dram_tensor("out_0", (T, D), F32, kind="ExternalOutput").ap()
    build(nc, args, out)
    r = run_bass_kernel_spmd(nc, [arrays], core_ids=[0])
    return r.results[0]["out_0"].reshape(1, T, D)
```

```python
from contextlib import ExitStack

import numpy as np

import concourse.bass as bass
from concourse import mybir

P = 128
D = 1024
KT = D // P
T = 256
TT = T // P
FF = 2816
FG = 256
NG = FF // FG
NFFN = 4
SLOT = 2048
NRING = 4
E_RING = 12
NADA = 4
EPS = 1e-6

HEADS = 16
NOPE, ROPE = 64, 32
QK = NOPE + ROPE
HD = 64
CH = 64
NCH = T // CH
GN_EPS = 64e-5

HYW = 512
HGH = 4
GRID = 64
NE = 16
CAP = 2 * T // NE
EFF = 2048

SEQ_MLA = 0
SEQ_RWKV = 12
SEQ_B2 = 32
SEQ_MOE = 52
PER_EXPERT = 24

ADA_FIRST = 2
N_MODS = 72 + 72 + 48

F32 = mybir.dt.float32
BF16 = mybir.dt.bfloat16
U32 = mybir.dt.uint32
ALU = mybir.AluOpType
ACT = mybir.ActivationFunctionType
AXX = mybir.AxisListType.X


def layout(sizes):
    at, out = 0, {}
    for name, n in sizes:
        out[name] = (at, n)
        at += n
    return out, at


VEC, NVEC = layout([
    ("norm_g", 48), ("final_g", 8), ("ada_b", N_MODS), ("q_norm", 3), ("kv_norm", 2),
    ("mu", 48), ("w0", 8), ("a0", 8), ("k_k", 8), ("k_a", 8), ("r_k", 8), ("gn_w", 8), ("gn_b", 8),
    ("norm1_g", 8), ("conv_w", 36), ("conv_b", 12), ("pos_b1", 1), ("freq1", 1), ("pos_b2", 1),
    ("freq2", 1), ("hy_norm_g", 4), ("hg_lb", 16), ("hg_norm_g", 1), ("norm2_g", 8), ("final_g2", 8),
    ("rw", KT * NE),
])
NLEV = 7
CON, NCON = layout([
    ("ident", P), ("ones", P), ("blk", P), ("causal", P), ("before", HD), ("upto", HD),
    ("low", NLEV * P), ("up", NLEV * P), ("low64", 6 * HD), ("up64", 6 * HD), ("i64", HD), ("i32", CAP), ("iota", CAP), ("rope", T), ("keep", T),
])
BIG, NBIG = layout([
    ("cos", 2 * T), ("sin", 2 * T), ("sinq", 2 * T), ("cosq", 2 * P), ("inv", 4 * T),
])
WIN, NWIN = layout([("win", TT * 2 * HYW), ("zT", T)])


def shape_constants():
    con = np.zeros((P, NCON), np.float32)

    def put(name, a):
        o, n = CON[name]
        con[:, o:o + n] = np.asarray(a).reshape(P, n)

    i = np.arange(P)
    put("ident", np.eye(P))
    put("ones", np.ones((P, P)))
    same = (i[:, None] // HD) == (i[None, :] // HD)
    put("blk", same)
    put("causal", np.where(i[None, :] <= i[:, None], 0.0, -1e30))
    j = np.arange(HD)
    put("before", np.concatenate([j[:, None] < j[None, :]] * 2))
    put("upto", np.concatenate([j[:, None] <= j[None, :]] * 2))
    low = np.zeros((P, NLEV, P), np.float32)
    for lev in range(NLEV):
        h = 1 << lev
        low[:, lev, :] = ((i[:, None] // (2 * h)) == (i[None, :] // (2 * h))) \
            & ((i[:, None] // h) % 2 == 1) & ((i[None, :] // h) % 2 == 0)
    put("low", low)
    put("up", low.transpose(2, 1, 0))
    put("low64", np.concatenate([low[:HD, :6, :HD]] * 2))
    put("up64", np.concatenate([low.transpose(2, 1, 0)[:HD, :6, :HD]] * 2))
    put("i64", np.concatenate([np.eye(HD)] * 2))
    put("i32", np.concatenate([np.eye(CAP)] * 4))
    put("iota", np.broadcast_to(np.arange(CAP), (P, CAP)))
    inv = (np.float32(10000.0) ** (-np.arange(0, ROPE, 2, dtype=np.float32) / np.float32(ROPE))).astype(np.float32)
    ang = (np.arange(T, dtype=np.float32)[:, None] * inv[None, :]).astype(np.float64)
    rope = np.zeros((P, T))
    rope[64:96] = np.concatenate([np.cos(ang), np.cos(ang)], 1).T
    rope[96:128] = np.concatenate([-np.sin(ang), np.sin(ang)], 1).T
    put("rope", rope)
    put("keep", np.broadcast_to(np.arange(T) % CH != 0, (P, T)))

    big = np.zeros((P, NBIG), np.float32)

    def put_big(name, a):
        o, n = BIG[name]
        big[:, o:o + n] = np.asarray(a).reshape(P, n)

    t = np.arange(T)
    f = np.arange(T)
    turn = 2 * np.pi * ((t[:, None] * f[None, :]) % (2 * T)) / (2 * T)
    alt = 1.0 - 2.0 * (t % 2)
    cos, sin = np.cos(turn), np.sin(turn)
    sinq, cosq = sin.copy(), cos.copy()
    sinq[:, 0] = alt
    cosq[:, 0] = alt

    def by_tile(a):
        return a.reshape(TT, P, -1).transpose(1, 0, 2)

    put_big("cos", by_tile(cos))
    put_big("sin", by_tile(sin))
    put_big("sinq", by_tile(sinq))
    put_big("cosq", by_tile(cosq[:, :P]))
    ci, si = cos.T / T, sin.T / T
    ci[0] = 1.0 / (2 * T)
    si[0] = alt / (2 * T)
    put_big("inv", np.concatenate([ci, si]).reshape(4, P, T).transpose(1, 0, 2))

    pos = np.linspace(0.0, 1.0, T, dtype=np.float32)
    first, last = np.log(1e-2) / 1.5, np.log(1e-2) / 0.3
    deltas = np.abs(np.linspace(first, last, HYW, dtype=np.float32))
    window = np.exp(-pos[:, None].astype(np.float64) * deltas[None, :]) + 0.05
    both = np.stack([window, window], 1)
    both[0, 1, :] = 0.0
    omega = 2.0 * np.pi * t[:, None] / T
    band = np.linspace(1e-4, 15, 16, dtype=np.float32)[None, :].astype(np.float64)
    z = np.concatenate([pos[:, None], np.cos(band * omega), -np.sin(band * omega)], 1)
    win = np.zeros((P, NWIN), np.float32)
    o, n = WIN["win"]
    win[:, o:o + n] = both.reshape(TT, P, 2 * HYW).transpose(1, 0, 2).reshape(P, n)
    o, n = WIN["zT"]
    win[:33, o:o + n] = z.T
    lt = (np.arange(T)[None, :] < t[:, None]).astype(np.float32)
    lt = lt.reshape(TT, P, T).transpose(1, 0, 2).reshape(P, TT * T)
    return {"con": con, "big": big, "win": win, "earlier": lt}


def cols(a):
    a = np.asarray(a).reshape(-1)
    return a.reshape(-1, P).T


def k_major(w):
    k = w.shape[0] // P
    return w.reshape(k, P, -1).transpose(1, 0, 2).reshape(P, -1)


def slots(w):
    n = -(-w.shape[1] // SLOT)
    out = np.zeros((P, n * SLOT), np.float32)
    out[:, :w.shape[1]] = w
    return out.reshape(P, n, SLOT).transpose(1, 0, 2)


def lay_out(i):
    out = dict(shape_constants())
    vec = np.zeros((P, NVEC), np.float32)

    def put(name, a):
        o, n = VEC[name]
        a = np.asarray(a)
        vec[:a.shape[0], o:o + n] = a

    put("norm_g", cols(i["norm_g"]))
    put("final_g", cols(i["final_g"]))
    put("ada_b", np.concatenate([cols(i["ada_b"]), cols(i["ada_b_2"])], 1))
    put("q_norm", cols(i["mla_q_norm"]))
    put("kv_norm", cols(i["mla_kv_norm"]))
    put("mu", cols(i["rwkv_mu"]))
    for name, key in (("w0", "rwkv_w0"), ("a0", "rwkv_a0"), ("k_k", "rwkv_k_k"), ("k_a", "rwkv_k_a"),
                      ("r_k", "rwkv_r_k"), ("gn_w", "rwkv_gn_w"), ("gn_b", "rwkv_gn_b"),
                      ("norm1_g", "norm1_g_2"), ("conv_w", "hy_conv_w_2"), ("conv_b", "hy_conv_b_2"),
                      ("hy_norm_g", "hy_norm_g_2"), ("hg_lb", "hg_lb_2"), ("hg_norm_g", "hg_norm_g_2"),
                      ("norm2_g", "norm2_g_2"), ("final_g2", "final_g_2")):
        put(name, cols(i[key]))
    for name, key in (("pos_b1", "hy_pos_b1_2"), ("freq1", "hy_freq1_2"), ("pos_b2", "hy_pos_b2_2"),
                      ("freq2", "hy_freq2_2")):
        put(name, np.asarray(i[key]).reshape(-1, 1))
    put("rw", k_major(np.asarray(i["router_w_2"])[0]))
    out["vec"] = vec

    out["xT"] = k_major(np.asarray(i["x"])[0].T)
    out["ctxT"] = k_major(np.asarray(i["ctx_2"])[0].T)
    out["c_rows"] = np.broadcast_to(np.concatenate([np.asarray(i[k]).reshape(1, D) for k in ("c", "c_2", "c_ctx_2")], 1),
                                    (P, 3 * D))
    ada = np.concatenate([np.asarray(i["ada_w"])[0].T, np.asarray(i["ada_w"])[1].T, np.asarray(i["ada_w_2"])[0].T])
    out["ada"] = ada.reshape(-1, 2, P, D).transpose(0, 2, 1, 3).reshape(-1, P, 2 * D)

    w_in = np.asarray(i["ffn_w_in"]).reshape(NFFN, KT, P, 2, NG, FG).transpose(3, 0, 4, 2, 1, 5)
    out["ffn_gate"] = w_in[0].reshape(NFFN * NG, P, SLOT)
    out["ffn_up"] = w_in[1].reshape(NFFN * NG, P, SLOT)
    out["ffn_down"] = np.asarray(i["ffn_w_out"]).reshape(NFFN * NG, 2, P, D).transpose(0, 2, 1, 3).reshape(NFFN * NG, P, SLOT)

    w = np.asarray(i["mla_w_in"])[0]
    kr = w[:, 640:672]
    w = np.concatenate([w[:, :640], kr, kr, kr, kr[:, 16:], kr[:, :16]], 1)
    uq = np.asarray(i["mla_w_uq"])[0].reshape(384, HEADS, QK)
    uq = np.concatenate([uq, uq[:, :, 80:], uq[:, :, 64:80]], 2).reshape(384, HEADS * P)
    ukv = np.asarray(i["mla_w_ukv"])[0].reshape(256, HEADS, P)
    ukv = np.concatenate([ukv[:, :, :NOPE].reshape(256, D), ukv[:, :, NOPE:].reshape(256, D)], 1)
    mla = [slots(k_major(w)), slots(k_major(uq)), slots(k_major(ukv)), slots(k_major(np.asarray(i["mla_w_out"])[0]))]

    low = np.zeros((4, P, SLOT), np.float32)
    dw = np.concatenate([np.asarray(i["rwkv_wd1"])[0], np.asarray(i["rwkv_wa1"])[0]], 1)
    low[0, :, :D] = k_major(dw)
    low[0, :64, D:] = np.asarray(i["rwkv_wd2"])[0]
    low[1, :, :KT * 160] = k_major(np.asarray(i["rwkv_wg1"])[0])
    low[2, :64, :D] = np.asarray(i["rwkv_wa2"])[0]
    low[2, :, D:] = np.asarray(i["rwkv_wg2"])[0][:P]
    low[3, :32, :D] = np.asarray(i["rwkv_wg2"])[0][P:]
    rwkv = [low] + [slots(k_major(np.asarray(i["rwkv_w_rkv"])[0, n])) for n in (1, 0, 2)] \
        + [slots(k_major(np.asarray(i["rwkv_w_out"])[0]))]

    w = np.asarray(i["w_in_2"])[0].reshape(KT, P, 16, 256).transpose(2, 1, 0, 3).reshape(16, P, SLOT)
    out["ring_w"] = np.concatenate(mla + rwkv + [w, slots(k_major(np.asarray(i["w_out_2"])[0]))])
    out["w1"] = np.asarray(i["exp_w1_2"])[0].reshape(NE * KT, P, EFF)
    out["w3"] = np.asarray(i["exp_w3_2"])[0].reshape(NE * KT, P, EFF)
    out["w2"] = np.asarray(i["exp_w2_2"])[0].reshape(NE * 8, 2, P, D)
    pos = np.zeros((P, P + HYW * 4), np.float32)
    pos[:33, :64] = np.asarray(i["hy_pos_w1_2"])[0]
    pos[:64, 64:128] = np.asarray(i["hy_pos_w2_2"])[0]
    pos[:64, 128:] = np.asarray(i["hy_pos_w3_2"])[0]
    out["pos_w"] = pos
    out["hy_bias"] = np.broadcast_to(np.asarray(i["hy_bias_2"]).reshape(1, 2 * HYW), (P, 2 * HYW))
    return out


def build(nc, a, out):
    with ExitStack() as ctx:
        def sb(name, n, dt=F32):
            return ctx.enter_context(nc.sbuf_tensor(name, [P, n], dt))

        sems = {}

        def sem(name):
            if name not in sems:
                sems[name] = ctx.enter_context(nc.semaphore(name))
            return sems[name]

        ring = sb("ring", NRING * SLOT)
        xT = sb("xT", KT * T)
        hT = sb("hT", KT * T)
        sq = sb("sq", KT * T)
        vec = sb("vec", NVEC)
        con = sb("con", NCON)
        mods = sb("mods", N_MODS)
        cmods = sb("cmods", 16)
        dots = sb("dots", 16)
        coef = sb("coef", 64)
        rstd = sb("rstd", T)
        sil = sb("sil", 2 * T)
        hid = sb("hid", 2 * T)
        small = sb("small", 256)
        zeros = sb("zeros", 512, BF16)
        ARENA = 32368
        arena = sb("arena", ARENA)
        FFN0 = ARENA - 3 * SLOT
        ADA0 = FFN0 - NADA * SLOT - 3 * D
        gate_w, up_w, down_w = (arena[:, FFN0 + i * SLOT:FFN0 + (i + 1) * SLOT] for i in range(3))
        c_rows = arena[:, FFN0 - 3 * D:FFN0]
        ps = ctx.enter_context(nc.psum_tensor("ps", [P, 8, 512], F32))

        def v(name, i=0, n=1):
            o, _ = VEC[name]
            return vec[:, o + i:o + i + n]

        def k(name, i=0, n=None):
            o, m = CON[name]
            return con[:, o + i:o + i + (m if n is None else n)]

        def ar(off, n):
            assert off + n <= ARENA, (off, n)
            return arena[:, off:off + n]

        def tiles(ap, b=T):
            return ap.rearrange("p (a b) -> p a b", b=b)

        x3, h3, sq3 = (tiles(t[:, :]) for t in (xT, hT, sq))
        gate3, up3 = tiles(gate_w[:, :], FG), tiles(up_w[:, :], FG)
        down3 = tiles(down_w[:, :], D)
        sil3, hid3 = tiles(sil[:, :]), tiles(hid[:, :])
        ident, ones, blk = k("ident"), k("ones"), k("blk")

        def slot(seq):
            s = seq % NRING
            return ring[:, s * SLOT:(s + 1) * SLOT]

        def ada_slot(j):
            return tiles(ar(ADA0 + j * SLOT, SLOT), D)

        def acc(m):
            return ps[:, 2 + m // 2, (m % 2) * T:(m % 2 + 1) * T]

        def half(bank, m):
            return ps[:, bank + m // 2, (m % 2) * T:(m % 2 + 1) * T]

        def norm_sums(i):
            return ps[:, 0 if i == 10 else 7, 0:T]

        def bc(ap, n):
            return ap.unsqueeze(2).to_broadcast([ap.shape[0], ap.shape[1], n])

        def bcm(ap, n):
            return ap.unsqueeze(1).to_broadcast([ap.shape[0], n, ap.shape[1]])

        m_c = tiles(ar(0, 6 * T))
        m_q = tiles(ar(1536, HEADS * T))
        m_k = tiles(ar(5632, HEADS * T))
        m_v = tiles(ar(9728, TT * D), D)
        m_p0 = tiles(ar(11776, 4 * P), P), tiles(ar(0, 4 * P), P)
        m_p1 = tiles(ar(12288, 4 * T)), tiles(ar(4 * P, 4 * T))
        m_t0 = tiles(ar(13312, 4 * T))
        m_t1 = tiles(ar(14336, 4 * P), P)
        m_rope = hid3
        m_st = small[:, 0:64]
        m_o = h3

        r_x = tiles(ar(0, 2048))
        r_g = tiles(ar(2048, 2048))
        r_b = tiles(ar(4096, 2048))
        r_r, r_k, r_v, r_a = (tiles(ar(6144 + 2048 * n, 2048)) for n in range(4))
        r_w = tiles(ar(14336, 2048))
        r_o = tiles(ar(16384, 2048))
        c_room = [ar(18432 + 512 * n, 512) for n in range(27)] \
            + [buf[:, 512 * n:512 * (n + 1)] for buf in (ar(2048, 2048), hT, sq) for n in range(4)] + [hid[:, :]]
        c_room = [tiles(buf, HD) for buf in c_room]
        c_ab, c_ak, c_rb, c_rk, c_vs, c_bt, c_kt, c_y, c_t, c_tt = (
            [c_room[(27 + 4 * n + c) % 40] for c in range(NCH)]
            for n in range(10))
        c_s = tiles(sil[:, :], HD)
        r_dec = small[:, 0:KT * NCH].rearrange("p (a b) -> p a b", b=NCH)
        r_e1, r_e2, r_e3 = (tiles(ar(18432 + 2048 * n, 2048)) for n in range(3))
        r_t = tiles(ar(24576, 2048))
        c_st = [small[:, 32 + 16 * c:48 + 16 * c] for c in range(NCH)]
        c_first = (("ab", r_a, r_x), ("m", r_x, r_a), ("vs", r_v, None), ("ak", r_k, r_x), ("bt", r_a, None), ("rb", r_a, r_r),
                   ("kt", r_k, None), ("rk", r_k, r_r))

        f_A = [tiles(ar(0 + 2560 * o, 1024), HYW) for o in range(2)]
        f_B = [tiles(ar(1024 + 2560 * o, 1024), HYW) for o in range(2)]
        f_D = [ar(2048 + 2560 * o, 512) for o in range(2)]
        big = ar(5120, NBIG)
        B0 = 5120 + NBIG
        hy_p = tiles(ar(B0, 3072))
        B1 = B0 + 3072
        f_win = ar(B1, NWIN)
        f_h = ar(B1 + NWIN, 4096).rearrange("p (t s c) -> p t s c", t=TT, c=HYW)
        f_pos = ar(B1 + NWIN + 4096, P + 2048)
        f_abs = sq[:, :], f_pos[:, 0:2048]
        f_rn = tiles(ar(B1 + NWIN + 8832, 1024), HYW)
        f_sum = tiles(f_pos[:, 0:1024], HYW)
        f_dif = tiles(f_pos[:, 1024:2048], HYW)
        f_in = f_rn
        f_bias = tiles(ar(B1 + NWIN + 9856, 1024), HYW)

        def bigt(name, n):
            o, m = BIG[name]
            return big[:, o:o + m].rearrange("p (a b) -> p a b", b=n)

        g_q = tiles(ar(B1, 1024))
        g_g = tiles(ar(B1 + 1024, 1024))
        g_f = ar(B1 + 2048, 2048).rearrange("p (d h t) -> p d h t", d=2, t=T)
        g_k = ar(B1 + 4096, 2048).rearrange("p (d h t) -> p d h t", d=2, t=T)
        g_F = ar(B1 + 6144, 2048).rearrange("p (d h t) -> p d h t", d=2, t=T)
        g_E = ar(B1 + 8192, 2048).rearrange("p (d h t) -> p d h t", d=2, t=T)
        g_Q = ar(B1 + 10240, 2048).rearrange("p (d h t) -> p d h t", d=2, t=T)
        g_K = ar(B1 + 12288, 2048).rearrange("p (d h t) -> p d h t", d=2, t=T)
        g_v = tiles(ar(B1 + 14336, 1024), HYW)
        g_A = ar(B1 + 15360, 2048).rearrange("p (d t h s) -> p d t h s", d=2, t=TT, s=P)
        g_X = ar(B1 + 17408, 1024).rearrange("p (d h s) -> p d h s", d=2, s=P)
        g_S = sil[:, :].rearrange("p (h s) -> p h s", s=P), hid[:, :].rearrange("p (h s) -> p h s", s=P)
        x_f, x_k, x_E = g_F, g_E, g_Q
        x_kt = ar(B1 + 12288, 2048).rearrange("p (d t c) -> p d t c", d=2, t=TT)
        x_v = tiles(ar(B1 + 15360, 1024), HYW)
        ctx3 = tiles(ar(B1 + 6144, 2048))
        hc3 = tiles(ar(B1 + 17408, 2048))
        mix3 = h3

        y_c = tiles(ar(B1 + 8192, 3072))
        y_t = ar(B1 + 11264, 3072).rearrange("p (t c) -> p t c", t=TT)
        y_cc = tiles(ar(B1 + 4096, 1024), HYW)
        y_ss = tiles(ar(B1 + 5120, 1024), HYW)
        y_z = y_m = tiles(ar(B1 + 16384, 1024), HYW)
        HY_CONV, HY_TURN, HY_FORWARD, HY_INVERSE, HY_NORM = 6, 10, (11, 14), (13, 16), 17

        e_h = tiles(ar(0, TT * D), D)
        e_aff = ar(2048, TT * NE).rearrange("p (t e) -> p t e", t=TT)
        e_rank = ar(2080, TT * NE).rearrange("p (t e) -> p t e", t=TT)
        e_tie = ar(2112, TT * NE).rearrange("p (t e) -> p t e", t=TT)
        e_row = ar(2144, T)
        e_st = ar(2400, 16)
        e_cmp = tiles(ar(8432, 8 * T))
        e_early = tiles(ar(2672, TT * T))
        e_sel = ar(3184, TT * NE * CAP).rearrange("p (t e c) -> p t e c", t=TT, c=CAP)
        e_rep = ar(4208, P)
        e_diag = tiles(ar(4336, TT * NE * P), P)
        e_back = tiles(ar(8432, NE * T))
        e_x = tiles(ar(12528, KT * NE * CAP), NE * CAP)
        e_four = [ar(off, TT * NE // 2 * P).rearrange("p (t e r c) -> p t e r c", t=TT, e=NE // 2, c=CAP) for off in (10480, 0)]
        e_xe = tiles(ar(16624, KT * CAP), CAP)
        e_s = ar(20976, 512)
        e_h2 = ar(21488, 512)
        e_hT = tiles(ar(22000, 512), P)
        e_y = ar(22512, 512)
        e_bk = ar(23024, T)
        E_FIRST, E_SECOND = 4, 10
        o_row = e_h

        def first_tokens(kt):
            return ps[:, kt // 4, (kt % 4) * E_FIRST * CAP:(kt % 4 + 1) * E_FIRST * CAP]

        def e_slot(j):
            j %= E_RING
            if j < NRING:
                return slot(SEQ_MOE + j)
            return (ar(16880, SLOT), ar(16880 + SLOT, SLOT), *(ar(ARENA - n * SLOT, SLOT) for n in (4, 3, 2, 1)),
                    hT[:, :], sq[:, :])[j - NRING]

        CTX_AT = 4
        FILTER_AT, FILTER_STEPS = 3, 7
        assert FILTER_AT + FILTER_STEPS == NG - 1

        block = ctx.enter_context(nc.Block())

        def slot_done(seq):
            if seq < 3:
                return "mla_in", 6
            if seq < 6:
                return "mla_q", 8
            if seq < 8:
                return "mla_kv", 8
            if seq < SEQ_RWKV:
                return "proj_slot", seq - 8 + 1
            if seq < 16:
                return (("rwkv_low2", 1), ("rwkv_low1", 3), ("rwkv_low2", 3), ("rwkv_low2", 3))[seq - SEQ_RWKV]
            if seq < 28:
                return "rkv_slot", seq - 16 + 1
            if seq < SEQ_B2:
                return "proj_slot", 4 + seq - 28 + 1
            if seq < 48:
                return "b2_unit", B2_LAST[seq - SEQ_B2] + 1
            return "proj_slot", 8 + seq - 48 + 1

        B2_UNITS = []
        for s in range(16):
            what = "hy" if s < 6 else ("q", "i", "zf", "zb", "g")[(s - 6) // 2]
            B2_UNITS.append((s, what, False))
            if what in ("i", "zf", "zb"):
                B2_UNITS.append((s, what, True))
        B2_LAST = [max(u for u, unit in enumerate(B2_UNITS) if unit[0] == s) for s in range(16)]

        @block.sync
        def _(sp):
            head = 2 * P

            def start():
                for dst, src in ((xT[:, :], a["xT"]), (vec[:, :], a["vec"]), (con[:, 0:head], a["con"][:, 0:head])):
                    sp.dma_start(dst, src).then_inc(sem("start_landed"), 16)

            def tables():
                sp.dma_start(con[:, head:], a["con"][:, head:]).then_inc(sem("tables_landed"), 16)
                sp.dma_start(c_rows[:, D:], a["c_rows"][:, D:]).then_inc(sem("tables_landed"), 16)

            def ada_round(r, wait):
                for j in range(NADA):
                    if wait:
                        sp.wait_ge(sem("ada_used"), 4 * r - 3 + j)
                    sp.dma_start(ada_slot(j).rearrange("p a b -> p (a b)"), a["ada"][4 * r + j, :, :]) \
                        .then_inc(sem(f"ada_landed{j}"), 16)

            def ffn_group(t):
                sp.wait_ge(sem("gate_used"), t + 1)
                sp.dma_start(gate_w[:, :], a["ffn_gate"][t, :, :]).then_inc(sem("gate_landed"), 16)
                sp.wait_ge(sem("gate_up_ready"), 2 * t + 1)
                sp.dma_start(up_w[:, :], a["ffn_up"][t, :, :]).then_inc(sem("up_landed"), 16)
                sp.wait_ge(sem("down_used"), t + 1)
                sp.dma_start(down_w[:, :], a["ffn_down"][t, :, :]).then_inc(sem("down_landed"), 16)

            def ffn(n, lo=0, hi=NG):
                with sp.Fori(lo + NG * n, hi + NG * n) as t:
                    ffn_group(t)
                    if n < 2:
                        ada_round(t + ADA_FIRST, True)

            def load(seq):
                if seq >= NRING:
                    name, n = slot_done(seq - NRING)
                    sp.wait_ge(sem(name), n)
                sp.dma_start(slot(seq), a["ring_w"][seq, :, :]).then_inc(sem(f"ring_landed{seq % NRING}"), 16)

            def expert_load(e, j):
                dst = e_slot(j)
                if j < 8:
                    d = sp.dma_start(dst, a["w1"][8 * e + j, :, :])
                elif j < 16:
                    d = sp.dma_start(dst, a["w3"][8 * e + (j - 8), :, :])
                else:
                    d = sp.dma_start(tiles(dst, D), a["w2"][8 * e + (j - 16), :, :, :].rearrange("t p n -> p t n"))
                d.then_inc(sem(f"ring_landed{j % E_RING}"), 16)

            sp.dma_start(c_rows[:, 0:D], a["c_rows"][:, 0:D]).then_inc(sem("c_landed"), 16)
            for r in range(ADA_FIRST):
                ada_round(r, r > 0)
                if r == 0:
                    start()
            ffn(0)
            tables()
            for seq in range(SEQ_MLA, SEQ_RWKV):
                load(seq)
            ffn(1)
            ffn(2)
            for seq in range(SEQ_RWKV, SEQ_B2):
                load(seq)
            sp.wait_ge(sem("rwkv_y"), KT)
            ffn(3, 0, 2)
            sp.wait_ge(sem("x_ready"), 5 * KT)
            for dst, name in ((big, "big"), (f_win, "win"), (f_pos, "pos_w"), (f_bias.rearrange("p a b -> p (a b)"), "hy_bias")):
                sp.dma_start(dst, a[name]).then_inc(sem("filter_landed"), 16)
            ffn(3, 2)
            for seq in range(SEQ_B2, SEQ_B2 + NRING):
                load(seq)
            sp.wait_ge(sem("filter_done"), 2)
            sp.dma_start(ctx3.rearrange("p a b -> p (a b)"), a["ctxT"]).then_inc(sem("ctx_landed"), 16)
            for seq in range(SEQ_B2 + NRING, SEQ_MOE):
                load(seq)
            sp.wait_ge(sem("hg_mixed"), 1)
            for j in range(NRING, E_RING - 2):
                expert_load(0, j)
            for j in range(NRING):
                sp.wait_ge(sem("proj_slot"), 8 + j + 1)
                expert_load(0, j)
            sp.wait_ge(sem("x_ready"), 8 * KT)
            sp.dma_start(e_early.rearrange("p a b -> p (a b)"), a["earlier"]).then_inc(sem("early_landed"), 16)
            sp.wait_ge(sem("e_turned"), 2)
            for j in range(E_RING - 2, E_RING):
                expert_load(0, j)
            with sp.Fori(0, NE - 1) as e:
                for j in range(E_RING, PER_EXPERT):
                    sp.wait_ge(sem("moe_slot"), PER_EXPERT * e + (j - E_RING + 1))
                    expert_load(e, j)
                for j in range(E_RING):
                    sp.wait_ge(sem("moe_slot"), PER_EXPERT * e + (PER_EXPERT - E_RING + j + 1))
                    expert_load(e + 1, j)
            for j in range(E_RING, PER_EXPERT):
                sp.wait_ge(sem("moe_slot"), PER_EXPERT * (NE - 1) + j - E_RING + 1)
                expert_load(NE - 1, j)
            sp.wait_ge(sem("row_ready"), 1)
            sp.dma_start(out.rearrange("(t p) n -> p t n", p=P), o_row).then_inc(sem("out_stored"), 16)
            sp.wait_ge(sem("out_stored"), 16)

        @block.tensor
        def _(pe):
            mm, tr = nc.tensor.matmul, nc.tensor.transpose

            def landed(seq):
                pe.wait_ge(sem(f"ring_landed{seq % NRING}"), 16 * (seq // NRING + 1))

            def norm(i):
                for kt in range(KT):
                    pe.wait_ge(sem("squares"), 4 * i + kt // 2 + 1)
                    last = mm(norm_sums(i), ones, sq3[:, kt, :], start=kt == 0, stop=kt == KT - 1)
                last.then_inc(sem("norm_sum"), 1)

            def h_part(i, kt):
                pe.wait_ge(sem("h_ready"), KT * (i - 1) + kt + 1)

            def open_banks(b0, signals=()):
                for b in range(4):
                    mm_ = mm(ps[:, b0 + b, :], zeros[:, 0:P], zeros[:, :], start=True, stop=False, skip_group_check=True)
                    if b < len(signals):
                        mm_.then_inc(sem(signals[b]), 1)

            def ffn(n, ready):
                if n > 0:
                    h_part(ready, 0)
                    open_banks(2)

                def group(t, final=False):
                    for ft in range(2):
                        if ft == 0:
                            pe.wait_ge(sem("gate_landed"), 16 * t + 16)
                        for kt in range(KT):
                            if ft == 0:
                                h_part(ready, kt)
                            last = mm(ps[:, ft, 0:T], gate3[:, kt, ft * P:(ft + 1) * P], h3[:, kt, :],
                                      start=kt == 0, stop=kt == KT - 1)
                        if ft == 1:
                            last.then_inc(sem("gate_used"), 1)
                        else:
                            pe.wait_ge(sem("up_landed"), 16 * t + 16)
                        for kt in range(KT):
                            last = mm(ps[:, ft, T:2 * T], up3[:, kt, ft * P:(ft + 1) * P], h3[:, kt, :],
                                      start=kt == 0, stop=kt == KT - 1)
                        last.then_inc(sem("gate_up_ready"), 1)
                    pe.wait_ge(sem("down_landed"), 16 * t + 16)
                    for ft in range(2):
                        pe.wait_ge(sem("hid_ready"), 2 * t + ft + 1)
                        for m in range(KT):
                            last = mm(acc(m), down3[:, ft, m * P:(m + 1) * P], hid3[:, ft, :],
                                      start=False, stop=True, skip_group_check=True)
                            if final and ft == 1 and m in (1, 3, 5):
                                last.then_inc(sem("out_part"), 1)
                    last.then_inc(sem("down_used"), 1)

                t0 = NG * n
                if n < 3:
                    with pe.Fori(t0, t0 + NG - 1) as t:
                        group(t)
                else:
                    with pe.Fori(t0, t0 + FILTER_AT) as t:
                        group(t)
                    for i in range(FILTER_STEPS):
                        filter_step(i)
                        group(t0 + FILTER_AT + i)
                group(t0 + NG - 1, final=True)

            def k_outer(out_of, seq0, rhs3, done, kts=range(KT), ready=None):
                for kt in kts:
                    if ready:
                        pe.wait_ge(sem(ready), kt + 1)
                    if kt % 2 == 0:
                        landed(seq0 + kt // 2)
                    for m in range(KT):
                        last = mm(out_of(m), slot(seq0 + kt // 2)[:, (kt % 2) * D + m * P:(kt % 2) * D + (m + 1) * P],
                                  rhs3[:, kt, :], start=(kt == 0 and m % 2 == 0), stop=kt == KT - 1,
                                  skip_group_check=True)
                        if done == "proj_slot" and kt == KT - 1 and m in (1, 3, 5):
                            last.then_inc(sem("out_part"), 1)
                    if kt % 2 == 1:
                        last.then_inc(sem(done), 1)

            def mla():
                for s in range(3):
                    landed(s)
                for m in range(6):
                    for kt in range(KT):
                        if m == 0:
                            h_part(2, kt)
                        last = mm(half(0, m), ring[:, kt * 768 + m * P:kt * 768 + (m + 1) * P], h3[:, kt, :],
                                  start=kt == 0, stop=kt == KT - 1)
                    last.then_inc(sem("mla_in"), 1)
                pe.wait_ge(sem("mla_c"), 4)
                for o, k0, k1 in ((0, 0, 3), (T, 3, 5)):
                    for kt in range(k0, k1):
                        last = mm(ps[:, 3, o:o + T], ones, sq3[:, kt, :], start=kt == k0, stop=kt == k1 - 1)
                last.then_inc(sem("mla_in"), 1)
                pe.wait_ge(sem("mla_normed"), 1)
                for s in range(3, 6):
                    landed(s)
                for h in range(HEADS):
                    for kt in range(3):
                        last = mm(half(0, h), slot(3 + kt)[:, h * P:(h + 1) * P], m_c[:, kt, :],
                                  start=kt == 0, stop=kt == 2)
                    if h % 2:
                        last.then_inc(sem("mla_q"), 1)
                for s in (6, 7):
                    landed(s)
                def queries_out(bank):
                    pe.wait_ge(sem("mla_q_nope"), bank + 1)
                    pe.wait_ge(sem("mla_q_rope"), bank + 1)

                pe.wait_ge(sem("mla_normed"), 2)
                for i in range(8):
                    if i % 2 == 0:
                        queries_out(i // 2)
                    for kt in range(2):
                        last = mm(half(0, i), slot(6 + kt)[:, i * P:(i + 1) * P], m_c[:, 3 + kt, :],
                                  start=kt == 0, stop=kt == 1)
                    if i % 2:
                        last.then_inc(sem("mla_kv"), 1)
                for i in range(4):
                    tt, hb = i // 2, i % 2
                    queries_out(4 + i)
                    for kt in range(2):
                        last = mm(ps[:, 4 + i, :], m_c[:, 3 + kt, tt * P:(tt + 1) * P],
                                  slot(6 + kt)[:, D + hb * 512:D + (hb + 1) * 512], start=kt == 0, stop=kt == 1)
                    last.then_inc(sem("mla_kv"), 1)

                def scores(b):
                    s = 3 * (b % 2)
                    if b == 0:
                        pe.wait_ge(sem("mla_k_nope"), 8)
                        pe.wait_ge(sem("mla_k_rope"), 1)
                        pe.wait_ge(sem("mla_v"), 4)
                    if b >= 2:
                        pe.wait_ge(sem("mla_o"), b - 1)
                    for hh in range(4):
                        h = 4 * b + hh
                        mm(ps[:, s, hh * P:(hh + 1) * P], m_q[0:QK, h, 0:P], m_k[0:QK, h, 0:P], start=True, stop=True)
                        last = mm(half(s + 1, hh), m_q[0:QK, h, P:T], m_k[0:QK, h, :], start=True, stop=True)
                    last.then_inc(sem("mla_scores"), 1)

                def turn(b):
                    s = 3 * (b % 2)
                    p0, p1 = m_p0[b % 2], m_p1[b % 2]
                    pe.wait_ge(sem("mla_probs"), b + 1)
                    if b >= 1:
                        pe.wait_ge(sem("mla_t0"), b)
                    for hh in range(4):
                        o = (hh % 2) * T
                        tr(ps[:, 6 + hh // 2, o:o + P], p0[:, hh, :], ident)
                        tr(ps[:, 6 + hh // 2, o + P:o + T], p1[:, hh, 0:P], ident)
                        last = tr(ps[:, s, hh * P:(hh + 1) * P], p1[:, hh, P:T], ident)
                    last.then_inc(sem("mla_turned"), 1)

                def values(b):
                    s = 3 * (b % 2)
                    pe.wait_ge(sem("mla_t0"), b + 1)
                    pe.wait_ge(sem("mla_t1"), b + 1)
                    for hh in range(4):
                        h, r, o = 4 * b + hh, 64 * (hh % 2), (hh // 2) * T
                        mm(ps[r:r + 64, s + 1, o:o + T], m_v[:, 0, h * 64:h * 64 + 64], m_t0[:, hh, :],
                           start=True, stop=False, skip_group_check=True)
                        last = mm(ps[r:r + 64, s + 1, o + P:o + T], m_v[:, 1, h * 64:h * 64 + 64], m_t1[:, hh, :],
                                  start=False, stop=True, skip_group_check=True)
                    last.then_inc(sem("mla_pv"), 1)

                scores(0)
                scores(1)
                for b in (0, 2):
                    turn(b)
                    values(b)
                    turn(b + 1)
                    if b == 0:
                        scores(2)
                    values(b + 1)
                    if b == 0:
                        scores(3)
                pe.wait_ge(sem("mla_o"), 4)
                k_outer(acc, 8, m_o, "proj_slot")

            def heads(bank, lhs, rhs, start=True, stop=True):
                for kt in range(KT):
                    for r in (slice(0, 64), slice(64, 128)):
                        last = mm(ps[r, bank, kt * HD:(kt + 1) * HD], lhs[r, kt, :], rhs[r, :] if len(rhs.shape) == 2 else rhs[r, kt, :],
                                  start=start and (stop or kt == 0), stop=stop, skip_group_check=True)
                return last

            def blocks(bank, lhs, rhs, to=None):
                for kt in range(KT):
                    for q in range(4) if to is None else (0, 2):
                        r, i, j, o = (q, q % 2, q % 2, q) if to is None else (q, 1, 0, q + 1) if to == "below" else (q + 1, 0, 1, q)
                        r, o = slice(32 * r, 32 * r + 32), slice(32 * o, 32 * o + 32)
                        last = mm(ps[o, bank, kt * HD + 32 * j:kt * HD + 32 * j + 32], lhs[r, kt, 32 * i:32 * i + 32],
                                  rhs[r, kt, 32 * j:32 * j + 32], start=True, stop=True, skip_group_check=True)
                return last

            def rwkv():
                pe.wait_ge(sem("rwkv_mix"), 1)
                landed(12)
                for n, (buf, o) in enumerate(((r_g, 0), (r_b, 64))):
                    pe.wait_ge(sem("rwkv_mix"), n + 1)
                    for kt in range(KT):
                        last = mm(ps[0:64, 6 - n, 0:T], slot(12)[:, kt * P + o:kt * P + o + 64], buf[:, kt, :],
                                  start=kt == 0, stop=kt == KT - 1)
                    last.then_inc(sem("rwkv_low1"), 1)
                pe.wait_ge(sem("rwkv_mix"), 3)
                landed(13)
                for o, w in ((0, P), (P, 32)):
                    for kt in range(KT):
                        last = mm(ps[0:w, 7, 2 * o:2 * o + T], slot(13)[:, kt * 160 + o:kt * 160 + o + w], r_g[:, kt, :],
                                  start=kt == 0, stop=kt == KT - 1)
                last.then_inc(sem("rwkv_low1"), 1)
                pe.wait_ge(sem("rwkv_low"), 1)
                for m in range(KT):
                    last = mm(half(0, m), slot(12)[0:64, D + m * P:D + (m + 1) * P], hid3[0:64, 0, :], start=True, stop=True)
                last.then_inc(sem("rwkv_low2"), 1)
                landed(14)
                pe.wait_ge(sem("rwkv_low"), 3)
                for m in range(KT):
                    last = mm(half(4, m), slot(14)[0:64, m * P:(m + 1) * P], hid3[0:64, 1, :], start=True, stop=True)
                last.then_inc(sem("rwkv_low2"), 1)
                landed(15)
                pe.wait_ge(sem("rwkv_sig"), 1)
                for m in range(KT):
                    mm(half(0, m), slot(14)[:, D + m * P:D + (m + 1) * P], sil3[:, 0, :], start=True, stop=False)
                    last = mm(half(0, m), slot(15)[:, m * P:(m + 1) * P], sil3[:, 1, :], start=False, stop=True)
                last.then_inc(sem("rwkv_low2"), 1)
                pe.wait_ge(sem("rwkv_mix"), 4)
                pe.wait_ge(sem("rwkv_sig"), 2)
                k_outer(lambda m: half(4, m), 16, r_b, "rkv_slot")
                pe.wait_ge(sem("rwkv_sig"), 3)
                pe.wait_ge(sem("rwkv_mix"), 5)
                k_outer(lambda m: half(0, m), 20, r_g, "rkv_slot")
                pe.wait_ge(sem("rwkv_kk2"), 1)
                for b in range(4):
                    last = mm(ps[:, 4 + b, :], blk, sq[:, b * 512:(b + 1) * 512], start=True, stop=True)
                last.then_inc(sem("rwkv_sums"), 1)
                pe.wait_ge(sem("rwkv_rkv"), 2)
                pe.wait_ge(sem("rwkv_mix"), 6)
                k_outer(lambda m: half(0, m), 24, r_b, "rkv_slot")
                pe.wait_ge(sem("rwkv_prod"), 1)
                for b in range(4):
                    last = mm(ps[:, 4 + b, :], blk, r_t[:, 2 * b:2 * b + 2, :].rearrange("p a b -> p (a b)"),
                              start=True, stop=True)
                last.then_inc(sem("rwkv_sums"), 1)
                pe.wait_ge(sem("rwkv_prep"), 1)
                pe.wait_ge(sem("rwkv_rkv"), 3)
                for p, (name, left, right) in enumerate(c_first):
                    for c in range(NCH):
                        cut = slice(c * CH, (c + 1) * CH)
                        if p == 1:
                            pe.wait_ge(sem("rwkv_prep"), 2)
                        if p >= 2:
                            n = {2: 0, 3: 1, 5: 2, 7: 3}.get(p)
                            if n is None:
                                pe.wait_ge(sem("rw_first_a"), 4 * (0 if p == 4 else 1) + c + 1)
                            else:
                                pe.wait_ge(sem("rw_first_d"), 4 * n + c + 1)
                        heads((4 * p + c) % 8, left[:, :, cut], k("i64") if right is None else right[:, :, cut]) \
                            .then_inc(sem("rw_first"), 1)
                for lev in range(1, 6):
                    n = 4 * (lev - 1)
                    for c in range(NCH):
                        pe.wait_ge(sem("rw_T"), n + c + 1)
                        if lev == 1:
                            pe.wait_ge(sem("rw_first_a"), 9 + c)
                        blocks(c, c_ab[c], c_t[c], "below" if lev == 5 else None).then_inc(sem("rw_Y"), 1)
                    for c in range(NCH):
                        pe.wait_ge(sem("rw_Ys"), n + c + 1)
                        if lev == 1:
                            pe.wait_ge(sem("rw_first_d"), 17 + c)
                        if lev < 5:
                            blocks(c, c_tt[c], c_y[c])
                        blocks(4 + c, c_y[c], c_tt[c], "above" if lev == 5 else None).then_inc(sem("rw_Z"), 1)
                pe.wait_ge(sem("rw_T"), 6 * NCH)
                for c in range(NCH + 1):
                    cut = slice(c * CH, (c + 1) * CH)
                    if c < NCH:
                        o = 2 + c % 2
                        heads(0, c_ak[c], c_vs[c], stop=c == 0)
                        if c >= 2:
                            pe.wait_ge(sem("rw_yb"), c - 1)
                        last = heads(o, c_rk[c], c_vs[c], stop=False)
                        if c > 0:
                            pe.wait_ge(sem("rw_S"), c)
                            last = heads(0, r_x[:, :, cut], c_s, start=False)
                        last.then_inc(sem("rw_rhs"), 1)
                        if c < NCH - 1:
                            heads(4, c_kt[c], c_vs[c], stop=False)
                        if c > 0:
                            heads(o, r_r[:, :, cut], c_s, start=False, stop=False)
                        pe.wait_ge(sem("rw_rhs_s"), c + 1)
                        heads(1, c_tt[c], c_y[c]).then_inc(sem("rw_u"), 1)
                        pe.wait_ge(sem("rw_u_s"), c + 1)
                        if c < NCH - 1:
                            heads(4, c_bt[c], c_t[c], start=False).then_inc(sem("rw_ds"), 1)
                        heads(o, c_rb[c], c_t[c], start=False).then_inc(sem("rw_o"), 1)
                    if c > 0:
                        pe.wait_ge(sem("rw_yb"), c)
                        if c >= 3:
                            pe.wait_ge(sem("rw_y"), c - 2)
                        heads(5 + (c - 1) % 2, c_ab[c - 1], k("i64")).then_inc(sem("rw_out"), 1)
                k_outer(acc, 28, r_w, "proj_slot", ready="rwkv_y")

            def filter_step(i):
                if i == 0:
                    pe.wait_ge(sem("filter_landed"), 64)
                    zT = f_win[0:33, WIN["zT"][0]:WIN["zT"][0] + T]
                    mm(ps[0:64, 6, 0:T], f_pos[0:33, 0:64], zT, start=True, stop=True).then_inc(sem("filter_mm"), 1)
                elif i == 1:
                    pe.wait_ge(sem("filter_sin"), 1)
                    mm(ps[0:64, 7, 0:T], f_pos[0:64, 64:128], f_in[0:64, 0, 0:T], start=True, stop=True) \
                        .then_inc(sem("filter_mm"), 1)
                elif i < 6:
                    tt, q0 = (i - 2) // 2, 2 * ((i - 2) % 2)
                    if i == 2:
                        pe.wait_ge(sem("filter_sin"), 2)
                    else:
                        pe.wait_ge(sem("filter_h"), 2 * (i - 2))
                    for q in (q0, q0 + 1):
                        mm(ps[:, 6 + q % 2, :], f_in[0:64, 0, tt * P:(tt + 1) * P],
                           f_pos[0:64, P + q * HYW:P + (q + 1) * HYW], start=True, stop=True).then_inc(sem("filter_mm"), 1)
                else:
                    for o in range(2):
                        pe.wait_ge(sem("filter_abs"), o + 1)
                        for m in range(4):
                            last = mm(ps[:, 6 + o, :], ones, f_abs[o][:, m * HYW:(m + 1) * HYW], start=m == 0, stop=m == 3)
                        last.then_inc(sem("filter_l1"), 1)

            def filter_freq(o):
                cos, sin, cosq = bigt("cos", T), bigt("sin", T), bigt("cosq", P)
                pe.wait_ge(sem("filter_sides"), o + 1)
                if o == 0:
                    pe.wait_ge(sem("x_ready"), 6 * KT)
                else:
                    pe.wait_ge(sem("filter_done"), 1)
                for ft in range(2):
                    for tt in range(TT):
                        mm(ps[:, 2 + ft, :], cos[:, tt, ft * P:(ft + 1) * P], f_sum[:, tt, :], start=tt == 0, stop=tt == 1)
                    for tt in range(TT):
                        mm(ps[:, 4 + ft, :], sin[:, tt, ft * P:(ft + 1) * P], f_dif[:, tt, :], start=tt == 0, stop=tt == 1)
                for tt in range(TT):
                    last = mm(ps[:, 6, :], cosq[:, tt, :], f_sum[:, tt, :], start=tt == 0, stop=tt == 1)
                last.then_inc(sem("filter_freq"), 1)

            def b2_in():
                h_part(7, KT - 1)
                for u, (s, what, context) in enumerate(B2_UNITS):
                    if u == CTX_AT:
                        norm(8)
                    if u == HY_TURN:
                        hyena_turn()
                    for o in range(2):
                        if u == HY_FORWARD[o]:
                            hyena_forward(o)
                        if u == HY_INVERSE[o]:
                            hyena_inverse(o)
                    if context:
                        h_part(8, KT - 1)
                    src = hc3 if context else h3
                    landed(SEQ_B2 + s)
                    if u >= 2:
                        pe.wait_ge(sem("b2_evac"), u - 1)
                    w = tiles(slot(SEQ_B2 + s), 256)
                    for j in range(2):
                        o = ps[:, u % 2, j * T:(j + 1) * T]
                        for kt in range(KT):
                            if what == "i":
                                last = mm(o, src[:, kt, j * P:(j + 1) * P], w[:, kt, :], start=kt == 0, stop=kt == KT - 1)
                            else:
                                last = mm(o, w[:, kt, j * P:(j + 1) * P], src[:, kt, :], start=kt == 0, stop=kt == KT - 1)
                    last.then_inc(sem("b2_unit"), 1)

            def hgrn():
                pe.wait_ge(sem("hg_gates"), 1)
                pe.wait_ge(sem("b2_evac"), len(B2_UNITS))
                pe.wait_ge(sem("hy_mixed"), 4)
                for d in range(2):
                    for tt in range(TT):
                        for h in range(HGH):
                            last = tr(ps[:, 2 * d + tt, h * P:(h + 1) * P], x_k[:, d, h, tt * P:(tt + 1) * P], ident)
                        last.then_inc(sem("hg_ctx_t"), 1)
                pe.wait_ge(sem("hg_ctx_kt"), 4)
                for d in range(2):
                    for h in range(HGH):
                        for tt in range(TT):
                            last = mm(ps[:, 4 + d, h * P:(h + 1) * P], x_kt[:, d, tt, h * P:(h + 1) * P],
                                      x_v[:, tt, h * P:(h + 1) * P], start=tt == 0, stop=tt == 1)
                    last.then_inc(sem("hg_state"), 1)

                def level(n, kk, qq):
                    for d in range(2):
                        for tt in range(TT):
                            for h in range(HGH):
                                last = mm(ps[:, 4 * (n % 2) + 2 * d + tt, h * P:(h + 1) * P],
                                          kk(d)[:, h, tt * P:(tt + 1) * P], qq(d)[:, h, tt * P:(tt + 1) * P],
                                          start=True, stop=True)
                    last.then_inc(sem("hg_level"), 1)

                pe.wait_ge(sem("hg_gates"), 2)
                level(0, lambda d: g_k[:, d], lambda d: g_q)
                pe.wait_ge(sem("hg_state_s"), 2)
                for lev in range(NLEV):
                    pe.wait_ge(sem("hg_scaled"), lev + 1)
                    if lev >= 1:
                        pe.wait_ge(sem("hg_taken"), lev)
                    level(lev + 1, lambda d: g_K[:, d], lambda d: g_Q[:, d])
                pe.wait_ge(sem("hg_scaled"), NLEV + 1)
                pe.wait_ge(sem("hg_taken"), NLEV)
                for d in range(2):
                    for h in range(HGH):
                        last = mm(ps[:, d, h * P:(h + 1) * P], g_K[:, d, h, d * P:(d + 1) * P],
                                  g_Q[:, d, h, (1 - d) * P:(2 - d) * P], start=True, stop=True)
                last.then_inc(sem("hg_cross"), 1)
                pe.wait_ge(sem("hg_cross_s"), 1)
                pe.wait_ge(sem("hg_taken"), NLEV + 1)
                pe.wait_ge(sem("hg_scaled"), NLEV + 2)
                for h in range(HGH):
                    o, e0 = half(2, h), slice(h * P, (h + 1) * P)
                    mm(o, g_S[0][:, h, :], g_Q[:, 0, h, :], start=True, stop=False, skip_group_check=True)
                    mm(o, g_S[1][:, h, :], g_Q[:, 1, h, :], start=False, stop=False, skip_group_check=True)
                    for d in range(2):
                        for tt in range(TT):
                            mm(o[:, tt * P:(tt + 1) * P], g_v[:, tt, e0], g_A[:, d, tt, h, :],
                               start=False, stop=False, skip_group_check=True)
                        last = mm(o[:, (1 - d) * P:(2 - d) * P], g_v[:, d, e0], g_X[:, d, h, :],
                                  start=False, stop=d == 1, skip_group_check=True)
                last.then_inc(sem("hg_out"), 1)
                pe.wait_ge(sem("hg_os"), 2)
                for b in range(2):
                    last = mm(ps[:, 4 + b, :], ones, sq[:, b * 512:(b + 1) * 512], start=True, stop=True)
                last.then_inc(sem("hg_out"), 1)
                k_outer(lambda m: half(0, m), 48, mix3, "proj_slot", kts=range(0, 4))

            def hyena_turn():
                pe.wait_ge(sem("hy_conv"), 1)
                pe.wait_ge(sem("filter_done"), 2)
                h_part(8, KT - 1)
                for tt in range(TT):
                    for w in range(3):
                        for j in range(4):
                            last = tr(ps[:, 2 + 3 * tt + w, j * P:(j + 1) * P], y_c[:, 4 * w + j, tt * P:(tt + 1) * P], ident)
                        last.then_inc(sem("hy_turned"), 1)

            def hyena_forward(o):
                cos, sinq = bigt("cos", T), bigt("sinq", T)
                if o == 0:
                    pe.wait_ge(sem("hy_rows"), 6)
                else:
                    pe.wait_ge(sem("hy_z"), 1)
                for ft in range(2):
                    for b, table in ((2, cos), (4, sinq)):
                        for tt in range(TT):
                            u = y_t[:, tt, 0:HYW] if o == 0 else y_z[:, tt, :]
                            last = mm(ps[:, b + ft, :], table[:, tt, ft * P:(ft + 1) * P], u, start=tt == 0, stop=tt == 1)
                last.then_inc(sem("hy_u"), 1)

            def hyena_inverse(o):
                inv = bigt("inv", T)
                pe.wait_ge(sem("hy_y"), o + 1)
                for tt in range(TT):
                    for f in range(4):
                        y = y_cc[:, f, :] if f < 2 else y_ss[:, f - 2, :]
                        last = mm(ps[:, 6 + tt, :], inv[:, f, tt * P:(tt + 1) * P], y, start=f == 0, stop=f == 3)
                last.then_inc(sem("hy_v"), 1)

            def hyena_back():
                pe.wait_ge(sem("hy_normed"), 1)
                for m in range(4):
                    for tt in range(TT):
                        last = tr(ps[:, 2 + m, tt * P:(tt + 1) * P], y_m[:, tt, m * P:(m + 1) * P], ident)
                    last.then_inc(sem("hy_back"), 1)

            def b2_out():
                pe.wait_ge(sem("hg_mixed"), 1)
                k_outer(lambda m: half(0, m), 48, mix3, "proj_slot", kts=range(4, KT))

            def gather(kt, out_, e0, e1):
                for tt in range(TT):
                    last = mm(out_, e_h[:, tt, kt * P:(kt + 1) * P],
                              e_sel[:, tt, e0:e1, :].rearrange("p e c -> p (e c)"), start=tt == 0, stop=tt == 1)
                last.then_inc(sem("e_gathers"), 1)

            def routing():
                for tt in range(TT):
                    for kt in range(KT):
                        h_part(9, kt)
                        last = tr(ps[:, 2 * tt + kt // 4, (kt % 4) * P:(kt % 4 + 1) * P], h3[:, kt, tt * P:(tt + 1) * P], ident)
                last.then_inc(sem("e_turned"), 1)
                for tt in range(TT):
                    for kt in range(KT):
                        last = mm(ps[:, 4, tt * NE:(tt + 1) * NE], h3[:, kt, tt * P:(tt + 1) * P], v("rw", kt * NE, NE),
                                  start=kt == 0, stop=kt == KT - 1)
                last.then_inc(sem("e_turned"), 1)
                pe.wait_ge(sem("e_aff"), 2)
                for tt in range(TT):
                    last = tr(ps[0:NE, 5, tt * P:(tt + 1) * P], e_aff[:, tt, :], ident)
                last.then_inc(sem("e_aff_t"), 1)
                pe.wait_ge(sem("e_rows"), 3)
                for e in range(NE):
                    if e == E_SECOND:
                        pe.wait_ge(sem("e_select"), 1)
                        for kt in range(KT):
                            gather(kt, first_tokens(kt), 0, E_FIRST)
                    mm(half(0, e), ident[0:NE, e:e + 1].to_broadcast([NE, P]), e_row[0:NE, :], start=True, stop=True) \
                        .then_inc(sem("e_spread"), 1)

            def way_back():
                pe.wait_ge(sem("e_select"), 3 + 2 * P // CAP)
                for e in range(NE):
                    if e % 2 == 0 and e >= 4:
                        pe.wait_ge(sem("e_back"), e // 2 - 1)
                    for tt in range(TT):
                        last = mm(half(2, e % 4)[:, tt * P:(tt + 1) * P],
                                  e_four[e // (NE // 2)][:, tt, e % (NE // 2), :, :].rearrange("p r c -> p (r c)"),
                                  e_diag[:, tt * NE + e, :], start=True, stop=True)
                    if e % 2:
                        last.then_inc(sem("e_gathers"), 1)
                pe.wait_ge(sem("e_back"), NE // 2)

            def experts():
                def expert(e, first=False):
                    def weights(j):
                        before = SEQ_MOE // NRING if j % E_RING < NRING else 0
                        pe.wait_ge(sem(f"ring_landed{j % E_RING}"), 16 * (PER_EXPERT // E_RING) * e
                                   + 16 * (before + j // E_RING + 1))
                        return e_slot(j)

                    pe.wait_ge(sem("moe_x"), e + 1)
                    for part in range(2):
                        for kt in range(KT):
                            w = weights(8 * part + kt)
                            for n in range(4):
                                last = mm(ps[32 * n:32 * n + 32, part, :], e_xe[:, kt, :], w[:, n * 512:(n + 1) * 512],
                                          start=kt == 0, stop=kt == KT - 1, skip_group_check=True)
                            last.then_inc(sem("moe_slot"), 1)
                    if first:
                        pe.wait_ge(sem("e_select"), 3)
                        for kt in range(KT):
                            if kt >= 4:
                                pe.wait_ge(sem("e_gather"), KT + kt - 3)
                            gather(kt, ps[:, 4 + kt % 4, 0:(NE - E_FIRST) * CAP], E_FIRST, NE)
                        way_back()
                        pe.wait_ge(sem("e_gather"), 2 * KT)
                        open_banks(4)
                    pe.wait_ge(sem("moe_h"), e + 1)
                    for i in range(4):
                        last = tr(ps[:, 2, i * P:(i + 1) * P], e_h2[:, i * P:(i + 1) * P], ident)
                    last.then_inc(sem("moe_turned"), 1)
                    pe.wait_ge(sem("moe_hT"), e + 1)
                    for j in range(8):
                        w = weights(16 + j)
                        for t2 in range(2):
                            n, i = (2 * j + t2) // 4, (2 * j + t2) % 4
                            for nn in range(2):
                                q = 64 * nn + 32 * t2
                                last = mm(ps[q:q + 32, 3, :], e_hT[:, i, 32 * n:32 * n + 32],
                                          w[:, t2 * D + nn * 512:t2 * D + (nn + 1) * 512],
                                          start=j == 0, stop=j == 7, skip_group_check=True)
                        last.then_inc(sem("moe_slot"), 1)
                    pe.wait_ge(sem("moe_y"), e + 1)
                    if first:
                        pe.wait_ge(sem("e_back"), NE // 2 + 1)
                    for i in range(4):
                        for nn in range(2):
                            r = slice(64 * nn, 64 * nn + 64)
                            last = mm(half(4, 4 * nn + i), e_y[r, i * P:(i + 1) * P], e_bk[r, :],
                                      start=False, stop=True, skip_group_check=True)
                    last.then_inc(sem("moe_o"), 1)

                expert(0, first=True)
                with pe.Fori(1, NE) as e:
                    expert(e)

            pe.wait_ge(sem("zeros"), 1)
            open_banks(2, ("gate_used", "gate_up_ready", "down_used"))
            pe.wait_ge(sem("start_landed"), 48)
            norm(0)
            ffn(0, 1)
            norm(1)
            mla()
            norm(2)
            ffn(1, 3)
            norm(3)
            ffn(2, 4)
            norm(4)
            rwkv()
            norm(5)
            ffn(3, 6)
            norm(6)
            filter_freq(0)
            norm(7)
            filter_freq(1)
            b2_in()
            hyena_back()
            hgrn()
            b2_out()
            norm(9)
            routing()
            experts()
            norm(10)
            for tt in range(TT):
                for kt in range(KT):
                    h_part(10, kt)
                    last = tr(ps[:, 2 * tt + kt // 4, (kt % 4) * P:(kt % 4 + 1) * P], h3[:, kt, tt * P:(tt + 1) * P], ident)
            last.then_inc(sem("row_turned"), 1)

        @block.scalar
        def _(act):
            f = nc.scalar.activation

            def copy(dst, src):
                return f(dst, src, ACT.Copy)

            def two(ap):
                return ap.rearrange("p b (h t) -> p (b h) t", t=T)

            n_root = [0]

            def root(buf):
                n_root[0] += 1
                act.wait_ge(sem("root_in"), n_root[0])
                f(buf, buf, ACT.Sqrt).then_inc(sem("root_out"), 1)

            n_shift = [0]

            def norm(i, ready, src=x3, dst=h3, shift=None):
                if i >= 1:
                    act.wait_ge(sem("norm_sum"), i)
                for b in range(4):
                    if ready is not None:
                        act.wait_ge(sem("x_ready"), KT * (ready - 1) + 2 * b + 2)
                    f(sq3[:, 2 * b:2 * b + 2, :], src[:, 2 * b:2 * b + 2, :], ACT.Square).then_inc(sem("squares"), 1)
                root(rstd[:, :])
                if shift is not None:
                    for m in range(KT):
                        act.wait_ge(sem("h_scaled"), KT * n_shift[0] + m + 1)
                        f(dst[:, m, :], dst[:, m, :], ACT.Identity, bias=shift[:, m:m + 1]).then_inc(sem("h_ready"), 1)
                    n_shift[0] += 1

            def modulated(i, ready, layer, s):
                at = 72 * layer + 24 * s
                norm(i, ready, shift=mods[:, at:at + 8])

            def ffn_group(t):
                for ft in range(2):
                    act.wait_ge(sem("gate_up_ready"), 2 * t + ft + 2)
                    f(sil3[:, ft, :], ps[:, ft, 0:T], ACT.Silu).then_inc(sem("silu_ready"), 1)

            def ffn(n, lo=0, hi=NG):
                with act.Fori(lo + NG * n, hi + NG * n) as t:
                    ffn_group(t)

            def mla():
                for b in range(3):
                    act.wait_ge(sem("mla_in"), 2 * b + 2)
                    copy(m_c[:, 2 * b:2 * b + 2, :], ps[:, b, :].rearrange("p (h t) -> p h t", t=T)).then_inc(sem("mla_c"), 1)
                act.wait_ge(sem("mla_c"), 3)
                act.wait_ge(sem("norm_sum"), 2)
                f(sq3[:, 0:5, :], m_c[:, 0:5, :], ACT.Square).then_inc(sem("mla_c"), 1)
                root(m_rope)
                for b in range(8):
                    act.wait_ge(sem("mla_q"), b + 1)
                    copy(m_q[0:64, 2 * b:2 * b + 2, :], ps[0:64, b, :].rearrange("p (h t) -> p h t", t=T)) \
                        .then_inc(sem("mla_q_nope"), 1)
                for b in range(4):
                    act.wait_ge(sem("mla_kv"), b + 1)
                    for o in range(2):
                        copy(m_k[0:64, 4 * b + o:4 * b + o + 3:2, :],
                             ps[64 * o:64 * o + 64, b, :].rearrange("p (h t) -> p h t", t=T)).then_inc(sem("mla_k_nope"), 1)
                def exponentials(b):
                    s, st = 3 * (b % 2), m_st[:, 32 * (b % 2):32 * (b % 2) + 32]
                    act.wait_ge(sem("mla_max"), b + 1)
                    if b >= 2:
                        act.wait_ge(sem("mla_turned"), b - 1)
                    for hh in range(4):
                        f(m_p0[b % 2][:, hh, :], ps[:, s, hh * P:(hh + 1) * P], ACT.Exp, bias=st[:, 8 + hh:9 + hh],
                          scale=QK ** -0.5, accum_out=st[:, 16 + hh:17 + hh]).then_inc(sem("mla_exp"), 1)
                        f(m_p1[b % 2][:, hh, :], half(s + 1, hh), ACT.Exp, bias=st[:, 12 + hh:13 + hh],
                          scale=QK ** -0.5, accum_out=st[:, 20 + hh:21 + hh]).then_inc(sem("mla_exp"), 1)

                def copies(b):
                    s = 3 * (b % 2)
                    act.wait_ge(sem("mla_turned"), b + 1)
                    copy(m_t0, two(ps[:, 6:8, :])).then_inc(sem("mla_t0"), 1)
                    act.wait_ge(sem("mla_pv"), b + 1)
                    copy(m_o[:, 2 * b:2 * b + 2, :], ps[:, s + 1, :].rearrange("p (h t) -> p h t", t=T)) \
                        .then_inc(sem("mla_o"), 1)

                for b in (0, 2):
                    exponentials(b)
                    exponentials(b + 1)
                    copies(b)
                    copies(b + 1)

            def heads(bank):
                return tiles(ps[:, bank, :], HD)

            def rwkv():
                act.wait_ge(sem("rwkv_low1"), 1)
                f(hid3[0:64, 0, :], ps[0:64, 6, 0:T], ACT.Tanh).then_inc(sem("rwkv_low"), 1)
                act.wait_ge(sem("rwkv_low1"), 2)
                copy(hid3[0:64, 1, :], ps[0:64, 5, 0:T]).then_inc(sem("rwkv_low"), 1)
                act.wait_ge(sem("rwkv_low1"), 3)
                act.wait_ge(sem("zeros"), 2)
                f(sil3[0:32, 1, :], ps[0:32, 7, T:2 * T], ACT.Sigmoid)
                f(sil3[:, 0, :], ps[:, 7, 0:T], ACT.Sigmoid).then_inc(sem("rwkv_low"), 1)
                for n, (dst, bias, bank) in enumerate(((r_w, "w0", 0), (r_a, "a0", 4))):
                    act.wait_ge(sem("rwkv_low2"), n + 1)
                    for m in range(KT):
                        last = f(dst[:, m, :], half(bank, m), ACT.Sigmoid, bias=v(bias, m))
                    last.then_inc(sem("rwkv_sig"), 1)
                act.wait_ge(sem("rwkv_low2"), 3)
                copy(r_o, two(ps[:, 0:4, :])).then_inc(sem("rwkv_sig"), 1)
                act.wait_ge(sem("rkv_slot"), 4)
                copy(r_k, two(ps[:, 4:8, :]))
                act.wait_ge(sem("rwkv_mix"), 6)
                for m in range(KT):
                    last = f(r_x[:, m, :], half(4, m), ACT.Copy, scale=v("k_k", m))
                last.then_inc(sem("rwkv_rkv"), 1)
                act.wait_ge(sem("rwkv_rkv"), 1)
                f(sq3, r_x, ACT.Square).then_inc(sem("rwkv_kk2"), 1)
                act.wait_ge(sem("rwkv_G"), 1)
                f(r_dec, r_e1[:, :, CH - 1::CH], ACT.Exp)
                f(r_e2, r_e1, ACT.Exp, scale=-1.0).then_inc(sem("rwkv_E"), 1)
                act.wait_ge(sem("rwkv_Gp"), 1)
                f(r_e3, r_w, ACT.Exp).then_inc(sem("rwkv_E"), 1)
                act.wait_ge(sem("rwkv_E"), 2)
                f(r_e1, r_e1, ACT.Exp).then_inc(sem("rwkv_E"), 1)
                act.wait_ge(sem("rkv_slot"), 8)
                copy(r_r, two(ps[:, 0:4, :])).then_inc(sem("rwkv_rkv"), 1)
                root(sq3)
                act.wait_ge(sem("rkv_slot"), 12)
                copy(r_v, two(ps[:, 0:4, :])).then_inc(sem("rwkv_rkv"), 1)
                for p, (name, left, right) in enumerate(c_first):
                    if right is None:
                        for c in range(NCH):
                            act.wait_ge(sem("rw_first"), 4 * p + c + 1)
                            copy({"vs": c_vs, "bt": c_bt, "kt": c_kt}[name][c], heads((4 * p + c) % 8)).then_inc(sem("rw_first_a"), 1)
                for n in range(5 * NCH):
                    act.wait_ge(sem("rw_Y"), n + 1)
                    copy(c_y[n % NCH], heads(n % NCH)).then_inc(sem("rw_Ys"), 1)
                for c in range(NCH + 1):
                    if c < NCH:
                        act.wait_ge(sem("rw_rhs"), c + 1)
                        copy(c_y[c], heads(0)).then_inc(sem("rw_rhs_s"), 1)
                        act.wait_ge(sem("rw_u"), c + 1)
                        copy(c_t[c], heads(1)).then_inc(sem("rw_u_s"), 1)
                    if c > 0:
                        root(c_st[c - 1][:, 8:16])
                        act.wait_ge(sem("rw_out"), c)
                        copy(r_w[:, :, (c - 1) * CH:c * CH], heads(5 + (c - 1) % 2)).then_inc(sem("rw_y"), 1)

            def filter_step(i):
                if i == 0:
                    act.wait_ge(sem("hg_lb_in"), 1)
                    f(small[:, 168:184], small[:, 168:184], ACT.Exp).then_inc(sem("hg_lb_exp"), 1)
                if i < 2:
                    act.wait_ge(sem("filter_arg"), i + 1)
                    f(f_in[0:64, 0, 0:T], f_in[0:64, 0, T:2 * T], ACT.Sin).then_inc(sem("filter_sin"), 1)
                elif i == 6:
                    act.wait_ge(sem("filter_h"), 8)
                    for o in range(2):
                        sides = f_abs[o].rearrange("p (t s c) -> p t s c", t=TT, c=HYW)
                        for tt in range(TT):
                            last = f(sides[:, tt, :, :], f_h[:, tt, 2 * o:2 * o + 2, :], ACT.Abs)
                        last.then_inc(sem("filter_abs"), 1)

            def b2_in():
                for u, (s, what, context) in enumerate(B2_UNITS):
                    if u == CTX_AT:
                        act.wait_ge(sem("ctx_landed"), 16)
                        norm(8, None, ctx3, hc3, shift=cmods[:, 0:8])
                    hyena_step(u)
                    act.wait_ge(sem("b2_unit"), u + 1)
                    src = ps[:, u % 2, :]
                    src2 = src.rearrange("p (h t) -> p h t", t=T)
                    j = (s - 6) % 2
                    if what == "hy":
                        last = copy(hy_p[:, 2 * s:2 * s + 2, :], src2)
                    elif what == "q":
                        last = f(g_q[:, 2 * j:2 * j + 2, :], src2, ACT.Silu)
                    elif what == "i":
                        last = copy((x_v if context else g_v)[:, :, j * T:(j + 1) * T], src2)
                    elif what == "g":
                        last = f(g_g[:, 2 * j:2 * j + 2, :], src2, ACT.Silu)
                    else:
                        d = 0 if what == "zf" else 1
                        last = f((x_f if context else g_f)[:, d, 2 * j:2 * j + 2, :], src2, ACT.Sigmoid)
                    last.then_inc(sem("b2_evac"), 1)

            def hgrn():
                for i in range(4):
                    act.wait_ge(sem("hg_ctx_t"), i + 1)
                    copy(x_kt[:, i // 2, i % 2, :], ps[:, i, :]).then_inc(sem("hg_ctx_kt"), 1)
                act.wait_ge(sem("hg_state"), 2)
                for d in range(2):
                    copy(g_S[d], ps[:, 4 + d, :].rearrange("p (h s) -> p h s", s=P)).then_inc(sem("hg_state_s"), 1)
                act.wait_ge(sem("hg_cross"), 1)
                copy(g_X, ps[:, 0:2, :].rearrange("p d (h s) -> p d h s", s=P)).then_inc(sem("hg_cross_s"), 1)
                act.wait_ge(sem("hg_out"), 1)
                copy(g_F[:, 0], two(ps[:, 2:4, :])).then_inc(sem("hg_os"), 1)
                act.wait_ge(sem("hg_os"), 1)
                f(sq3[:, 0:4, :], g_F[:, 0], ACT.Square).then_inc(sem("hg_os"), 1)
                root(g_F[:, 1])

            def hyena_step(u):
                if u == HY_CONV:
                    act.wait_ge(sem("b2_evac"), HY_CONV)
                    for m in range(12):
                        f(y_c[:, m, :], hy_p[:, m, :], ACT.Identity, scale=v("conv_w", 12 + m), bias=v("conv_b", m)) \
                            .then_inc(sem("hy_middle"), 1)
                elif u == HY_TURN:
                    for i in range(6):
                        act.wait_ge(sem("hy_turned"), i + 1)
                        copy(y_t[:, i // 3, (i % 3) * HYW:(i % 3 + 1) * HYW], ps[:, 2 + i, :]).then_inc(sem("hy_rows"), 1)
                elif u == HY_NORM:
                    act.wait_ge(sem("hy_z"), 2)
                    for tt in range(TT):
                        f(sq[:, tt * HYW:(tt + 1) * HYW], y_m[:, tt, :], ACT.Square, accum_out=small[:, 208 + tt:209 + tt]) \
                            .then_inc(sem("hy_square"), 1)
                    root(small[:, 208:210])

            def hyena_back():
                for m in range(4):
                    act.wait_ge(sem("hy_back"), m + 1)
                    f(mix3[:, m, :], ps[:, 2 + m, 0:T], ACT.Copy, scale=v("hy_norm_g", m)).then_inc(sem("hy_mixed"), 1)

            def routing():
                act.wait_ge(sem("e_turned"), 1)
                copy(e_h, ps[:, 0:4, :].rearrange("p (t b) c -> p t (b c)", t=TT)).then_inc(sem("e_rows"), 1)
                act.wait_ge(sem("e_aff"), 1)
                f(e_aff, e_aff, ACT.Exp).then_inc(sem("e_rows"), 1)
                act.wait_ge(sem("e_aff_t"), 1)
                copy(e_row[0:NE, :], ps[0:NE, 5, 0:T]).then_inc(sem("e_rows"), 1)
                for kt in range(KT):
                    act.wait_ge(sem("e_gathers"), 4 * (kt // 4) + 4)
                    copy(e_x[:, kt, 0:E_FIRST * CAP], first_tokens(kt)).then_inc(sem("e_gather"), 1)

            def experts():
                def expert(e, first=False):
                    act.wait_ge(sem("moe_slot"), PER_EXPERT * e + 8)
                    f(e_s, ps[:, 0, :], ACT.Silu).then_inc(sem("moe_silu"), 1)
                    if first:
                        for kt in range(KT):
                            act.wait_ge(sem("e_gathers"), KT + kt + 1)
                            copy(e_x[:, kt, E_FIRST * CAP:], ps[:, 4 + kt % 4, 0:(NE - E_FIRST) * CAP]).then_inc(sem("e_gather"), 1)
                        for b in range(NE // 2):
                            act.wait_ge(sem("e_gathers"), 2 * KT + b + 1)
                            copy(e_back[:, 2 * b:2 * b + 2, :], ps[:, 2 + b % 2, :].rearrange("p (h t) -> p h t", t=T)) \
                                .then_inc(sem("e_back"), 1)
                    act.wait_ge(sem("moe_turned"), e + 1)
                    copy(e_hT, ps[:, 2, :].rearrange("p (i c) -> p i c", c=P)).then_inc(sem("moe_hT"), 1)
                    act.wait_ge(sem("moe_slot"), PER_EXPERT * e + PER_EXPERT)
                    copy(e_y, ps[:, 3, :]).then_inc(sem("moe_y"), 1)

                expert(0, first=True)
                with act.Fori(1, NE) as e:
                    expert(e)

            act.wait_ge(sem("c_landed"), 16)
            f(c_rows[:, 0:D], c_rows[:, 0:D], ACT.Silu).then_inc(sem("c_ready"), 1)
            act.wait_ge(sem("start_landed"), 48)
            modulated(0, None, 0, 0)
            ffn(0)
            modulated(1, 1, 0, 1)
            act.wait_ge(sem("tables_landed"), 32)
            f(c_rows[:, D:], c_rows[:, D:], ACT.Silu).then_inc(sem("c_ready"), 1)
            mla()
            modulated(2, 2, 0, 2)
            ffn(1)
            modulated(3, 3, 1, 0)
            ffn(2)
            modulated(4, 4, 1, 1)
            rwkv()
            modulated(5, 5, 1, 2)
            ffn(3, 0, FILTER_AT)
            for i in range(FILTER_STEPS):
                filter_step(i)
                ffn_group(3 * NG + FILTER_AT + i)
            ffn(3, FILTER_AT + FILTER_STEPS)
            norm(6, 6)
            norm(7, 7, shift=mods[:, 144:152])
            b2_in()
            hyena_back()
            hgrn()
            norm(9, 8, shift=mods[:, 144 + 24:144 + 32])
            routing()
            experts()
            norm(10, 9)
            act.wait_ge(sem("row_turned"), 1)
            copy(o_row, ps[:, 0:4, :].rearrange("p (t b) c -> p t (b c)", t=TT)).then_inc(sem("row_ready"), 1)

        @block.gpsimd
        def _(pool):
            nc.gpsimd.memset(zeros[:, :], 0.0).then_inc(sem("zeros"), 1)
            pool.wait_ge(sem("h_ready"), 5 * KT)
            for c in range(NCH):
                for buf in (c_t[c], c_tt[c]):
                    nc.gpsimd.tensor_copy(buf, bcm(k("i64"), KT)).then_inc(sem("rw_ident"), 1)

        @block.vector
        def _(dve):
            n_order = [0]

            def done(ins):
                n_order[0] += 1
                ins.then_inc(sem("dve_order"), 1)
                dve.wait_ge(sem("dve_order"), n_order[0])

            tt_, ts, stt, cp = (nc.vector.tensor_tensor, nc.vector.tensor_scalar, nc.vector.scalar_tensor_tensor,
                                nc.vector.tensor_copy)
            red = nc.vector.tensor_reduce

            def two(ap):
                return ap.rearrange("p b (h t) -> p (b h) t", t=T)

            n_root = [0]

            def root(ins):
                n_root[0] += 1
                ins.then_inc(sem("root_in"), 1)
                dve.wait_ge(sem("root_out"), n_root[0])

            def inverse_root(ins, buf):
                root(ins)
                done(nc.vector.reciprocal(buf, buf))

            def norm(i, src, dst, scale, name="h_scaled"):
                dve.wait_ge(sem("norm_sum"), i + 1)
                inverse_root(ts(rstd[:, :], norm_sums(i), 1.0 / D, EPS, ALU.mult, ALU.add), rstd[:, :])
                for m in range(KT):
                    stt(out=dst[:, m, :], in0=src[:, m, :], scalar=scale[:, m:m + 1], in1=rstd[:, :], op0=ALU.mult, op1=ALU.mult) \
                        .then_inc(sem(name), 1)

            def scale_of(at, g, src=mods, to=0):
                done(stt(out=coef[:, to:to + 8], in0=src[:, at:at + 8], scalar=1.0, in1=g, op0=ALU.add, op1=ALU.mult))

            def gate_of(at, factor):
                done(ts(coef[:, 8:16], mods[:, at:at + 8], factor, None, ALU.mult))

            n_residual = [0]

            def residual(src=None, end=None):
                for m in range(KT):
                    if end and m in (0, 2, 4):
                        dve.wait_ge(sem("out_part"), 3 * n_residual[0] + m // 2 + 1)
                    elif end and m == 6:
                        dve.wait_ge(sem(end[0]), end[1])
                    stt(out=x3[:, m, :], in0=acc(m) if src is None else src(m), scalar=coef[:, 8 + m:9 + m],
                        in1=x3[:, m, :], op0=ALU.mult, op1=ALU.add).then_inc(sem("x_ready"), 1)
                n_residual[0] += 1

            def ada_round(r, row, context=False, junk=sq):
                def dot(w, which, col, out_at, buf, done_sem):
                    nc.vector.tensor_tensor_reduce(buf[:, out_at * D:(out_at + 1) * D], w, c_rows[:, which * D:(which + 1) * D],
                                                   1.0, 0.0, ALU.mult, ALU.add, dots[:, col:col + 1]).then_inc(sem(done_sem), 1)

                dve.wait_ge(sem("ada_kept"), r)
                for j in range(NADA):
                    dve.wait_ge(sem(f"ada_landed{j}"), 16 * r + 16)
                    w = ada_slot(j)
                    if context:
                        dve.wait_ge(sem("ada_context"), 9 * (r - 18) + 2 * j)
                        for i in range(2):
                            dot(w[:, i, :], 2, 8 + 2 * j + i, i, ar(0, 2 * D), "ada_context")
                    dve.wait_ge(sem("ada_first"), 4 * r + j)
                    dot(w[:, 0, :], row, 2 * j, 0, junk, "ada_first")
                    dve.wait_ge(sem("ada_used"), 4 * r + j)
                    dot(w[:, 1, :], row, 2 * j + 1, 1, junk, "ada_used")
                dve.wait_ge(sem("ada_first"), 4 * r + 4)
                dve.wait_ge(sem("ada_used"), 4 * r + 4)
                cp(mods[:, bass.ds(8 * r, 8)], dots[:, 0:8]).then_inc(sem("ada_kept"), 1)
                if context:
                    dve.wait_ge(sem("ada_context"), 9 * (r - 18) + 8)
                    cp(cmods[:, bass.ds(8 * (r - 18), 8)], dots[:, 8:16]).then_inc(sem("ada_context"), 1)

            def hidden(t):
                for ft in range(2):
                    dve.wait_ge(sem("silu_ready"), 2 * t + ft + 1)
                    tt_(hid3[:, ft, :], sil3[:, ft, :], ps[:, ft, T:2 * T], ALU.mult).then_inc(sem("hid_ready"), 1)

            def ffn(n):
                t0 = NG * n
                for lo, hi, row, context in {1: [(0, 5, 0, False), (5, 7, 1, True), (7, NG - 1, 1, False)],
                                             3: [(0, FILTER_AT, None, False)]}.get(n, [(0, NG, None, False)]):
                    if context:
                        dve.wait_ge(sem("c_ready"), 2)
                        for t in range(t0 + lo, t0 + hi):
                            hidden(t)
                            ada_round(t + ADA_FIRST, row, True)
                        continue
                    with dve.Fori(t0 + lo, t0 + hi) as t:
                        hidden(t)
                        if row is not None:
                            ada_round(t + ADA_FIRST, row)
                if n == 1:
                    hidden(t0 + NG - 1)
                if n == 3:
                    for i in range(FILTER_STEPS):
                        filter_step(i)
                        hidden(t0 + FILTER_AT + i)
                    with dve.Fori(t0 + FILTER_AT + FILTER_STEPS, t0 + NG) as t:
                        hidden(t)
                residual(end=("down_used", NG * (n + 1) + 1))

            def ada_bias(lo, hi, kept):
                dve.wait_ge(sem("ada_kept"), kept)
                done(tt_(mods[:, lo:hi], mods[:, lo:hi], v("ada_b", lo, hi - lo), ALU.add))

            def mixed(n, src=None):
                residual(src, ("proj_slot", 4 * n + 4))

            def mla():
                dve.wait_ge(sem("mla_in"), 7)
                r2 = m_rope
                done(ts(r2[:, 0, :], ps[:, 3, 0:T], 1.0 / 384, EPS, ALU.mult, ALU.add))
                root(ts(r2[:, 1, :], ps[:, 3, T:2 * T], 1.0 / 256, EPS, ALU.mult, ALU.add))
                for n, (name, m0, m1) in enumerate((("q_norm", 0, 3), ("kv_norm", 3, 5))):
                    done(nc.vector.reciprocal(r2[:, n, :], r2[:, n, :]))
                    for m in range(m0, m1):
                        last = stt(out=m_c[:, m, :], in0=m_c[:, m, :], scalar=v(name, m - m0), in1=r2[:, n, :],
                                   op0=ALU.mult, op1=ALU.mult)
                    last.then_inc(sem("mla_normed"), 1)
                dve.wait_ge(sem("mla_normed"), 2)
                rope = k("rope")
                done(tt_(m_k[64:96, 0, :], m_c[64:96, 5, :], rope[64:96, :], ALU.mult))
                done(tt_(m_rope[64:96, 0, :], m_c[96:128, 5, :], rope[96:128, :], ALU.mult))
                done(tt_(m_k[64:96, 0, :], m_k[64:96, 0, :], m_rope[64:96, 0, :], ALU.add))
                cp(m_k[64:96, 1:HEADS, :], bcm(m_k[64:96, 0, :], HEADS - 1)).then_inc(sem("mla_k_rope"), 1)
                for b in range(8):
                    dve.wait_ge(sem("mla_q"), b + 1)
                    q, src = m_q[:, 2 * b:2 * b + 2, :], ps[:, b, :].rearrange("p (h t) -> p h t", t=T)
                    done(tt_(q[64:96], src[64:96], bcm(rope[64:96, :], 2), ALU.mult))
                    done(tt_(m_rope[64:96], src[96:128], bcm(rope[96:128, :], 2), ALU.mult))
                    tt_(q[64:96], q[64:96], m_rope[64:96], ALU.add).then_inc(sem("mla_q_rope"), 1)
                    dve.wait_ge(sem("mla_q_rope"), b + 1)
                for i in range(4):
                    dve.wait_ge(sem("mla_kv"), 5 + i)
                    cp(m_v[:, i // 2, (i % 2) * 512:(i % 2 + 1) * 512], ps[:, 4 + i, :]).then_inc(sem("mla_v"), 1)
                def bank_of(b):
                    return 3 * (b % 2), m_st[:, 32 * (b % 2):32 * (b % 2) + 32]

                def maxima(b):
                    s, st = bank_of(b)
                    s0, s1 = ps[:, s, :].rearrange("p (h t) -> p h t", t=P), two(ps[:, s + 1:s + 3, :])
                    dve.wait_ge(sem("mla_scores"), b + 1)
                    done(tt_(s0, s0, bcm(k("causal"), 4), ALU.add))
                    done(tt_(s1[:, :, P:T], s1[:, :, P:T], bcm(k("causal"), 4), ALU.add))
                    done(red(st[:, 0:4], s0, AXX, ALU.max))
                    done(red(st[:, 4:8], s1, AXX, ALU.max))
                    ts(st[:, 8:16], st[:, 0:8], -(QK ** -0.5), None, ALU.mult).then_inc(sem("mla_max"), 1)

                def normalised(b):
                    s, st = bank_of(b)
                    p0, p1 = m_p0[b % 2], m_p1[b % 2]
                    dve.wait_ge(sem("mla_exp"), 8 * b + 8)
                    done(nc.vector.reciprocal(st[:, 24:32], st[:, 16:24]))
                    done(tt_(p0, p0, bc(st[:, 24:28], P), ALU.mult))
                    tt_(p1, p1, bc(st[:, 28:32], T), ALU.mult).then_inc(sem("mla_probs"), 1)
                    dve.wait_ge(sem("mla_turned"), b + 1)
                    cp(m_t1, ps[:, s, :].rearrange("p (h t) -> p h t", t=P)).then_inc(sem("mla_t1"), 1)

                for b in (0, 2):
                    maxima(b)
                    maxima(b + 1)
                    normalised(b)
                    normalised(b + 1)

            def heads(bank):
                return tiles(ps[:, bank, :], HD)

            def rwkv():
                dve.wait_ge(sem("h_ready"), 5 * KT)
                nc.vector.memset(sil3[:, 1, :], 0.0).then_inc(sem("zeros"), 1)
                done(tt_(r_x[:, :, 1:T], h3[:, :, 0:T - 1], h3[:, :, 1:T], ALU.subtract))
                done(ts(r_x[:, :, 0:1], h3[:, :, 0:1], -1.0, None, ALU.mult))
                def mix(n):
                    part = (3, 4, 5, 1, 0, 2)[n]
                    dst = r_b if n % 2 else r_g
                    if n in (2, 3):
                        dve.wait_ge(sem("rwkv_low1"), n - 1)
                    elif n == 4:
                        dve.wait_ge(sem("rwkv_low1"), 3)
                    elif n == 5:
                        dve.wait_ge(sem("rkv_slot"), 4)
                    for m in range(KT):
                        last = stt(out=dst[:, m, :], in0=r_x[:, m, :], scalar=v("mu", 8 * part + m), in1=h3[:, m, :],
                                   op0=ALU.mult, op1=ALU.add)
                    last.then_inc(sem("rwkv_mix"), 1)

                for n in range(5):
                    mix(n)
                dve.wait_ge(sem("rwkv_sig"), 2)
                done(ts(r_w, r_w, -float(np.exp(-0.5)), None, ALU.mult))
                for m in range(KT):
                    last = nc.vector.tensor_tensor_scan(r_e1[:, m, :], k("keep"), r_w[:, m, :], 0.0, ALU.mult, ALU.add)
                last.then_inc(sem("rwkv_G"), 1)
                dve.wait_ge(sem("rwkv_G"), 1)
                tt_(r_w, r_e1, r_w, ALU.subtract).then_inc(sem("rwkv_Gp"), 1)
                for m in range(KT):
                    last = ts(r_t[:, m, :], r_a[:, m, :], -1.0, v("k_a", m), ALU.add, ALU.mult)
                done(last)
                mix(5)
                dve.wait_ge(sem("rwkv_rkv"), 1)
                done(stt(out=r_k, in0=r_t, scalar=1.0, in1=r_k, op0=ALU.add, op1=ALU.mult))
                dve.wait_ge(sem("rwkv_sums"), 1)
                n_root[0] += 1
                ts(sq3, two(ps[:, 4:8, :]), 1e-24, None, ALU.max).then_inc(sem("root_in"), 1)
                dve.wait_ge(sem("rwkv_rkv"), 2)
                for m in range(KT):
                    last = stt(out=r_t[:, m, :], in0=r_r[:, m, :], scalar=v("r_k", m), in1=r_k[:, m, :],
                               op0=ALU.mult, op1=ALU.mult)
                last.then_inc(sem("rwkv_prod"), 1)
                dve.wait_ge(sem("root_out"), n_root[0])
                nc.vector.reciprocal(sq3, sq3)
                dve.wait_ge(sem("rwkv_prod"), 1)
                dve.wait_ge(sem("rwkv_E"), 3)
                tt_(r_r, r_r, r_e1, ALU.mult)
                done(tt_(r_k, r_k, r_e2, ALU.mult))
                done(tt_(r_x, r_x, sq3, ALU.mult))
                done(tt_(r_a, r_a, r_x, ALU.mult))
                stt(out=r_x, in0=r_x, scalar=-1.0, in1=r_e3, op0=ALU.mult, op1=ALU.mult)
                tt_(r_a, r_a, r_e2, ALU.mult).then_inc(sem("rwkv_prep"), 1)
                dve.wait_ge(sem("rwkv_sums"), 2)
                dve.wait_ge(sem("rwkv_rkv"), 3)
                tt_(r_b, two(ps[:, 4:8, :]), r_v, ALU.mult).then_inc(sem("rwkv_prep"), 1)
                dve.wait_ge(sem("rwkv_prep"), 2)
                dve.wait_ge(sem("rw_ident"), 2 * NCH)
                low, up = (k(name).bitcast(U32) for name in ("low64", "up64"))
                n = 0
                for p, (name, left, right) in enumerate(c_first):
                    if right is not None:
                        for c in range(NCH):
                            src = heads((4 * p + c) % 8)
                            n += 1
                            dve.wait_ge(sem("rw_first"), 4 * p + c + 1)
                            if name == "m":
                                nc.vector.copy_predicated(c_t[c], bcm(low[:, 0:HD], KT), src).then_inc(sem("rw_first_d"), 1)
                                dve.wait_ge(sem("rw_first_d"), n)
                                nc.vector.copy_predicated(c_tt[c], bcm(up[:, 0:HD], KT), c_ab[c]).then_inc(sem("rw_T"), 1)
                            else:
                                dst = {"ab": c_ab, "ak": c_ak, "rb": c_rb, "rk": c_rk}[name][c]
                                tt_(dst, src, bcm(k("before" if name in ("ab", "ak") else "upto"), KT), ALU.mult) \
                                    .then_inc(sem("rw_first_d"), 1)
                for lev in range(1, 6):
                    for c in range(NCH):
                        dve.wait_ge(sem("rw_Z"), 4 * (lev - 1) + c + 1)
                        dve.wait_ge(sem("rw_T"), 4 * (lev - 1) + c + 1)
                        at = slice(lev * HD, (lev + 1) * HD)
                        if lev < 5:
                            nc.vector.copy_predicated(c_t[c], bcm(low[:, at], KT), heads(c))
                        nc.vector.copy_predicated(c_tt[c], bcm(up[:, at], KT), heads(4 + c)).then_inc(sem("rw_T"), 1)
                for c in range(NCH):
                    if c < NCH - 1:
                        dve.wait_ge(sem("rw_ds"), c + 1)
                        ds_ = heads(4)
                        if c > 0:
                            done(tt_(c_s, c_s, ds_, ALU.add))
                            ds_ = c_s
                        tt_(c_s, ds_, bc(r_dec[:, :, c], HD), ALU.mult).then_inc(sem("rw_S"), 1)
                    st, mid, square = c_st[c], c_tt[c], c_y[c]
                    dve.wait_ge(sem("rw_o"), c + 1)
                    done(red(st[:, 0:8], heads(2 + c % 2), AXX, ALU.add))
                    done(ts(st[:, 0:8], st[:, 0:8], 1.0 / HD, None, ALU.mult))
                    done(tt_(mid, heads(2 + c % 2), bc(st[:, 0:8], HD), ALU.subtract))
                    done(tt_(square, mid, mid, ALU.mult))
                    done(red(st[:, 8:16], square, AXX, ALU.add))
                    inverse_root(ts(st[:, 8:16], st[:, 8:16], 1.0 / HD, GN_EPS, ALU.mult, ALU.add), st[:, 8:16])
                    tt_(c_ab[c], mid, bc(st[:, 8:16], HD), ALU.mult).then_inc(sem("rw_yb"), 1)
                for m in range(KT):
                    last = ts(r_b[:, m, :], r_b[:, m, :], v("gn_b", m), None, ALU.add)
                done(last)
                dve.wait_ge(sem("rw_y"), NCH)
                before = n_order[0]
                for m in range(KT + 1):
                    if m < KT:
                        stt(out=r_w[:, m, :], in0=r_w[:, m, :], scalar=v("gn_w", m), in1=r_b[:, m, :], op0=ALU.mult,
                            op1=ALU.add).then_inc(sem("dve_order"), 1)
                    if m > 0:
                        dve.wait_ge(sem("dve_order"), before + m)
                        tt_(r_w[:, m - 1, :], r_w[:, m - 1, :], r_o[:, m - 1, :], ALU.mult).then_inc(sem("rwkv_y"), 1)
                n_order[0] += KT

            def filter_step(i):
                if i == 0:
                    lb0, lb1 = v("hg_lb", 0, 8), v("hg_lb", 8, 8)
                    done(tt_(small[:, 160:168], lb0, lb1, ALU.max))
                    done(tt_(small[:, 168:176], lb0, small[:, 160:168], ALU.subtract))
                    tt_(small[:, 176:184], lb1, small[:, 160:168], ALU.subtract).then_inc(sem("hg_lb_in"), 1)
                    dve.wait_ge(sem("hg_lb_exp"), 1)
                    done(tt_(small[:, 184:192], small[:, 168:176], small[:, 176:184], ALU.add))
                    done(nc.vector.reciprocal(small[:, 184:192], small[:, 184:192]))
                    done(tt_(small[:, 192:200], small[:, 168:176], small[:, 184:192], ALU.mult))
                    done(ts(small[:, 200:208], small[:, 192:200], -1.0, 1.0, ALU.mult, ALU.add))
                if i < 2:
                    arg, turns = f_in[0:64, 0, T:2 * T], f_in[0:64, 1, 0:T]
                    magic = 1.5 * 2.0 ** 23
                    c1 = 6.28125
                    c2 = float(np.floor((2 * np.pi - c1) * 2.0 ** 22) / 2.0 ** 22)
                    c3 = 2 * np.pi - c1 - c2
                    b, fr = (("pos_b1", "freq1"), ("pos_b2", "freq2"))[i]
                    dve.wait_ge(sem("filter_mm"), i + 1)
                    done(ts(arg, ps[0:64, 6 + i, 0:T], v(b)[0:64], v(fr)[0:64], ALU.add, ALU.mult))
                    done(ts(turns, arg, 1.0 / (2 * np.pi), magic, ALU.mult, ALU.add))
                    done(ts(turns, turns, magic, None, ALU.subtract))
                    for part in (c1, c2, c3):
                        done(stt(out=arg, in0=turns, scalar=-part, in1=arg, op0=ALU.mult, op1=ALU.add))
                    ts(arg, arg, 3.1415925, -3.1415925, ALU.min, ALU.max).then_inc(sem("filter_arg"), 1)
                elif i < 6:
                    win = f_win[:, 0:TT * 2 * HYW].rearrange("p (t s c) -> p t s c", t=TT, c=HYW)
                    for n in (2 * (i - 2), 2 * (i - 2) + 1):
                        dve.wait_ge(sem("filter_mm"), 3 + n)
                        tt_(f_h[:, n // 4, n % 4, :], ps[:, 6 + n % 2, :], win[:, n // 4, n % 2, :], ALU.mult) \
                            .then_inc(sem("filter_h"), 1)
                else:
                    for o in range(2):
                        dve.wait_ge(sem("filter_l1"), o + 1)
                        done(ts(f_rn[:, o, :], ps[:, 6 + o, :], EPS, None, ALU.add))
                        done(nc.vector.reciprocal(f_rn[:, o, :], f_rn[:, o, :]))
                    filter_sides(0)

            def filter_sides(o):
                done(tt_(f_sum, f_h[:, :, 2 * o, :], f_h[:, :, 2 * o + 1, :], ALU.add))
                tt_(f_dif, f_h[:, :, 2 * o, :], f_h[:, :, 2 * o + 1, :], ALU.subtract).then_inc(sem("filter_sides"), 1)

            def filter_end(o):
                dve.wait_ge(sem("filter_freq"), o + 1)
                if o == 0:
                    filter_sides(1)
                rn, bias = f_rn[:, o, :], f_bias[:, o, :]
                tt_(f_A[o], ps[:, 2:4, :], bcm(rn, 2), ALU.mult)
                done(tt_(f_D[o], ps[:, 6, :], rn, ALU.mult))
                tt_(f_A[o], f_A[o], bcm(bias, 2), ALU.add)
                tt_(f_D[o], f_D[o], bias, ALU.add)
                tt_(f_B[o], ps[:, 4:6, :], bcm(rn, 2), ALU.mult).then_inc(sem("filter_done"), 1)

            def gates(f_, k_):
                for d in range(2):
                    for h in range(HGH):
                        i = 4 * d + h
                        last = ts(f_[:, d, h, :], f_[:, d, h, :], small[:, 200 + i:201 + i], small[:, 192 + i:193 + i],
                                  ALU.mult, ALU.add)
                done(last)
                done(ts(k_, f_, -1.0, 1.0, ALU.mult, ALU.add))

            def hgrn():
                dve.wait_ge(sem("b2_evac"), len(B2_UNITS))
                done(nc.vector.memset(rstd[:, :], 0.0))
                gates(x_f, x_k)
                done(nc.vector.memset(x_E[:, 0, :, T - 1:T], 1.0))
                done(nc.vector.memset(x_E[:, 1, :, 0:1], 1.0))
                for h in range(HGH):
                    nc.vector.tensor_tensor_scan(x_E[:, 0, h, 0:T - 1][:, ::-1], x_f[:, 0, h, 1:T][:, ::-1], rstd[:, 0:T - 1],
                                                 1.0, ALU.mult, ALU.add)
                    last = nc.vector.tensor_tensor_scan(x_E[:, 1, h, 1:T], x_f[:, 1, h, 0:T - 1], rstd[:, 0:T - 1],
                                                        1.0, ALU.mult, ALU.add)
                done(last)
                tt_(x_k, x_k, x_E, ALU.mult).then_inc(sem("hg_gates"), 1)
                gates(g_f, g_k)
                ts(g_q, g_q, float(P) ** -0.5, None, ALU.mult).then_inc(sem("hg_gates"), 1)
                dve.wait_ge(sem("hg_gates"), 2)
                dve.wait_ge(sem("hg_ctx_t"), 4)
                cp(g_F, g_f)
                done(nc.vector.memset(g_E, 1.0))
                dve.wait_ge(sem("hg_state"), 2)
                for lev in range(NLEV + 2):
                    hb = 1 << lev
                    if lev <= NLEV:
                        if lev >= 1:
                            dve.wait_ge(sem("hg_level"), lev + 1)
                        for d in range(2):
                            late, early = (1, 0) if d == 0 else (0, 1)

                            def cut(ap, side):
                                return ap.rearrange("p h (b s t) -> p (h b) s t", s=2, t=hb)[:, :, side, :]

                            tt_(cut(g_Q[:, d], late), cut(g_q, late), cut(g_F[:, d], late), ALU.mult)
                            last = tt_(cut(g_K[:, d], early), cut(g_k[:, d], early), cut(g_E[:, d], early), ALU.mult)
                        last.then_inc(sem("hg_scaled"), 1)
                        dve.wait_ge(sem("hg_scaled"), lev + 1)
                        for d in range(2):
                            late, early = (1, 0) if d == 0 else (0, 1)
                            end = hb - 1 if d == 0 else 0
                            edge_l = cut(g_F[:, d], late)[:, :, end:end + 1].to_broadcast([P, HGH * T // (2 * hb), hb])
                            edge_e = cut(g_F[:, d], early)[:, :, end:end + 1].to_broadcast([P, HGH * T // (2 * hb), hb])
                            done(tt_(cut(g_E[:, d], early), cut(g_E[:, d], early), edge_l, ALU.mult))
                            done(tt_(cut(g_F[:, d], late), cut(g_F[:, d], late), edge_e, ALU.mult))
                    else:
                        dve.wait_ge(sem("hg_cross"), 1)
                        for d in range(2):
                            last = tt_(g_Q[:, d], g_q, g_F[:, d], ALU.mult)
                        last.then_inc(sem("hg_scaled"), 1)
                    if lev <= NLEV:
                        dve.wait_ge(sem("hg_level"), lev + 1)
                        for d in range(2):
                            for tt in range(TT):
                                src = ps[:, 4 * (lev % 2) + 2 * d + tt, :].rearrange("p (h s) -> p h s", s=P)
                                if lev == 0:
                                    last = tt_(g_A[:, d, tt], src, bcm(ident, HGH), ALU.mult)
                                else:
                                    mask = k("up" if d == 0 else "low", (lev - 1) * P, P).bitcast(U32)
                                    last = nc.vector.copy_predicated(g_A[:, d, tt], bcm(mask, HGH), src)
                        last.then_inc(sem("hg_taken"), 1)
                dve.wait_ge(sem("hg_out"), 2)
                o, r = g_F[:, 0], g_F[:, 1]
                inverse_root(ts(r, two(ps[:, 4:6, :]), 1.0 / P, EPS, ALU.mult, ALU.add), r)
                done(stt(out=o, in0=o, scalar=v("hg_norm_g"), in1=r, op0=ALU.mult, op1=ALU.mult))
                tt_(mix3[:, 4:8, :], o, g_g, ALU.mult).then_inc(sem("hg_mixed"), 1)

            def hyena():
                rows = T // GRID
                for m in range(12):
                    dve.wait_ge(sem("hy_middle"), m + 1)
                    y = y_c[:, m, :].rearrange("p (r g) -> p r g", g=GRID)
                    p_ = hy_p[:, m, :].rearrange("p (r g) -> p r g", g=GRID)
                    done(stt(out=y[:, :, 1:GRID], in0=p_[:, :, 0:GRID - 1], scalar=v("conv_w", m), in1=y[:, :, 1:GRID],
                             op0=ALU.mult, op1=ALU.add))
                    last = stt(out=y[:, :, 0:GRID - 1], in0=p_[:, :, 1:GRID], scalar=v("conv_w", 24 + m),
                               in1=y[:, :, 0:GRID - 1], op0=ALU.mult, op1=ALU.add)
                last.then_inc(sem("hy_conv"), 1)
                for o in range(2):
                    dve.wait_ge(sem("hy_u"), o + 1)
                    tmp = sq[:, 1024:1536]
                    for ft in range(2):
                        uc, us = ps[:, 2 + ft, :], ps[:, 4 + ft, :]
                        A, B, Dd = f_A[o][:, ft, :], f_B[o][:, ft, :], (f_D[o] if ft == 0 else f_A[o][:, 1, :])
                        done(tt_(y_cc[:, ft, :], uc, A, ALU.mult))
                        done(tt_(tmp, us, B, ALU.mult))
                        done(tt_(y_cc[:, ft, :], y_cc[:, ft, :], tmp, ALU.subtract))
                        done(tt_(y_ss[:, ft, :], uc, B, ALU.mult))
                        done(tt_(tmp, us, Dd, ALU.mult))
                        last = tt_(y_ss[:, ft, :], y_ss[:, ft, :], tmp, ALU.add)
                    last.then_inc(sem("hy_y"), 1)
                    dve.wait_ge(sem("hy_v"), o + 1)
                    for tt in range(TT):
                        last = tt_((y_m if o else y_z)[:, tt, :], ps[:, 6 + tt, :], y_t[:, tt, HYW * (o + 1):HYW * (o + 2)], ALU.mult)
                    last.then_inc(sem("hy_z"), 1)
                dve.wait_ge(sem("hy_square"), 2)
                inverse_root(ts(small[:, 208:210], small[:, 208:210], 1.0 / HYW, EPS, ALU.mult, ALU.add), small[:, 208:210])
                tt_(y_m, y_m, bc(small[:, 208:210], HYW), ALU.mult).then_inc(sem("hy_normed"), 1)

            def four_times(half_):
                for r in range(P // CAP):
                    cp(e_four[half_][:, :, :, r, :], e_sel[:, :, half_ * NE // 2:(half_ + 1) * NE // 2, :]) \
                        .then_inc(sem("e_select"), 1)

            def tokens(at):
                cp(e_xe, e_x[:, :, at]).then_inc(sem("moe_x"), 1)

            def routing():
                dve.wait_ge(sem("e_turned"), 2)
                lg = ps[:, 4, 0:TT * NE].rearrange("p (t e) -> p t e", t=TT)
                done(red(e_st[:, 0:2], lg, AXX, ALU.max))
                tt_(e_aff, lg, bc(e_st[:, 0:2], NE), ALU.subtract).then_inc(sem("e_aff"), 1)
                dve.wait_ge(sem("e_rows"), 2)
                done(red(e_st[:, 2:4], e_aff, AXX, ALU.add))
                done(nc.vector.reciprocal(e_st[:, 4:6], e_st[:, 2:4]))
                tt_(e_aff, e_aff, bc(e_st[:, 4:6], NE), ALU.mult).then_inc(sem("e_aff"), 1)
                dve.wait_ge(sem("e_aff"), 2)
                unit = e_y[:, 0:T]
                done(nc.vector.memset(unit, 1.0))
                dve.wait_ge(sem("early_landed"), 16)

                def select(e0, e1):
                    before = n_order[0]
                    for e in range(e0, e1):
                        dve.wait_ge(sem("e_spread"), min(2 * (e // 2) + 2, e1))
                        if e >= e0 + 2:
                            dve.wait_ge(sem("dve_order"), before + e - e0 - 1)
                        for tt in range(TT):
                            n = (tt + 1) * P
                            cmp = e_cmp[:, 4 * (e % 2) + 2 * tt:4 * (e % 2) + 2 * tt + 2, :]
                            stt(out=cmp[:, 0, :], in0=half(0, e), scalar=e_aff[:, tt, e:e + 1], in1=unit, op0=ALU.is_gt,
                                op1=ALU.mult, accum_out=e_rank[:, tt, e:e + 1])
                            last = stt(out=cmp[:, 1, 0:n], in0=half(0, e)[:, 0:n], scalar=e_aff[:, tt, e:e + 1],
                                       in1=e_early[:, tt, 0:n], op0=ALU.is_equal, op1=ALU.mult,
                                       accum_out=e_tie[:, tt, e:e + 1])
                        last.then_inc(sem("dve_order"), 1)
                    n_order[0] += e1 - e0
                    dve.wait_ge(sem("dve_order"), n_order[0])
                    done(tt_(e_rank[:, :, e0:e1], e_rank[:, :, e0:e1], e_tie[:, :, e0:e1], ALU.add))
                    for tt in range(TT):
                        last = tt_(e_sel[:, tt, e0:e1], bcm(k("iota"), e1 - e0), bc(e_rank[:, tt, e0:e1], CAP), ALU.is_equal)
                    last.then_inc(sem("e_select"), 1)

                select(0, E_FIRST)
                select(E_FIRST, E_SECOND)
                dve.wait_ge(sem("e_gather"), KT)
                tokens(slice(0, CAP))
                select(E_SECOND, NE)
                for tt in range(TT):
                    tt_(e_diag[:, tt * NE:(tt + 1) * NE, :], bcm(ident, NE), bc(e_aff[:, tt, :], P), ALU.mult)
                dve.wait_ge(sem("e_select"), 3)
                four_times(0)

            def experts():
                back = e_back.rearrange("p a b -> p (a b)")

                def gated(e):
                    dve.wait_ge(sem("moe_slot"), PER_EXPERT * e + 8)
                    cp(e_bk, back[:, bass.ds(T * e, T)])
                    dve.wait_ge(sem("moe_slot"), PER_EXPERT * e + 16)
                    dve.wait_ge(sem("moe_silu"), e + 1)
                    tt_(e_h2, e_s, ps[:, 1, :], ALU.mult).then_inc(sem("moe_h"), 1)

                dve.wait_ge(sem("moe_slot"), 16)
                dve.wait_ge(sem("moe_silu"), 1)
                tt_(e_h2, e_s, ps[:, 1, :], ALU.mult).then_inc(sem("moe_h"), 1)
                tokens(slice(CAP, 2 * CAP))
                dve.wait_ge(sem("e_gather"), 2 * KT)
                four_times(1)
                dve.wait_ge(sem("e_back"), NE // 2)
                cp(e_bk, back[:, 0:T]).then_inc(sem("e_back"), 1)
                with dve.Fori(1, NE - 1) as e:
                    gated(e)
                    tokens(bass.ds(CAP * e + CAP, CAP))
                gated(NE - 1)

            def site(layer, s):
                return 72 * layer + 24 * s

            def modulated(i, layer, s, factor):
                at = site(layer, s)
                scale_of(at + 8, v("norm_g", 8 * (3 * layer + s), 8))
                norm(i, x3, h3, coef[:, 0:8])

            dve.wait_ge(sem("c_ready"), 1)
            for r in range(ADA_FIRST):
                ada_round(r, 0, junk=hT)
            dve.wait_ge(sem("start_landed"), 48)
            ada_bias(0, 16, ADA_FIRST)
            modulated(0, 0, 0, 0.5)
            with dve.Fori(0, NG - 1) as g:
                hidden(g)
                ada_round(g + ADA_FIRST, 0)
            hidden(NG - 1)
            last_ada = ADA_FIRST + NG - 1
            ada_bias(16, 8 * last_ada, last_ada)
            gate_of(site(0, 0) + 16, 0.5)
            residual(end=("down_used", NG + 1))
            modulated(1, 0, 1, 1.0)
            ada_round(last_ada, 0, junk=ar(12288, 2 * D))
            dve.wait_ge(sem("tables_landed"), 32)
            mla()
            gate_of(site(0, 1) + 16, 1.0)
            mixed(0)
            modulated(2, 0, 2, 0.5)
            gate_of(site(0, 2) + 16, 0.5)
            ffn(1)
            ada_bias(8 * last_ada, N_MODS - 8, ADA_FIRST + 2 * NG - 1)
            dve.wait_ge(sem("ada_context"), 18)
            done(tt_(cmods[:, :], cmods[:, :], v("ada_b", 144, 16), ALU.add))
            modulated(3, 1, 0, 0.5)
            ada_round(ADA_FIRST + 2 * NG - 1, 1)
            ada_bias(N_MODS - 8, N_MODS, ADA_FIRST + 2 * NG)
            gate_of(site(1, 0) + 16, 0.5)
            ffn(2)
            modulated(4, 1, 1, 1.0)
            rwkv()
            gate_of(site(1, 1) + 16, 1.0)
            mixed(1)
            modulated(5, 1, 2, 0.5)
            gate_of(site(1, 2) + 16, 0.5)
            ffn(3)
            norm(6, x3, x3, v("final_g", 0, 8), name="x_ready")
            scale_of(144 + 8, v("norm1_g", 0, 8))
            filter_end(0)
            norm(7, x3, h3, coef[:, 0:8])
            filter_end(1)
            scale_of(8, v("norm1_g", 0, 8), src=cmods, to=16)
            norm(8, ctx3, hc3, coef[:, 16:24])
            hyena()
            hgrn()
            gate_of(144 + 16, 1.0)
            mixed(2, lambda m: half(0, m))
            scale_of(144 + 32, v("norm2_g", 0, 8))
            norm(9, x3, h3, coef[:, 0:8])
            routing()
            experts()
            gate_of(144 + 40, 1.0)
            dve.wait_ge(sem("moe_o"), NE)
            residual(lambda m: half(4, m))
            norm(10, x3, h3, v("final_g2", 0, 8), name="h_ready")


INPUTS = ("con", "big", "win", "earlier", "vec", "xT", "ctxT", "c_rows", "ada", "ffn_gate", "ffn_up", "ffn_down",
          "ring_w", "w1", "w3", "w2", "pos_w", "hy_bias")


def kernel(**inputs):
    import concourse.bacc as bacc
    from concourse.bass_utils import run_bass_kernel_spmd

    laid = lay_out(inputs)
    nc = bacc.Bacc("TRN2", target_bir_lowering=False, num_devices=1)
    arrays, args = {}, {}
    for name in INPUTS:
        arrays[f"in_{name}"] = np.ascontiguousarray(laid[name])
        args[name] = nc.dram_tensor(f"in_{name}", arrays[f"in_{name}"].shape, F32, kind="ExternalInput").ap()
    out = nc.dram_tensor("out_0", (T, D), F32, kind="ExternalOutput").ap()
    build(nc, args, out)
    r = run_bass_kernel_spmd(nc, [arrays], core_ids=[0])
    return r.results[0]["out_0"].reshape(1, T, D)
```
